# Optimizing a Trainium2 kernel written in Bass

```python
import jax
import jax.numpy as jnp
from jax import lax
import numpy as np

D_MODEL = 1024
BATCH = 1
SEQ = 256
DEPTH = 2

D_GROUP = D_MODEL // 4
HEAD_DIM = 64
N_GROUP_HEADS = D_GROUP // HEAD_DIM

RWKV_LORA_DECAY = 64
RWKV_LORA_AAA = 64
RWKV_LORA_GATE = 128
RWKV_LN_EPS = 64e-5

DILATED_PATTERNS = ((128, 1), (512, 4), (2048, 16))

MLA_Q_RANK = D_MODEL // 4
MLA_KV_RANK = D_MODEL // 8
MLA_NOPE_DIM = 64
MLA_ROPE_DIM = 32
MLA_V_DIM = D_GROUP // N_GROUP_HEADS

HGRN_CHUNK = 16

D_FF = 2816
N_EXPERTS = 8
TOP_K = 2
D_FF_EXPERT = 3584

ROPE_THETA = 10000.0
RMS_EPS = 1e-6
ATTN_BLOCK = 128
NEG_INF = -1e30

RWKV_COLS = (D_GROUP, D_GROUP, D_GROUP, RWKV_LORA_DECAY, RWKV_LORA_AAA, RWKV_LORA_GATE)
N_RWKV_COLS = sum(RWKV_COLS)
N_DIL_COLS = 3 * D_GROUP
MLA_COLS = (MLA_Q_RANK, MLA_KV_RANK, MLA_ROPE_DIM)
N_MLA_COLS = sum(MLA_COLS)
N_HGRN_COLS = 4 * D_GROUP
MIXER_COLS = (N_RWKV_COLS, N_DIL_COLS, N_MLA_COLS, N_HGRN_COLS)
N_IN_COLS = sum(MIXER_COLS)
N_DENSE_LAYERS = (DEPTH + 1) // 2
N_MOE_LAYERS = DEPTH // 2

kernel_name = 'hybrid_rwkv7_dilated_mla_hgrn2_moe'

def split_cols(a, sizes):
    out, start = [], 0
    for s in sizes:
        out.append(a[..., start:start + s])
        start += s
    return out

def rms_norm(x, w):
    xf = x.astype(jnp.float32)
    y = xf * lax.rsqrt(jnp.mean(xf * xf, axis=-1, keepdims=True) + RMS_EPS)
    return (y * w).astype(x.dtype)

def rope_tables(positions, dim):
    inv_freq = 1.0 / (ROPE_THETA ** (jnp.arange(0, dim, 2, dtype=jnp.float32) / dim))
    ang = positions.astype(jnp.float32)[..., None] * inv_freq
    return jnp.cos(ang), jnp.sin(ang)

def apply_rope(x, cos, sin):
    half = x.shape[-1] // 2
    x1 = x[..., :half].astype(jnp.float32)
    x2 = x[..., half:].astype(jnp.float32)
    c, s = cos[:, None], sin[:, None]
    return jnp.concatenate([x1 * c - x2 * s, x2 * c + x1 * s], axis=-1).astype(x.dtype)

def to_heads(t, n_heads):
    b, s, _ = t.shape
    return t.reshape(b, s, n_heads, -1).transpose(0, 2, 1, 3)

def token_shift(a, mu):
    prev = jnp.pad(a, ((0, 0), (1, 0), (0, 0)))[:, :-1]
    return a + (prev - a) * mu

def rwkv7_time_mix(cols, mu, w0, w2, a0, a2, g2, k_k, k_a, r_k, ln_w, ln_b):
    b_, t_, _ = cols.shape
    h_, n_ = N_GROUP_HEADS, HEAD_DIM
    r, k, v, xw, xa, xg = split_cols(token_shift(cols, mu), RWKV_COLS)
    w = -jax.nn.softplus(-(w0 + jnp.tanh(xw) @ w2).astype(jnp.float32)) - 0.5
    decay = jnp.exp(-jnp.exp(w))
    a = jax.nn.sigmoid((a0 + xa @ a2).astype(jnp.float32))
    g = (jax.nn.sigmoid(xg) @ g2).astype(jnp.float32)
    heads = lambda t: t.reshape(b_, t_, h_, n_)
    kk = heads((k * k_k).astype(jnp.float32))
    kk = kk / jnp.maximum(jnp.sqrt(jnp.sum(kk * kk, axis=-1, keepdims=True)), 1e-12)
    k = k.astype(jnp.float32) * (1.0 + (a - 1.0) * k_a)
    r_h, k_h, v_h = heads(r.astype(jnp.float32)), heads(k), heads(v.astype(jnp.float32))
    w_h, a_h = heads(decay), heads(a)

    def step(state, inp):
        r_t, w_t, k_t, v_t, kk_t, a_t = inp
        s_kk = jnp.einsum('bhvk,bhk->bhv', state, kk_t)
        state = (state * w_t[:, :, None, :]
                 - s_kk[..., None] * (kk_t * a_t)[:, :, None, :]
                 + v_t[..., None] * k_t[:, :, None, :])
        return state, jnp.einsum('bhvk,bhk->bhv', state, r_t)

    xs = tuple(jnp.moveaxis(t, 1, 0) for t in (r_h, w_h, k_h, v_h, kk, a_h))
    s0 = jnp.zeros((b_, h_, n_, n_), jnp.float32)
    _, y = lax.scan(step, s0, xs)
    y = jnp.moveaxis(y, 0, 1)
    mean = jnp.mean(y, axis=-1, keepdims=True)
    var = jnp.mean((y - mean) ** 2, axis=-1, keepdims=True)
    y = ((y - mean) * lax.rsqrt(var + RWKV_LN_EPS)).reshape(b_, t_, D_GROUP) * ln_w + ln_b
    bonus = jnp.sum(r_h * k_h * r_k.reshape(h_, n_), axis=-1, keepdims=True) * v_h
    y = y + bonus.reshape(b_, t_, D_GROUP)
    return (y * g).astype(cols.dtype)

def banded_causal_attention(q, k, v, span):
    *lead, l_, hd = q.shape
    blk = span
    nb = -(-l_ // blk)
    pad = nb * blk - l_
    padw = [(0, 0)] * len(lead) + [(0, pad), (0, 0)]
    q, k, v = (jnp.pad(t, padw).reshape(*lead, nb, blk, hd) for t in (q, k, v))

    def with_prev(t):
        prev = jnp.concatenate([jnp.zeros_like(t[..., :1, :, :]), t[..., :-1, :, :]], axis=-3)
        return jnp.concatenate([prev, t], axis=-2)

    kb, vb = with_prev(k), with_prev(v).astype(jnp.float32)
    s = jnp.einsum('...qd,...kd->...qk', q, kb).astype(jnp.float32) * (hd ** -0.5)
    dist = (jnp.arange(blk)[:, None] + blk) - jnp.arange(2 * blk)[None, :]
    in_band = (dist >= 0) & (dist <= span)
    after_start = (jnp.arange(nb)[:, None, None] > 0) | (jnp.arange(2 * blk)[None, None, :] >= blk)
    s = jnp.where(in_band & after_start, s, NEG_INF)
    m = jnp.max(s, axis=-1, keepdims=True)
    p = jnp.exp(s - m)
    den = jnp.sum(p, axis=-1, keepdims=True)
    o = jnp.einsum('...qk,...kd->...qd', p, vb) / den
    lse = (m + jnp.log(den))[..., 0]
    o = o.reshape(*lead, nb * blk, hd)[..., :l_, :]
    lse = lse.reshape(*lead, nb * blk)[..., :l_]
    return o, lse

def dilated_attention(q, k, v):
    b_, h_, t_, hd = q.shape
    outs, lses = [], []
    for window, dil in DILATED_PATTERNS:
        l_ = t_ // dil

        def fold(a):
            return a.reshape(b_, h_, l_, dil, hd).swapaxes(2, 3)

        o, lse = banded_causal_attention(fold(q), fold(k), fold(v), window // dil)
        outs.append(o.swapaxes(2, 3).reshape(b_, h_, t_, hd))
        lses.append(lse.swapaxes(2, 3).reshape(b_, h_, t_))
    weights = jax.nn.softmax(jnp.stack(lses), axis=0)
    return jnp.sum(weights[..., None] * jnp.stack(outs), axis=0)

def blocked_causal_attention(q, k, v):
    b_, h_, t_, dq = q.shape
    nb = t_ // ATTN_BLOCK
    qb = jnp.moveaxis(q.reshape(b_, h_, nb, ATTN_BLOCK, dq), 2, 0)
    vf = v.astype(jnp.float32)
    kpos = jnp.arange(t_)
    scale = dq ** -0.5

    def attend(args):
        q_blk, blk_idx = args
        s = jnp.einsum('bhqd,bhkd->bhqk', q_blk, k).astype(jnp.float32) * scale
        qpos = blk_idx * ATTN_BLOCK + jnp.arange(ATTN_BLOCK)
        s = jnp.where(kpos[None, :] <= qpos[:, None], s, NEG_INF)
        return jnp.einsum('bhqk,bhkd->bhqd', jax.nn.softmax(s, axis=-1), vf)

    o = lax.map(attend, (qb, jnp.arange(nb)))
    return jnp.moveaxis(o, 0, 2).reshape(b_, h_, t_, v.shape[-1])

def mla_attention(cols, q_norm, w_uq, kv_norm, w_ukv, cos_r, sin_r):
    b_, t_, _ = cols.shape
    h_ = N_GROUP_HEADS
    c_q, c_kv, k_rope = split_cols(cols, MLA_COLS)
    q = to_heads(rms_norm(c_q, q_norm) @ w_uq, h_)
    kv = to_heads(rms_norm(c_kv, kv_norm) @ w_ukv, h_)
    q_nope, q_rope = q[..., :MLA_NOPE_DIM], q[..., MLA_NOPE_DIM:]
    k_nope, v = kv[..., :MLA_NOPE_DIM], kv[..., MLA_NOPE_DIM:]
    q_rope = apply_rope(q_rope, cos_r, sin_r)
    k_rope = apply_rope(k_rope[:, None], cos_r, sin_r)
    qf = jnp.concatenate([q_nope, q_rope], axis=-1)
    kf = jnp.concatenate([k_nope, jnp.broadcast_to(k_rope, (b_, h_, t_, MLA_ROPE_DIM))], axis=-1)
    o = blocked_causal_attention(qf, kf, v)
    return o.transpose(0, 2, 1, 3).reshape(b_, t_, h_ * MLA_V_DIM).astype(cols.dtype)

def gated_linear_recurrence_chunked(q, k, v, log_f):
    b_, h_, t_, dk = q.shape
    dv = v.shape[-1]
    c_ = HGRN_CHUNK
    n_ = t_ // c_
    q, k, v, log_f = (t.reshape(b_, h_, n_, c_, t.shape[-1]) for t in (q, k, v, log_f))
    b = jnp.cumsum(log_f, axis=3)
    b_end = b[:, :, :, c_ - 1:]
    causal = jnp.tril(jnp.ones((c_, c_), dtype=bool))[:, :, None]
    diff = b[:, :, :, :, None, :] - b[:, :, :, None, :, :]
    intra_decay = jnp.exp(jnp.where(causal, diff, NEG_INF))
    scores = jnp.einsum('bhnck,bhnsk,bhncsk->bhncs', q, k, intra_decay)
    o_intra = jnp.einsum('bhncs,bhnsv->bhncv', scores, v)
    chunk_update = jnp.einsum('bhnsk,bhnsv->bhnkv', k * jnp.exp(b_end - b), v)
    chunk_decay = jnp.exp(b_end[:, :, :, 0])

    def step(state, inp):
        upd, dec = inp
        return state * dec[..., None] + upd, state

    s0 = jnp.zeros((b_, h_, dk, dv), q.dtype)
    _, s_start = lax.scan(step, s0, (jnp.moveaxis(chunk_update, 2, 0), jnp.moveaxis(chunk_decay, 2, 0)))
    o_inter = jnp.einsum('bhnck,nbhkv->bhncv', q * jnp.exp(b), s_start)
    return (o_intra + o_inter).reshape(b_, h_, t_, dv)

def hgrn2_mixer(cols, lower_bound, g_norm):
    b_, t_, _ = cols.shape
    h_, n_ = N_GROUP_HEADS, HEAD_DIM
    q, f, i, g = split_cols(cols, (D_GROUP,) * 4)
    heads = lambda t: to_heads(t, h_).astype(jnp.float32)
    z = heads(f)
    lb = lower_bound.astype(jnp.float32).reshape(h_, n_)[:, None, :]
    forget = lb + (1.0 - lb) * jax.nn.sigmoid(z)
    log_f = jnp.log(forget)
    k = 1.0 - forget
    o = gated_linear_recurrence_chunked(heads(jax.nn.silu(q)), k, heads(i), log_f)
    o = o * lax.rsqrt(jnp.mean(o * o, axis=-1, keepdims=True) + RMS_EPS)
    o = o.transpose(0, 2, 1, 3).reshape(b_, t_, D_GROUP) * g_norm
    return (o * jax.nn.silu(g)).astype(cols.dtype)

def swiglu(h, w1, w3, w2):
    return (jax.nn.silu(h @ w1) * (h @ w3)) @ w2

def moe_swiglu(h, w_router, w1, w3, w2):
    logits = (h @ w_router).astype(jnp.float32)
    top_v, top_i = lax.top_k(logits, TOP_K)
    gates = jax.nn.softmax(top_v, axis=-1)
    combine = jnp.sum(jax.nn.one_hot(top_i, N_EXPERTS, dtype=jnp.float32) * gates[..., None], axis=-2)
    out = jnp.zeros_like(h)
    for e in range(N_EXPERTS):
        out = out + combine[..., e:e + 1].astype(h.dtype) * swiglu(h, w1[e], w3[e], w2[e])
    return out

def setup_inputs(seed: int = 0) -> dict:
    key = jax.random.key(seed)
    keys = jax.random.split(key, 40)
    counter = [0]

    def nxt():
        kk = keys[counter[0]]
        counter[0] += 1
        return kk

    def nrm(shape, scale):
        return scale * jax.random.normal(nxt(), shape, jnp.float32)

    def gain(shape):
        return 1.0 + 0.02 * jax.random.normal(nxt(), shape, jnp.float32)

    x = nrm((BATCH, SEQ, D_MODEL), 1.0)
    positions = (jax.random.randint(nxt(), (BATCH, 1), 0, SEQ, dtype=jnp.int32)
                 + jnp.arange(SEQ, dtype=jnp.int32)[None, :])
    return {
        'x': x,
        'positions': positions,
        'mix_norm': gain((DEPTH, D_MODEL)),
        'w_in': nrm((DEPTH, D_MODEL, N_IN_COLS), D_MODEL ** -0.5),
        'w_out': nrm((DEPTH, D_MODEL, D_MODEL), D_MODEL ** -0.5),
        'rwkv_mu': jax.random.uniform(nxt(), (DEPTH, N_RWKV_COLS), jnp.float32),
        'rwkv_w0': nrm((DEPTH, D_GROUP), 0.5) - 1.0,
        'rwkv_w2': nrm((DEPTH, RWKV_LORA_DECAY, D_GROUP), 0.5 * RWKV_LORA_DECAY ** -0.5),
        'rwkv_a0': nrm((DEPTH, D_GROUP), 0.1),
        'rwkv_a2': nrm((DEPTH, RWKV_LORA_AAA, D_GROUP), RWKV_LORA_AAA ** -0.5),
        'rwkv_g2': nrm((DEPTH, RWKV_LORA_GATE, D_GROUP), RWKV_LORA_GATE ** -0.5),
        'rwkv_k_k': nrm((DEPTH, D_GROUP), 0.05) + 0.85,
        'rwkv_k_a': gain((DEPTH, D_GROUP)),
        'rwkv_r_k': nrm((DEPTH, D_GROUP), 0.1),
        'rwkv_ln_w': gain((DEPTH, D_GROUP)),
        'rwkv_ln_b': nrm((DEPTH, D_GROUP), 0.02),
        'mla_q_norm': gain((DEPTH, MLA_Q_RANK)),
        'mla_w_uq': nrm((DEPTH, MLA_Q_RANK, N_GROUP_HEADS * (MLA_NOPE_DIM + MLA_ROPE_DIM)), MLA_Q_RANK ** -0.5),
        'mla_kv_norm': gain((DEPTH, MLA_KV_RANK)),
        'mla_w_ukv': nrm((DEPTH, MLA_KV_RANK, N_GROUP_HEADS * (MLA_NOPE_DIM + MLA_V_DIM)), MLA_KV_RANK ** -0.5),
        'hgrn_lb_logits': nrm((DEPTH, D_GROUP), 1.0),
        'hgrn_g_norm': gain((DEPTH, D_GROUP)),
        'ffn_norm': gain((DEPTH, D_MODEL)),
        'ffn_w1': nrm((N_DENSE_LAYERS, D_MODEL, D_FF), D_MODEL ** -0.5),
        'ffn_w3': nrm((N_DENSE_LAYERS, D_MODEL, D_FF), D_MODEL ** -0.5),
        'ffn_w2': nrm((N_DENSE_LAYERS, D_FF, D_MODEL), D_FF ** -0.5),
        'moe_router': nrm((N_MOE_LAYERS, D_MODEL, N_EXPERTS), D_MODEL ** -0.5),
        'moe_w1': nrm((N_MOE_LAYERS, N_EXPERTS, D_MODEL, D_FF_EXPERT), D_MODEL ** -0.5),
        'moe_w3': nrm((N_MOE_LAYERS, N_EXPERTS, D_MODEL, D_FF_EXPERT), D_MODEL ** -0.5),
        'moe_w2': nrm((N_MOE_LAYERS, N_EXPERTS, D_FF_EXPERT, D_MODEL), D_FF_EXPERT ** -0.5),
        'final_norm': gain((D_MODEL,)),
    }

def reference(x, positions, mix_norm, w_in, w_out, rwkv_mu, rwkv_w0, rwkv_w2, rwkv_a0, rwkv_a2,
              rwkv_g2, rwkv_k_k, rwkv_k_a, rwkv_r_k, rwkv_ln_w, rwkv_ln_b, mla_q_norm, mla_w_uq,
              mla_kv_norm, mla_w_ukv, hgrn_lb_logits, hgrn_g_norm, ffn_norm, ffn_w1, ffn_w3, ffn_w2,
              moe_router, moe_w1, moe_w3, moe_w2, final_norm):
    b_, t_, _ = x.shape
    cos_d, sin_d = rope_tables(positions, HEAD_DIM)
    cos_m, sin_m = rope_tables(positions, MLA_ROPE_DIM)
    lb_sm = jax.nn.softmax(hgrn_lb_logits.astype(jnp.float32), axis=0)
    lower_bounds = jnp.cumsum(lb_sm, axis=0) - lb_sm[0]
    for layer in range(DEPTH):
        h = rms_norm(x, mix_norm[layer])
        c_rwkv, c_dil, c_mla, c_hgrn = split_cols(h @ w_in[layer], MIXER_COLS)
        y_a = rwkv7_time_mix(c_rwkv, rwkv_mu[layer], rwkv_w0[layer], rwkv_w2[layer], rwkv_a0[layer],
                             rwkv_a2[layer], rwkv_g2[layer], rwkv_k_k[layer], rwkv_k_a[layer],
                             rwkv_r_k[layer], rwkv_ln_w[layer], rwkv_ln_b[layer])
        q_d, k_d, v_d = (to_heads(t, N_GROUP_HEADS) for t in split_cols(c_dil, (D_GROUP,) * 3))
        y_b = dilated_attention(apply_rope(q_d, cos_d, sin_d), apply_rope(k_d, cos_d, sin_d), v_d)
        y_b = y_b.transpose(0, 2, 1, 3).reshape(b_, t_, D_GROUP).astype(x.dtype)
        y_c = mla_attention(c_mla, mla_q_norm[layer], mla_w_uq[layer], mla_kv_norm[layer],
                            mla_w_ukv[layer], cos_m, sin_m)
        y_d = hgrn2_mixer(c_hgrn, lower_bounds[layer], hgrn_g_norm[layer])
        x = x + jnp.concatenate([y_a, y_b, y_c, y_d], axis=-1) @ w_out[layer]
        h = rms_norm(x, ffn_norm[layer])
        if layer % 2 == 0:
            j = layer // 2
            x = x + swiglu(h, ffn_w1[j], ffn_w3[j], ffn_w2[j])
        else:
            j = layer // 2
            x = x + moe_swiglu(h, moe_router[j], moe_w1[j], moe_w3[j], moe_w2[j])
    return rms_norm(x, final_norm)


_drawn_inputs = setup_inputs


def setup_inputs(seed=0):
    import zlib

    import numpy as np

    out = dict(_drawn_inputs(seed))
    spreads = {}
    factors = {'rwkv_k_k': 42.177,
     'rwkv_ln_b': 10.634,
     'mla_q_norm': 3.992,
     'mla_kv_norm': 4.609,
     'hgrn_g_norm': 11.633,
     'final_norm': 21.464,
     'rwkv_a0': 2.845,
     'rwkv_k_a': 5.832,
     'rwkv_ln_w': 8.0,
     'ffn_norm': 3.291}
    for name, (base, spread) in spreads.items():
        noise = np.random.default_rng([zlib.crc32(name.encode()), seed]).standard_normal(out[name].shape)
        drawn = base * np.exp(spread * noise) if base else spread * noise
        out[name] = jnp.asarray(drawn.astype(out[name].dtype))
    for name, factor in factors.items():
        out[name] = (out[name] * factor).astype(out[name].dtype)
    return out
```

```python
from contextlib import ExitStack

import numpy as np

import concourse.bass as bass
from concourse import mybir

F32 = mybir.dt.float32
I32 = mybir.dt.int32
U32 = mybir.dt.uint32
BF16 = mybir.dt.bfloat16
ALU = mybir.AluOpType
ACT = mybir.ActivationFunctionType
AX = mybir.AxisListType

P = 128
D = 1024
T = 256
DEPTH = 2
KT = D // P
TT = T // P
G = D // 4
GT = G // P
HD = 64
NH = G // HD
NM = NH * TT
N_IN = 3232
UQ = 96
FF = 2816
FE = 3584
NE = 8
C = 96
MAXJOBS = 16
RWKV_EPS = 64e-5
RMS_EPS = 1e-6
DECAY = float(np.exp(np.float32(-0.5)))
NEG = -1e30
ROUND = 1.5 * 2.0 ** 23
TURN = (6.28125, 0.0019340515136718750, 1.2556659146e-06)
LEVELS = 7

UNITS = [(0, 256, False), (256, 256, False), (512, 256, False), (768, 256, False),
         (2208, 256, False), (2464, 256, False), (2720, 256, True), (2976, 256, False),
         (1024, 256, False), (1280, 256, False), (1536, 256, True),
         (1792, 256, False), (2048, 160, False)]
NU = len(UNITS)
J_R, J_K, J_V, J_X, J_HQ, J_HF, J_HI, J_HG, J_DQ, J_DK, J_DV, J_CQ, J_CKV, J_KR = \
    0, 2, 4, 6, 8, 10, 12, 14, 16, 18, 20, 22, 24, 25
NO = 4
LU = NU + NO
SLOTS = 6

PARAMS = [("mix_norm", 8), ("rwkv_mu", 8), ("rwkv_w0", 2), ("rwkv_a0", 2), ("rwkv_k_k", 2), ("rwkv_k_a", 2),
          ("rwkv_r_k", 2), ("rwkv_ln_w", 2), ("rwkv_ln_b", 2), ("mla_q_norm", 2), ("mla_kv_norm", 1),
          ("hgrn_g_norm", 2), ("hgrn_lb_logits", 2), ("ffn_norm", 8)]
PCOL, _at = {}, 0
for _name, _n in PARAMS:
    PCOL[_name] = (_at, _n)
    _at += DEPTH * _n
PCOL["final_norm"] = (_at, KT)
NPAR = _at + KT

CCOL, _at = {}, 0
for _name, _n in [("id", P), ("ones", P), ("blk", P), ("r64", P), ("r96", UQ), ("upi", P), ("ups", P),
                  ("lv", LEVELS * P), ("dil", 3 * P), ("caus", 3 * P), ("iota", P), ("f64", 1), ("f96", 1),
                  ("eps_rms", 1), ("eps_ln", 1), ("zero", 1)]:
    CCOL[_name] = (_at, _n)
    _at += _n
NCONST = _at


def constants():
    c = np.zeros((P, NCONST), np.float32)

    def put(name, a):
        at, n = CCOL[name]
        a = np.asarray(a, np.float32)
        c[:a.shape[0], at:at + n] = a.reshape(a.shape[0], n)

    i = np.arange(P)
    put("id", np.eye(P))
    put("ones", np.ones((P, P)))
    put("blk", (i[:, None] // HD == i[None, :] // HD))

    def rotate(lo, n, width):
        r = np.zeros((width, width))
        for b in range(lo, width, n):
            for q in range(n // 2):
                r[b + n // 2 + q, b + q] = -1.0
                r[b + q, b + n // 2 + q] = 1.0
        return r

    put("r64", rotate(0, HD, P))
    put("r96", rotate(HD, UQ - HD, UQ))
    put("upi", i[:, None] <= i[None, :])
    put("ups", i[:, None] < i[None, :])
    lv = np.zeros((P, LEVELS, P))
    for l in range(LEVELS):
        half = 1 << l
        same = i[:, None] // (2 * half) == i[None, :] // (2 * half)
        lv[:, l] = same & ((i[:, None] // half) % 2 == 0) & ((i[None, :] // half) % 2 == 1)
    put("lv", lv)
    q, k = np.arange(T)[:, None], np.arange(T)[None, :]
    d = q - k
    count = ((d >= 0) & (d <= 128)) + 0.0
    count += (d >= 0) & (d % 4 == 0) & (d // 4 <= 128)
    count += (d >= 0) & (d % 16 == 0) & (d // 16 <= 128)
    dil = np.where(count > 0, np.log(np.maximum(count, 1.0)), NEG)
    caus = np.where(d >= 0, 0.0, NEG)
    for name, m in (("dil", dil), ("caus", caus)):
        put(name, np.concatenate([m[:P, :P], m[P:, :]], axis=1))
    put("iota", np.broadcast_to(i, (P, P)))
    f64 = 1.0 / (np.float32(10000.0) ** (np.arange(0, HD, 2, dtype=np.float32) / np.float32(HD)))
    f32_ = 1.0 / (np.float32(10000.0) ** (np.arange(0, 32, 2, dtype=np.float32) / np.float32(32)))
    put("f64", f64[i % 32][:, None])
    put("f96", np.where((i >= HD) & (i < UQ), f32_[(i - HD) % 16], 0.0)[:, None])
    put("eps_rms", np.full((P, 1), RMS_EPS))
    put("eps_ln", np.full((P, 1), RWKV_EPS))
    put("zero", np.zeros((P, 1)))
    return c


def program(nc, A, out):
    ctx = ExitStack()
    with ctx:
        def sb(name, shape, dt=F32):
            return ctx.enter_context(nc.sbuf_tensor(name, shape, dt))

        sems = {}

        def sem(name):
            if name not in sems:
                sems[name] = ctx.enter_context(nc.semaphore(name))
            return sems[name]

        ring = sb("ring", [P, SLOTS, KT, T])
        const = sb("const", [P, NCONST])
        prow = sb("prow", [P, P])
        par = sb("par", [P, P])
        omka = sb("omka", [P, DEPTH * GT])
        lbc = sb("lbc", [P, DEPTH * GT])
        omlb = sb("omlb", [P, DEPTH * GT])
        lora = sb("lora", [P, DEPTH, G])
        g2 = sb("g2", [P, DEPTH, G])
        wuq = sb("wuq", [P, 2, NH * UQ])
        wukv = sb("wukv", [P, NH, 2 * HD])
        router = sb("router", [P, KT, NE])
        trig = sb("trig", [P, 4, T])
        xT = sb("xT", [P, KT, T])
        hT = sb("hT", [P, KT, T])
        wide = sb("wide", [P, KT, T])
        rstd = sb("rstd", [P, 2, T])
        proj = sb("proj", [P, 26, T])
        zeros = sb("zeros", [1, 640], BF16)
        diff = sb("diff", [P, GT, T])
        tw = sb("tw", [HD, T])
        sg = sb("sg", [P, T])
        rw = sb("rw", [P, 10, GT, T])
        kap, bet, kha, rha = (sb(n, [P, GT, T]) for n in ("kap", "bet", "kha", "rha"))
        mtm = sb("mtm", [P, NM, P])
        pin = sb("pin", [P, NM, P])
        vtok = sb("vtok", [P, TT, G])
        btok = sb("btok", [P, 2, G])
        rsol = sb("rsol", [P, NH, HD])
        usol = sb("usol", [P, TT, NH, HD])
        st = sb("st", [P, GT, HD])
        fac = sb("fac", [P, 2 * GT])
        hq = sb("hq", [P, 2, GT * T])
        hk = sb("hk", [P, 2, GT * T])
        hend = sb("hend", [P, GT * T])
        hs = sb("hs", [P, NM, P])
        hx = sb("hx", [P, NH, P])
        ssb = sb("ssb", [P, 2, 3 * P])
        pts = sb("pts", [P, 2, 3 * P])
        rtmp = sb("rtmp", [P, 2, T])
        mx = sb("mx", [P, 2, 2])
        den = sb("den", [P, 2, 2])
        sh = wide
        yT = hT
        SW, SA, CS, CP, KK, KM, WT, WI, GG, BN = range(10)

        def pair(buf, at):
            return buf[:, at:at + 2].rearrange("p s a (b c) -> p (s a b) c", c=P)

        atm, btm, ctm, dtm = (pair(rw, 2 * i) for i in range(4))
        xin = proj[:, 0:4].rearrange("p a (b c) -> p (a b) c", c=P)
        xit = proj[:, 4:8].rearrange("p a (b c) -> p (a b) c", c=P)
        mtok = proj[:, J_HF:J_HF + 2]
        qf = hq[0:UQ].rearrange("p a (h t) -> p (a h) t", t=T)
        kf = hk[0:UQ].rearrange("p a (h t) -> p (a h) t", t=T)
        ysb = diff
        gts = rw[:, 0:4, 0]
        hgat = rw[:, 4:6].rearrange("p s a b -> p (s a b)")[:, 0:KT * C].rearrange("p (k c) -> p k c", c=C)
        yjt = rw[:, 6:8].rearrange("p s a b -> p (s a b)")[:, 0:KT * C].rearrange("p (k c) -> p k c", c=C)
        yj = rw[:, 8:10].rearrange("p s a b -> p (s a b)")
        sel = kap[:, 0]
        pgt = bet[:, 0]
        rt = bet[:, 1]
        jt = kha[:, 0, 0:2 * MAXJOBS].bitcast(I32)
        idx = kha[:, 1, 0:16].bitcast(U32)
        posi = rtmp[:, 0].bitcast(I32)

        bank = [ctx.enter_context(nc.psum_tensor(f"bank{i}", [P, 512], F32)) for i in range(8)]

        def cst(name, rows=P):
            at, n = CCOL[name]
            return const[0:rows, at:at + n]

        def lvl(l):
            at = CCOL["lv"][0] + l * P
            return const[:, at:at + P]

        def prm(name, layer, j, lo=0, hi=P):
            at, n = PCOL[name]
            return par[lo:hi, at + layer * n + j:at + layer * n + j + 1]

        def over(ap, n):
            return ap.unsqueeze(1).broadcast_to([ap.shape[0], n, ap.shape[1]])

        block = ctx.enter_context(nc.Block())

        CH_D, CH_E = FF // P, FE // P
        PAIRS_D, PAIRS_E = CH_D // 2, CH_E // 2

        def last_unit(s):
            return max(u for u in range(LU) if u % SLOTS == s)


        def own(eng, chain):
            count = {}

            def settle(ins, sig=chain):
                ins.then_inc(sem(sig), 1)
                count[sig] = count.get(sig, 0) + 1
                eng.wait_ge(sem(sig), count[sig])
            return settle

        def wait(eng, name, n):
            if not isinstance(n, int) or n > 0:
                eng.wait_ge(sem(name), n)

        unit_loads = [len([u for u in range(LU) if u % SLOTS == s]) for s in range(SLOTS)]
        dense_loads = [(PAIRS_D + (1 if s < 3 else 0)) // 2 for s in range(SLOTS)]

        def before(phase, s):
            return [0, unit_loads[s], unit_loads[s] + dense_loads[s], 2 * unit_loads[s] + dense_loads[s]][phase]

        def pe_up(pe, half, s0, loads, g, cols, rhs):
            pe.wait_ge(sem("gated"), g + 1)
            for kind in range(2):
                if half == 0:
                    pe.wait_ge(sem(f"w_ready{s0 + kind}"), 16 * loads(s0 + kind))
                for k in range(KT):
                    ins = nc.tensor.matmul(bank[6 * kind + half][:, 0:cols],
                                           ring[:, s0 + kind, k, half * P:(half + 1) * P], rhs(k),
                                           start=k == 0, stop=k == KT - 1)
                ins.then_inc(sem("up_ready"), 1)

        def pe_down(pe, half, s0, loads, g, cols, acc):
            if half == 0:
                pe.wait_ge(sem(f"w_ready{s0 + 2}"), 16 * loads(s0 + 2))
            pe.wait_ge(sem("gated"), g + 3)
            w2 = ring[:, s0 + 2].rearrange("p (a b) t -> p a (b t)", a=2)
            for dt in range(KT):
                ins = nc.tensor.matmul(acc(dt), w2[:, half, dt * P:(dt + 1) * P], gts[:, 2 + half, 0:cols],
                                       start=False, stop=False, skip_group_check=True)
            ins.then_inc(sem("down_done"), 1)

        def pe_swiglu(pe, loads, g0, chunks, cols, rhs, acc):
            def step(i, c, up):
                if up:
                    m = c + 1
                    s0, nxt = 3 * (m // 2 % 2), i + m // 4
                    pe_up(pe, m % 2, s0, lambda s: loads(s, nxt), g0 + 4 * i + m, cols, rhs)
                s0 = 3 * (c // 2)
                pe_down(pe, c % 2, s0, lambda s: loads(s, i), g0 + 4 * i + c, cols, acc)

            pe_up(pe, 0, 0, lambda s: loads(s, 0), g0, cols, rhs)
            groups = (chunks - 1) // 4
            with pe.Fori(0, groups) as i:
                for c in range(4):
                    step(i, c, True)
            rest = chunks - 4 * groups
            for c in range(rest):
                step(groups, c, c < rest - 1)

        def zero_acc(pe, banks_, sig):
            for b in banks_:
                ins = nc.tensor.matmul(bank[b][:], zeros[:, 0:P], zeros[:, P:P + 512], start=True, stop=True)
                if sig and b in banks_[-2:]:
                    ins.then_inc(sem("down_done"), 1)

        def act_swiglu(act, g0, chunks, cols):
            with act.Fori(0, chunks // 2) as i:
                for half in range(2):
                    g = g0 + 2 * i + half
                    act.wait_ge(sem("gated"), g + 1)
                    act.wait_ge(sem("up_ready"), 2 * g + 1)
                    nc.scalar.activation(gts[:, half, 0:cols], bank[half][:, 0:cols], ACT.Silu, bias=cst("zero")
                                         ).then_inc(sem("silu_done"), 1)

        def dve_swiglu(dve, g0, chunks, cols):
            with dve.Fori(0, chunks // 2) as i:
                for half in range(2):
                    g = g0 + 2 * i + half
                    dve.wait_ge(sem("down_done"), g + 1)
                    dve.wait_ge(sem("up_ready"), 2 * g + 2)
                    dve.wait_ge(sem("silu_done"), g + 1)
                    nc.vector.tensor_tensor(gts[:, 2 + half, 0:cols], bank[6 + half][:, 0:cols], gts[:, half, 0:cols],
                                            ALU.mult).then_inc(sem("gated"), 1)

        def pe_ffn_dense(pe, mm, w_wait):
            pe.wait_ge(sem("hT_ready"), 2 * KT)
            zero_acc(pe, (2, 3, 4, 5), True)
            pe_swiglu(pe, lambda s, i: before(1, s) + i + 1, 0, CH_D, T, lambda k: hT[:, k],
                      lambda dt: bank[2 + dt // 2][:, dt % 2 * T:(dt % 2 + 1) * T])

        def act_ffn_dense(act):
            act_swiglu(act, 0, CH_D, T)

        def dve_ffn_dense(dve, tt_):
            dve_swiglu(dve, 0, CH_D, T)
            dve.wait_ge(sem("down_done"), 2 + CH_D)
            for u in range(NO):
                x = xT[:, 2 * u:2 * u + 2].rearrange("p a t -> p (a t)")
                tt_(x, x, bank[2 + u][:], ALU.add, "xT_ready" if u == NO - 1 else "dve_chain")

        rtc = {}
        _c = 0
        for _n, _w in (("logit", 16), ("top", 16), ("idx", 16), ("oh1", 16), ("oh2", 16), ("sel", 16), ("e", 2),
                       ("gate", 4), ("slot", 4), ("pos", 16), ("cnt", 8), ("blk", 8), ("cum", 8), ("start", 8),
                       ("tmp", 16), ("job", MAXJOBS + 1)):
            rtc[_n] = (_c, _w)
            _c += _w
        assert _c <= T

        def R(name, i=0, n=None):
            at, w = rtc[name]
            return rt[:, at + i:at + (w if n is None else i + n)]

        def jobs_of(eng):
            eng.wait_ge(sem("jobs_ready"), 1)
            return eng.value_load(jt[0:1, MAXJOBS:MAXJOBS + 1], min_val=1, max_val=MAXJOBS - 1)

        def hrows():
            return wide[:].rearrange("p (a b) t -> p a (b t)", a=TT)

        def moe_acc(dt):
            return bank[2 + dt // 4][:, dt % 4 * C:(dt % 4 + 1) * C]

        def pe_moe(pe, mm, turn, w_wait):
            pe.wait_ge(sem("hT_ready"), 4 * KT)
            for b in range(4):
                for k in range(2):
                    for tt in range(TT):
                        turn(bank[b][:, tt * T + k * P:tt * T + (k + 1) * P], hT[:, 2 * b + k, tt * P:(tt + 1) * P],
                             sig="h_turned" if k and tt else None)
            pe.wait_ge(sem("router_in"), 16)
            for tt in range(TT):
                for k in range(KT):
                    mm(bank[7][:, tt * NE:(tt + 1) * NE], hT[:, k, tt * P:(tt + 1) * P], router[:, k], k == 0, k == KT - 1,
                       "logits_ready" if tt and k == KT - 1 else None)
            pe.wait_ge(sem("sel_ready"), 1)
            mm(bank[6][:, 0:NE], cst("ups"), R("sel", 0, NE))
            mm(bank[6][:, NE:2 * NE], cst("ups"), R("sel", NE, NE), True, False)
            mm(bank[6][:, NE:2 * NE], cst("ones"), R("sel", 0, NE), False, True)
            mm(bank[6][:, 2 * NE:3 * NE], cst("ones"), R("sel", 0, NE), True, False)
            mm(bank[6][:, 2 * NE:3 * NE], cst("ones"), R("sel", NE, NE), False, True, "pos_ready")
            pe.wait_ge(sem("h_copied"), 4)
            n_jobs = jobs_of(pe)
            with pe.Fori(0, n_jobs) as j:
                pe.wait_ge(sem("sel_built"), j + 1)
                pe.wait_ge(sem("jobs_ready"), j + 1)
                for half in range(2):
                    for d in range(4):
                        for tt in range(TT):
                            k = 4 * half + d
                            mm(bank[6 + half][:, d * C:(d + 1) * C], hrows()[:, tt, k * P:(k + 1) * P],
                               kap[:, 0, tt * C:(tt + 1) * C], tt == 0, tt == 1,
                               "gathered" if d == 3 and tt else None)
                for tt in range(TT):
                    turn(bank[4][0:C, tt * P:(tt + 1) * P], kap[:, 1, tt * C:(tt + 1) * C], sig="gathered" if tt else None)
                zero_acc(pe, (2, 3), False)
                pe.wait_ge(sem("gather_copied"), 3 * j + 2)
                pe_swiglu(pe, lambda s, i: before(3, s) + (PAIRS_E // 2) * j + i + 1, CH_D + CH_E * j, CH_E, C,
                          lambda k: hgat[:, k], moe_acc)
                for half in range(2):
                    pe.wait_ge(sem("acc_copied"), 4 * j + half + 1)
                    for d in range(4):
                        turn(bank[6 + half][0:C, d * P:(d + 1) * P], yjt[:, 4 * half + d], sig="acc_turned" if d == 3 else None)
                pe.wait_ge(sem("gather_copied"), 3 * j + 3)
                pe.wait_ge(sem("acc_copied"), 4 * j + 4)
                for b in range(4):
                    for k in range(2):
                        dt = 2 * b + k
                        mm(bank[4 + b][:, k * T:(k + 1) * T], yj[0:C, dt * P:(dt + 1) * P], pgt[0:C, :],
                           sig="scattered" if k else None)

        def act_moe(act, copy, f):
            for b in range(4):
                act.wait_ge(sem("h_turned"), b + 1)
                copy(hrows()[:, :, b * T:(b + 1) * T], bank[b][:].rearrange("p (a t) -> p a t", a=TT), "h_copied")
            act.wait_ge(sem("gate_logit"), 1)
            f(R("e"), R("e"), ACT.Exp, "gate_exp")
            n_jobs = jobs_of(act)
            with act.Fori(0, n_jobs) as j:
                for half in range(2):
                    act.wait_ge(sem("gathered"), 3 * j + half + 1)
                    nc.scalar.copy(hgat[:, 4 * half:4 * half + 4].rearrange("p k c -> p (k c)"),
                                   bank[6 + half][:, 0:4 * C]).then_inc(sem("gather_copied"), 1)
                act.wait_ge(sem("gathered"), 3 * j + 3)
                nc.scalar.copy(pgt[0:C, :], bank[4][0:C, 0:T]).then_inc(sem("gather_copied"), 1)
                act_swiglu(act, CH_D + CH_E * j, CH_E, C)
                act.wait_ge(sem("down_done"), 2 + CH_D + CH_E + CH_E * j)
                for half in range(2):
                    nc.scalar.copy(yjt[:, 4 * half:4 * half + 4].rearrange("p k c -> p (k c)"),
                                   bank[2 + half][:, 0:4 * C]).then_inc(sem("acc_copied"), 1)
                for half in range(2):
                    act.wait_ge(sem("acc_turned"), 2 * j + half + 1)
                    nc.scalar.copy(yj[0:C, half * 512:(half + 1) * 512], bank[6 + half][0:C, :]
                                   ).then_inc(sem("acc_copied"), 1)

        def dve_moe(dve, settle, tt_, ts, stt, recip):
            iota8 = cst("iota")[:, 0:NE]
            dve.wait_ge(sem("logits_ready"), 1)
            settle(nc.vector.tensor_copy(R("logit"), bank[7][:, 0:TT * NE]))
            for tt in range(TT):
                settle(nc.vector.max(R("top", tt * 8, 8), R("logit", tt * NE, NE)))
                settle(nc.vector.max_index(idx[:, tt * 8:(tt + 1) * 8], R("top", tt * 8, 8), R("logit", tt * NE, NE)))
            settle(nc.vector.tensor_copy(R("idx"), idx))
            for tt in range(TT):
                ts(R("oh1", tt * NE, NE), iota8, R("idx", tt * 8, 1), None, ALU.is_equal)
                ts(R("oh2", tt * NE, NE), iota8, R("idx", tt * 8 + 1, 1), None, ALU.is_equal)
                tt_(R("e", tt, 1), R("top", tt * 8 + 1, 1), R("top", tt * 8, 1), ALU.subtract,
                    "gate_logit" if tt else "dve_chain")
            tt_(R("sel"), R("oh1"), R("oh2"), ALU.add, "sel_ready")
            dve.wait_ge(sem("gate_exp"), 1)
            for tt in range(TT):
                ts(R("gate", 2 * tt, 1), R("e", tt, 1), 1.0, None, ALU.add)
                recip(R("gate", 2 * tt, 1), R("gate", 2 * tt, 1))
                tt_(R("gate", 2 * tt + 1, 1), R("gate", 2 * tt, 1), R("e", tt, 1), ALU.mult)
            dve.wait_ge(sem("pos_ready"), 1)
            settle(nc.vector.tensor_copy(R("pos"), bank[6][:, 0:2 * NE]))
            settle(nc.vector.tensor_copy(R("cnt"), bank[6][:, 2 * NE:3 * NE]))
            ts(R("blk"), R("cnt"), 0.0, None, ALU.is_gt)
            for b in range(1, -(-T // C)):
                stt(R("blk"), R("cnt"), float(b * C), R("blk"), ALU.is_gt, ALU.add)
            settle(nc.vector.tensor_tensor_scan(R("cum"), cst("ones")[:, 0:NE], R("blk"), 0.0, ALU.mult, ALU.add))
            tt_(R("start"), R("cum"), R("blk"), ALU.subtract)
            ts(R("start"), R("start"), float(C), None, ALU.mult)
            for tt in range(TT):
                tt_(R("pos", tt * NE, NE), R("pos", tt * NE, NE), R("start"), ALU.add)
                for i, oh in enumerate(("oh1", "oh2")):
                    tt_(R("tmp", 0, NE), R(oh, tt * NE, NE), R("pos", tt * NE, NE), ALU.mult)
                    settle(nc.vector.tensor_reduce(R("slot", 2 * tt + i, 1), R("tmp", 0, NE), AX.X, ALU.add))
            iota16 = cst("iota")[:, 0:MAXJOBS]
            ts(R("job", 0, MAXJOBS), iota16, R("cum", 0, 1), None, ALU.is_ge)
            for e in range(1, NE):
                stt(R("job", 0, MAXJOBS), iota16, R("cum", e, 1), R("job", 0, MAXJOBS), ALU.is_ge, ALU.add)
            settle(nc.vector.tensor_copy(R("job", MAXJOBS, 1), R("cum", NE - 1, 1)))
            settle(nc.vector.tensor_copy(jt[:, 0:MAXJOBS + 1], R("job")), "jobs_ready")
            n_jobs = jobs_of(dve)
            chain = sem("job_chain")
            STEPS = 14
            with dve.Fori(0, n_jobs) as j:
                done = [0]

                def step(ins):
                    done[0] += 1
                    ins.then_inc(chain, 1)
                    dve.wait_ge(chain, STEPS * j + done[0])

                iota = cst("iota")[:, 0:C]
                for tt in range(TT):
                    s1, s2 = R("slot", 2 * tt, 1), R("slot", 2 * tt + 1, 1)
                    o = kap[:, 0, tt * C:(tt + 1) * C]
                    og = kap[:, 1, tt * C:(tt + 1) * C]
                    step(nc.vector.tensor_scalar(o, iota, s1, None, ALU.is_equal))
                    step(nc.vector.scalar_tensor_tensor(o, iota, s2, o, ALU.is_equal, ALU.add))
                    step(nc.vector.tensor_scalar(og, iota, s1, R("gate", 2 * tt, 1), ALU.is_equal, ALU.mult))
                    step(nc.vector.tensor_scalar(diff[:, 0, 0:C], iota, s2,
                                                 R("gate", 2 * tt + 1, 1), ALU.is_equal, ALU.mult))
                    step(nc.vector.tensor_tensor(og, og, diff[:, 0, 0:C], ALU.add))
                nc.vector.tensor_scalar(R("slot"), R("slot"), -float(C), None, ALU.add).then_inc(sem("sel_built"), 1)
                dve_swiglu(dve, CH_D + CH_E * j, CH_E, C)
                dve.wait_ge(sem("sel_built"), j + 1)
                for b in range(4):
                    dve.wait_ge(sem("scattered"), 4 * j + b + 1)
                    x = xT[:, 2 * b:2 * b + 2].rearrange("p a t -> p (a t)")
                    ins = nc.vector.tensor_tensor(x, x, bank[4 + b][:], ALU.add)
                    if b < 3:
                        step(ins)
                    else:
                        ins.then_inc(sem("jobs_ready"), 1)
                        dve.wait_ge(sem("jobs_ready"), j + 2)
                step(nc.vector.memset(mx[:, 0, 0:1], 0.0))
                assert done[0] == STEPS
            settle(nc.vector.memset(mx[:, 0, 0:1], 0.0), "xT_ready")

        @block.sync
        def _(sp):
            def load(slot, dst, src):
                sp.dma_start(dst, src).then_inc(sem(f"w_ready{slot}"), 16)

            def columns(slot, w, at, n):
                load(slot, ring[:, slot, :, 0:n], w[:, at:at + n].rearrange("(k p) n -> p k n", p=P))

            def mixer_unit(layer, u):
                if u < NU:
                    columns(u % SLOTS, A["w_in"][layer], UNITS[u][0], UNITS[u][1])
                else:
                    columns(u % SLOTS, A["w_out"][layer], (u - NU) * T, T)

            def rows(slot, w, at):
                load(slot, ring[:, slot].rearrange("p (a b) t -> p a (b t)", a=2),
                     w[at:at + 2 * P, :].rearrange("(a p) d -> p a d", p=P))

            sp.dma_start(const[:], A["const"]).then_inc(sem("const_in"), 16)
            sp.dma_start(wide[:].rearrange("p (a b) t -> p a (b t)", a=TT),
                         A["x"][0].rearrange("(a p) d -> p a d", p=P)).then_inc(sem("x_in"), 16)
            for layer in range(DEPTH):
                for u in range(LU):
                    slot = u % SLOTS
                    if u >= SLOTS:
                        sp.wait_ge(sem("unit_used"), layer * LU + u - SLOTS + 1)
                    elif layer:
                        q = PAIRS_D + 1 if slot < 3 else PAIRS_D
                        wait(sp, "down_done", 2 * q)
                    mixer_unit(layer, u)
                if layer == 0:
                    w1, w3, w2 = A["ffn_w1"][0], A["ffn_w3"][0], A["ffn_w2"][0]
                    for q in range(2):
                        for kind, w in enumerate((w1, w3)):
                            s = 3 * q + kind
                            sp.wait_ge(sem("unit_used"), last_unit(s) + 1)
                            columns(s, w, q * T, T)
                        s = 3 * q + 2
                        sp.wait_ge(sem("unit_used"), last_unit(s) + 1)
                        rows(s, w2, q * T)

                    def pair_d(q, s0):
                        sp.wait_ge(sem("up_ready"), 4 * q - 5)
                        sp.dma_start(ring[:, s0], w1[:, bass.ds(q * T, T)].rearrange("(k p) n -> p k n", p=P)
                                     ).then_inc(sem(f"w_ready{s0}"), 16)
                        sp.wait_ge(sem("up_ready"), 4 * q - 4)
                        sp.dma_start(ring[:, s0 + 1], w3[:, bass.ds(q * T, T)].rearrange("(k p) n -> p k n", p=P)
                                     ).then_inc(sem(f"w_ready{s0 + 1}"), 16)
                        sp.wait_ge(sem("down_done"), 2 * q)
                        sp.dma_start(ring[:, s0 + 2].rearrange("p (a b) t -> p a (b t)", a=2),
                                     w2[bass.ds(q * T, T), :].rearrange("(a p) d -> p a d", p=P)
                                     ).then_inc(sem(f"w_ready{s0 + 2}"), 16)

                    with sp.Fori(1, PAIRS_D // 2) as i:
                        pair_d(2 * i, 0)
                        pair_d(2 * i + 1, 3)
                    pair_d(PAIRS_D - 1, 0)

            for s in range(SLOTS):
                sp.wait_ge(sem("unit_used"), LU + last_unit(s) + 1)
            sp.wait_ge(sem("jobs_ready"), 1)
            n_jobs = sp.value_load(jt[0:1, MAXJOBS:MAXJOBS + 1], min_val=1, max_val=MAXJOBS - 1)
            w1, w3 = (A[n][0].rearrange("e d f -> (e d) f") for n in ("moe_w1", "moe_w3"))
            w2 = A["moe_w2"][0].rearrange("e f d -> (e f) d")
            with sp.Fori(0, n_jobs) as j:
                e = sp.value_load(jt[0:1, bass.ds(j, 1)], min_val=0, max_val=NE - 1)
                with sp.Fori(0, PAIRS_E // 2) as i:
                    for half in range(2):
                        q = PAIRS_D + PAIRS_E * j + 2 * i + half
                        s0 = 3 * half
                        at = 2 * T * i + T * half
                        sp.wait_ge(sem("up_ready"), 4 * q - 5)
                        sp.dma_start(ring[:, s0], w1[bass.ds(e * D, D), bass.ds(at, T)]
                                     .rearrange("(k p) n -> p k n", p=P)).then_inc(sem(f"w_ready{s0}"), 16)
                        sp.wait_ge(sem("up_ready"), 4 * q - 4)
                        sp.dma_start(ring[:, s0 + 1], w3[bass.ds(e * D, D), bass.ds(at, T)]
                                     .rearrange("(k p) n -> p k n", p=P)).then_inc(sem(f"w_ready{s0 + 1}"), 16)
                        sp.wait_ge(sem("down_done"), 2 * q)
                        sp.dma_start(ring[:, s0 + 2].rearrange("p (a b) t -> p a (b t)", a=2),
                                     w2[bass.ds(e * FE + at, T), :].rearrange("(a p) d -> p a d", p=P)
                                     ).then_inc(sem(f"w_ready{s0 + 2}"), 16)
            sp.wait_ge(sem("out_ready"), KT // 2)
            sp.dma_start(out[0].rearrange("(a p) d -> p a d", p=P),
                         wide[:].rearrange("p (a b) t -> p a (b t)", a=TT)).then_inc(sem("out_stored"), 16)
            sp.wait_ge(sem("out_stored"), 16)

        @block.gpsimd
        def _(pool):
            settle = own(pool, "pool_chain")
            for name, n in PARAMS:
                at = PCOL[name][0]
                pool.dma_start(prow[at:at + DEPTH * n, :], A[name].rearrange("l (t p) -> (l t) p", p=P)
                               ).then_inc(sem("prow_in"), 16)
            at = PCOL["final_norm"][0]
            pool.dma_start(prow[at:at + KT, :], A["final_norm"].rearrange("(t p) -> t p", p=P)
                           ).then_inc(sem("prow_in"), 16)
            pool.dma_start(posi, A["positions"].broadcast_to([P, T])).then_inc(sem("pos_in"), 16)
            pool.dma_start(lora[0:HD], A["rwkv_w2"].rearrange("l r g -> r l g")).then_inc(sem("lora_in"), 16)
            pool.dma_start(lora[HD:P], A["rwkv_a2"].rearrange("l r g -> r l g")).then_inc(sem("lora_in"), 16)
            pool.dma_start(g2[:], A["rwkv_g2"].rearrange("l r g -> r l g")).then_inc(sem("lora_in"), 16)
            pool.dma_start(router[:], A["moe_router"][0].rearrange("(k p) e -> p k e", p=P)
                           ).then_inc(sem("router_in"), 16)

            def mla_weights(layer):
                pool.dma_start(wuq[:], A["mla_w_uq"][layer].rearrange("(k p) n -> p k n", p=P)
                               ).then_inc(sem("mla_w_in"), 16)
                pool.dma_start(wukv[:].rearrange("p h n -> p (h n)"), A["mla_w_ukv"][layer]
                               ).then_inc(sem("mla_w_in"), 16)

            mla_weights(0)
            pool.wait_ge(sem("omlb_ready"), 1)
            for layer in range(DEPTH):
                if layer:
                    pool.wait_ge(sem("mla_v_ready"), layer)
                    mla_weights(layer)
                pool.wait_ge(sem("hsig_ready"), 3 * layer + 3)
                fq = proj[:, J_HQ:J_HQ + 2].rearrange("p a t -> p (a t)")
                ff = proj[:, J_HF:J_HF + 2].rearrange("p a t -> p (a t)")
                fg = proj[:, J_HG:J_HG + 2].rearrange("p a t -> p (a t)")
                flat = hs[:].rearrange("p a b -> p (a b)")
                sf, sq = flat[:, 0:2 * T], flat[:, 2 * T:4 * T]
                sgt = hx[:].rearrange("p a b -> p (a b)")
                settle(nc.gpsimd.tensor_tensor(fq, fq, sq, ALU.mult))
                settle(nc.gpsimd.tensor_tensor(fg, fg, sgt, ALU.mult))
                for j in range(GT):
                    c = layer * GT + j
                    settle(nc.gpsimd.tensor_scalar(ff[:, j * T:(j + 1) * T], sf[:, j * T:(j + 1) * T],
                                                   omlb[:, c:c + 1], lbc[:, c:c + 1], ALU.mult, ALU.add))
                settle(nc.gpsimd.tensor_scalar(hk[:, 0], ff, -1.0, 1.0, ALU.mult, ALU.add), "hgrn_level")
                ends = ff
                for l in range(LEVELS + 1):
                    n = 1 << l
                    new, old = l % 2, (l + 1) % 2
                    if l == 0:
                        settle(nc.gpsimd.tensor_tensor(hq[:, 0], fq, ff, ALU.mult), "hgrn_level")
                        continue
                    half = n // 2
                    nb = GT * T // n
                    qo = hq[:, old].rearrange("p (b h i) -> p b h i", h=2, i=half)
                    qn = hq[:, new].rearrange("p (b h i) -> p b h i", h=2, i=half)
                    ko = hk[:, old].rearrange("p (b h i) -> p b h i", h=2, i=half)
                    kn = hk[:, new].rearrange("p (b h i) -> p b h i", h=2, i=half)
                    ev = ends.rearrange("p (b h) -> p b h", h=2)
                    if l >= 2:
                        pool.wait_ge(sem("hgrn_scored"), layer * 16 + 2 * l)
                    else:
                        pool.wait_ge(sem("hgrn_scored"), layer * 16 + 2)
                    nxt = hend[:, GT * T - 2 * nb:GT * T - nb]
                    e1 = ev[:, :, 0:1].broadcast_to([P, nb, half])
                    e2 = ev[:, :, 1:2].broadcast_to([P, nb, half])
                    settle(nc.gpsimd.tensor_tensor(qn[:, :, 1], qo[:, :, 1], e1, ALU.mult))
                    settle(nc.gpsimd.tensor_copy(qn[:, :, 0], qo[:, :, 0]))
                    settle(nc.gpsimd.tensor_tensor(kn[:, :, 0], ko[:, :, 0], e2, ALU.mult))
                    settle(nc.gpsimd.tensor_tensor(nxt, ev[:, :, 0], ev[:, :, 1], ALU.mult))
                    settle(nc.gpsimd.tensor_copy(kn[:, :, 1], ko[:, :, 1]), "hgrn_level")
                    ends = nxt
                pool.wait_ge(sem("chunk_masked"), 4 * layer + 1)
                for l in range(1, LEVELS):
                    for half in range(2):
                        if l > 1:
                            pool.wait_ge(sem("mx_ready"), 12 * layer + 2 * (l - 2) + half + 1)
                        hv = slice(4 * half, 4 * half + 4)
                        settle(nc.gpsimd.tensor_tensor(mtm[:, hv], atm[:, hv], over(lvl(l), 4), ALU.mult), "level_masked")

        @block.tensor
        def _(pe):
            def mm(o, l, r, start=True, stop=True, sig=None):
                ins = nc.tensor.matmul(o, l, r, start=start, stop=stop)
                if sig:
                    ins.then_inc(sem(sig), 1)

            def turn(o, i, rows=P, sig=None):
                ins = nc.tensor.transpose(o, i, cst("id")[0:rows, 0:rows])
                if sig:
                    ins.then_inc(sem(sig), 1)

            def w_wait(slot, n):
                pe.wait_ge(sem(f"w_ready{slot}"), 16 * n)

            def norm(n):
                for half in range(2):
                    pe.wait_ge(sem("sq_ready"), 2 * n + half + 1)
                    for k in range(4 * half, 4 * half + 4):
                        mm(bank[7][:, 0:T], cst("ones"), wide[:, k], k == 0, k == KT - 1,
                           "ss_ready" if k == KT - 1 else None)

            pe.wait_ge(sem("const_in"), 16)
            pe.wait_ge(sem("x_in"), 16)
            xr = wide[:].rearrange("p (a b) t -> p a (b t)", a=TT)
            for b in range(4):
                for k in range(2):
                    for tt in range(TT):
                        turn(bank[b][:, k * T + tt * P:k * T + (tt + 1) * P],
                             xr[:, tt, (2 * b + k) * P:(2 * b + k + 1) * P],
                             sig="x_turned" if k == 1 and tt == TT - 1 else None)
            pe.wait_ge(sem("prow_in"), 16 * (len(PARAMS) + 1))
            turn(bank[4][:, 0:NPAR], prow[0:NPAR, :], NPAR, "par_turned")

            def unit(layer, u):
                slot, b = u % SLOTS, u % 2
                _, cols, token_major = UNITS[u]
                w_wait(slot, before(2 * layer, slot) + u // SLOTS + 1)
                if u >= 2:
                    pe.wait_ge(sem("unit_copied"), layer * NU + u - 1)
                if token_major:
                    for tt in range(TT):
                        for k in range(KT):
                            mm(bank[b][:, tt * G:(tt + 1) * G], hT[:, k, tt * P:(tt + 1) * P],
                               ring[:, slot, k, 0:G], k == 0, k == KT - 1,
                               "unit_used" if tt == 1 and k == KT - 1 else None)
                    return
                for ct in range(2):
                    n = min(P, cols - ct * P)
                    lo = HD if n < P else 0
                    for k in range(KT):
                        if u == 0 and ct == 0:
                            pe.wait_ge(sem("hT_ready"), 2 * layer * KT + k + 1)
                        mm(bank[b][lo:lo + n, ct * T:(ct + 1) * T], ring[:, slot, k, ct * P:ct * P + n], hT[:, k],
                           k == 0, k == KT - 1, "unit_used" if ct == 1 and k == KT - 1 else None)

            def rows(h):
                lo = HD * (h % 2)
                return lo, lo + HD, h // 2

            def mat(h, c):
                return 4 * (h % 2) + 2 * (h // 2) + c

            for layer in range(DEPTH):
                def nth(per, i=0):
                    return layer * per + i + 1

                norm(2 * layer)
                for u in range(8):
                    unit(layer, u)
                if layer == 0:
                    pe.wait_ge(sem("lora_in"), 48)
                pe.wait_ge(sem("tw_ready"), nth(2))
                for j in range(GT):
                    mm(bank[2][:, j * T:(j + 1) * T], lora[0:HD, layer, j * P:(j + 1) * P], tw[:],
                       sig="lora_ready" if j else None)
                for j in range(GT):
                    mm(bank[3][:, j * T:(j + 1) * T], lora[HD:P, layer, j * P:(j + 1) * P], sh[HD:P, 6],
                       sig="lora_ready" if j else None)
                pe.wait_ge(sem("tw_ready"), nth(2, 1))
                for j in range(GT):
                    mm(bank[4][:, j * T:(j + 1) * T], g2[:, layer, j * P:(j + 1) * P], sg[:],
                       sig="lora_ready" if j else None)
                pe.wait_ge(sem("kksq_ready"), nth(1))
                mm(bank[5][:], cst("blk"), diff[:].rearrange("p a t -> p (a t)"), sig="kkss_ready")
                for u in range(8, 11):
                    unit(layer, u)
                for e in range(LEVELS + 1):
                    pe.wait_ge(sem("hgrn_level"), nth(9, 0 if e == 0 else e))
                    for half in range(2):
                        if e or layer:
                            pe.wait_ge(sem("hgrn_masked"), layer * 16 + 2 * e + half - 1)
                        for m in range(4):
                            h, c = 2 * (m // 2) + half, m % 2
                            lo, hi, j = rows(h)
                            s = slice(j * T + c * P, j * T + (c + 1) * P)
                            src = hk[lo:hi, 0 if e == 0 else (e - 1) % 2, s]
                            qry = (proj[lo:hi, J_HQ + j, c * P:(c + 1) * P] if e == 0
                                   else hq[lo:hi, (e - 1) % 2, s])
                            mm(bank[6 + half][:, m * P:(m + 1) * P], src, qry, sig="hgrn_scored" if m == 3 else None)
                pe.wait_ge(sem("hgrn_level"), nth(9, 8))
                pe.wait_ge(sem("hgrn_masked"), nth(16, 14))
                pe.wait_ge(sem("hgrn_masked"), nth(16, 15))
                for h in range(NH):
                    lo, hi, j = rows(h)
                    mm(bank[6 + h % 2][:, j * P:(j + 1) * P], hk[lo:hi, 1, j * T:j * T + P],
                       hq[lo:hi, 1, j * T + P:j * T + T], sig="hgrn_crossed" if h == NH - 1 else None)
                for u in range(11, NU):
                    unit(layer, u)
                pe.wait_ge(sem("rkk_ready"), nth(1))
                mm(bank[5][:], cst("blk"), diff[:].rearrange("p a t -> p (a t)"), sig="bonus_ready")
                pe.wait_ge(sem("sig_ready"), nth(5, 4))
                for c in range(TT):
                    for j in range(GT):
                        turn(bank[2][:, c * G + j * P:c * G + (j + 1) * P], sh[:, J_V + j, c * P:(c + 1) * P],
                             sig="tok_turned" if c and j else None)
                pe.wait_ge(sem("chunks_ready"), nth(1))
                for i, a in enumerate((bet, kha)):
                    for j in range(GT):
                        turn(bank[3][:, i * G + j * P:i * G + (j + 1) * P], a[:, j, 0:P],
                             sig="tok_turned" if i and j else None)
                for n, (a, b, bk) in enumerate(((bet, kap, 4), (kha, kap, 6), (bet, rha, 4), (kha, rha, 6))):
                    if n == 0:
                        pe.wait_ge(sem("bonus_used"), nth(1))
                    elif n == 1:
                        pe.wait_ge(sem("hgrn_masked"), nth(16, 15))
                        pe.wait_ge(sem("hx_copied"), nth(1))
                    else:
                        pe.wait_ge(sem("chunk_masked"), nth(4, n - 2))
                    for m in range(NM):
                        h, c = 2 * (m // 2 % 2) + m // 4, m % 2
                        lo, hi, j = rows(h)
                        mm(bank[bk + m // 4][:, m % 4 * P:(m % 4 + 1) * P], a[lo:hi, j, c * P:(c + 1) * P],
                           b[lo:hi, j, c * P:(c + 1) * P], sig="chunk_ready" if m == NM - 1 else None)
                pe.wait_ge(sem("xit_ready"), nth(2 * LEVELS, 1))
                pe.wait_ge(sem("tok_copied"), nth(2, 1))
                for half in range(2):
                    for m in range(4):
                        turn(bank[2 + half][:, m * P:(m + 1) * P], xit[:, 4 * half + m], sig="xt_turned" if m == 3 else None)
                for l in range(1, LEVELS):
                    last = l == LEVELS - 1
                    for half in range(2):
                        pe.wait_ge(sem("level_masked"), nth(2 * (LEVELS - 1), 2 * (l - 1) + half))
                        pe.wait_ge(sem("xin_ready"), nth(2 * (LEVELS - 1), 2 * (l - 1) + half))
                        for m in range(4):
                            mm(bank[2 + half][:, m * P:(m + 1) * P], mtm[:, 4 * half + m], xin[:, 4 * half + m],
                               sig="mx_ready" if m == 3 else None)
                    for half in range(2):
                        pe.wait_ge(sem("pin_ready"), nth(2 * (LEVELS - 1), 2 * (l - 1) + half))
                        if l == 1 and half == 0:
                            pe.wait_ge(sem("chunk_masked"), nth(4, 3))
                        pe.wait_ge(sem("xit_ready"), nth(2 * LEVELS, 2 * (l - 1) + half))
                        if not last:
                            for m in range(4):
                                mm(bank[4 + half][:, m * P:(m + 1) * P], xit[:, 4 * half + m], pin[:, 4 * half + m],
                                   sig="xmx_ready" if m == 3 else None)
                        for m in range(4):
                            mm(bank[6 + half][:, m * P:(m + 1) * P], pin[:, 4 * half + m], xit[:, 4 * half + m],
                               sig="xmx_t_ready" if m == 3 else None)
                pe.wait_ge(sem("xit_ready"), nth(2 * LEVELS, 2 * LEVELS - 1))
                for c in range(TT):
                    for h in range(NH):
                        lo, hi, j = rows(h)
                        o = bank[2 + h % 2][:, j * HD:(j + 1) * HD]
                        if c:
                            if h == 0:
                                pe.wait_ge(sem("state_ready"), nth(1))
                            mm(o, kap[lo:hi, j, P:T], st[lo:hi, j], True, False)
                        mm(o, btm[:, mat(h, c)], vtok[:, c, h * HD:(h + 1) * HD], c == 0, True,
                           "r_ready" if h == NH - 1 else None)
                    pe.wait_ge(sem("rsol_ready"), nth(2, c))
                    for h in range(NH):
                        mm(bank[6][:, h * HD:(h + 1) * HD], xit[:, mat(h, c)], rsol[:, h],
                           sig="u_ready" if h == NH - 1 else None)
                    pe.wait_ge(sem("usol_ready"), nth(2, c))
                    if c == 0:
                        for h in range(NH):
                            lo, hi, j = rows(h)
                            o = bank[4][lo:hi, j * HD:(j + 1) * HD]
                            mm(o, btok[:, 0, h * HD:(h + 1) * HD], usol[:, 0, h], True, False)
                            mm(o, btok[:, 1, h * HD:(h + 1) * HD], vtok[:, 0, h * HD:(h + 1) * HD], False, True,
                               "state_summed" if h == NH - 1 else None)
                for h in range(NH):
                    lo, hi, j = rows(h)
                    for c in range(TT):
                        o = bank[5 - h % 2][lo:hi, j * T + c * P:j * T + (c + 1) * P]
                        if c:
                            mm(o, st[lo:hi, j], rha[lo:hi, j, P:T], True, False)
                        mm(o, usol[:, c, h], ctm[:, mat(h, c)], c == 0, False)
                        mm(o, vtok[:, c, h * HD:(h + 1) * HD], dtm[:, mat(h, c)], False, True,
                           "y_ready" if c and h == NH - 1 else None)
                pe.wait_ge(sem("ysb_ready"), nth(1))
                mm(bank[6][:], cst("blk"), ysb[:].rearrange("p a t -> p (a t)"), sig="mean_ready")
                pe.wait_ge(sem("ysq_ready"), nth(1))
                mm(bank[7][:], cst("blk"), mtm[:, 0:4].rearrange("p a t -> p (a t)"), sig="var_ready")
                pe.wait_ge(sem("unit_copied"), nth(NU, NU - 1))
                for h in range(NH):
                    lo, hi, j = rows(h)
                    it = [proj[:, J_HI + c, h * HD:(h + 1) * HD] for c in range(TT)]
                    mm(bank[0][lo:hi, j * T:j * T + P], it[0], hs[:, mat(h, 0)])
                    mm(bank[0][lo:hi, j * T + P:j * T + T], it[0], hx[:, h], True, False)
                    mm(bank[0][lo:hi, j * T + P:j * T + T], it[1], hs[:, mat(h, 1)], False, True,
                       "ho_ready" if h == NH - 1 else None)
                pe.wait_ge(sem("hosq_ready"), nth(1))
                mm(bank[1][:], cst("blk"), pin[:, 0:4].rearrange("p a t -> p (a t)"), sig="hoss_ready")
                for i, at in enumerate((J_DQ, J_DK)):
                    mm(bank[2 + i][:], cst("r64"), proj[:, at:at + 2].rearrange("p a t -> p (a t)"), sig="partner_ready")

                def attend(kind, h, query, key, value, ready):
                    lo, hi, j = rows(h)
                    n = kind * NH + h
                    b = n % 2
                    pe.wait_ge(sem(ready[0]), ready[1])
                    if n >= 2:
                        pe.wait_ge(sem("scores_used"), nth(2 * NH, n - 2))
                    mm(bank[4 + b][:, 0:P], query(0), key(0, P))
                    mm(bank[4 + b][:, P:3 * P], query(1), key(0, T), sig="scores_ready")

                def attend2(kind, h, value):
                    lo, hi, j = rows(h)
                    n = kind * NH + h
                    b = n % 2
                    pe.wait_ge(sem("probs_ready"), nth(2 * NH, n))
                    if n >= 2:
                        pe.wait_ge(sem("pts_ready"), nth(2 * NH, n - 2))
                    elif n == 0:
                        pe.wait_ge(sem("var_used"), nth(1))
                    turn(bank[6 + b][:, 0:P], ssb[:, b, 0:P])
                    turn(bank[6 + b][:, P:T], ssb[:, b, P:2 * P])
                    turn(bank[6 + b][:, T:3 * P], ssb[:, b, 2 * P:3 * P], sig="pts_turned")
                    pe.wait_ge(sem("pts_ready"), nth(2 * NH, n))
                    if n == 0:
                        pe.wait_ge(sem("ho_used"), nth(1))
                    if n == NH:
                        pe.wait_ge(sem("attn_copied"), nth(2))
                    o = bank[0]
                    mm(o[lo:hi, j * T:(j + 1) * T], value(0), pts[:, b, 0:T], True, False)
                    mm(o[lo:hi, j * T + P:(j + 1) * T], value(1), pts[:, b, T:3 * P], False, True, "attended")

                def dq(h):
                    lo, hi, j = rows(h)
                    return lambda qt: proj[lo:hi, J_DQ + j, qt * P:(qt + 1) * P]

                def dk(h):
                    lo, hi, j = rows(h)
                    return lambda a, b: proj[lo:hi, J_DK + j, a:b]

                for h in range(NH):
                    attend(0, h, dq(h), dk(h), None, ("rope_ready", nth(2, 1)))
                    if h:
                        attend2(0, h - 1, lambda kt, h=h - 1: proj[:, J_DV + kt, h * HD:(h + 1) * HD])
                attend2(0, NH - 1, lambda kt: proj[:, J_DV + kt, (NH - 1) * HD:NH * HD])
                pe.wait_ge(sem("latsq_ready"), nth(1))
                pe.wait_ge(sem("hoss_used"), nth(1))
                sq = mtm[:].rearrange("p a b -> p (a b)")
                mm(bank[1][:, 0:T], cst("ones"), sq[:, 0:T], True, False)
                mm(bank[1][:, 0:T], cst("ones"), sq[:, T:2 * T], False, True)
                mm(bank[1][:, T:2 * T], cst("ones"), sq[:, 2 * T:3 * T], sig="latss_ready")
                pe.wait_ge(sem("lat_ready"), nth(3, 2))
                pe.wait_ge(sem("mla_w_in"), 32 * (layer + 1))
                for h in range(NH):
                    for k in range(2):
                        mm(bank[2 + h // 2][0:UQ, h % 2 * T:(h % 2 + 1) * T], wuq[:, k, h * UQ:(h + 1) * UQ],
                           proj[:, J_CQ + k], k == 0, k == 1, "mlaq_ready" if k and h % 2 else None)
                mm(bank[1][HD:UQ, 0:T], cst("r96")[HD:UQ, HD:UQ], proj[HD:UQ, J_KR], sig="kr_partner")
                pe.wait_ge(sem("pts_ready"), nth(2 * NH, NH - 1))
                for h in range(NH):
                    mm(bank[6 + h // 2][0:HD, h % 2 * T:(h % 2 + 1) * T], wukv[:, h, 0:HD], proj[:, J_CKV],
                       sig="mlak_ready" if h % 2 else None)
                pe.wait_ge(sem("scores_used"), nth(2 * NH, NH - 1))
                pe.wait_ge(sem("mlaq_copied"), nth(2, 1))
                for half in range(2):
                    mm(bank[4 + half][0:UQ, :], cst("r96")[0:UQ, :], qf[:, 2 * half:2 * half + 2].rearrange("p a t -> p (a t)"),
                       sig="q_partner")
                for tt in range(TT):
                    mm(bank[2][:, tt * G:(tt + 1) * G], proj[:, J_CKV, tt * P:(tt + 1) * P], wukv[:, :, HD:2 * HD],
                       sig="mla_v_ready" if tt else None)
                for h in range(NH):
                    if h == 0:
                        pe.wait_ge(sem("mlakv_copied"), nth(3, 2))
                        pe.wait_ge(sem("kf_ready"), nth(1))
                    attend(1, h, lambda qt, h=h: qf[:, h, qt * P:(qt + 1) * P], lambda a, b, h=h: kf[:, h, a:b], None,
                           ("qf_ready", nth(1)))
                    if h:
                        attend2(1, h - 1, lambda kt, h=h - 1: mtok[:, kt, h * HD:(h + 1) * HD])
                attend2(1, NH - 1, lambda kt: mtok[:, kt, (NH - 1) * HD:NH * HD])
                for name, n in (("ya_ready", 2), ("yd_ready", 2)):
                    pe.wait_ge(sem(name), n * (layer + 1))
                pe.wait_ge(sem("attn_copied"), nth(2, 1))
                for u in range(NU, LU):
                    slot, b = u % SLOTS, 2 + u - NU
                    w_wait(slot, before(2 * layer, slot) + u // SLOTS + 1)
                    for ct in range(2):
                        for k in range(KT):
                            mm(bank[b][:, ct * T:(ct + 1) * T], ring[:, slot, k, ct * P:(ct + 1) * P], yT[:, k],
                               k == 0, k == KT - 1, "unit_used" if ct and k == KT - 1 else None)
                norm(2 * layer + 1)
                if layer == 0:
                    pe_ffn_dense(pe, mm, w_wait)
            pe_moe(pe, mm, turn, w_wait)
            norm(2 * DEPTH)
            for k in range(KT):
                pe.wait_ge(sem("hT_ready"), 2 * DEPTH * KT + k + 1)
                for tt in range(TT):
                    turn(bank[k // 2][:, tt * T + k % 2 * P:tt * T + (k % 2 + 1) * P], hT[:, k, tt * P:(tt + 1) * P],
                         sig="out_turned" if k % 2 and tt else None)

        @block.scalar
        def _(act):
            settle = own(act, "act_chain")

            def f(o, i, func, sig="act_chain", scale=1.0, bias=None, accum=None):
                if bias is None and func != ACT.Copy:
                    bias = cst("zero", o.shape[0])
                kw = {"scale": scale}
                if bias is not None:
                    kw["bias"] = bias
                if accum is not None:
                    kw["accum_out"] = accum
                settle(nc.scalar.activation(o, i, func, **kw), sig)

            def copy(o, i, sig="act_chain"):
                settle(nc.scalar.copy(o, i), sig)

            def flat(a):
                return a.rearrange("p a t -> p (a t)")

            def norm(n):
                if n:
                    act.wait_ge(sem("xT_ready"), n)
                for half in range(2):
                    f(flat(wide[:, 4 * half:4 * half + 4]), flat(xT[:, 4 * half:4 * half + 4]), ACT.Square, "sq_ready")
                act.wait_ge(sem("ss_ready"), n + 1)
                f(rstd[:, 0], bank[7][:, 0:T], ACT.Sqrt, "std_ready", 1.0 / D, cst("eps_rms"))

            act.wait_ge(sem("const_in"), 16)
            for b in range(4):
                act.wait_ge(sem("x_turned"), b + 1)
                copy(flat(xT[:, 2 * b:2 * b + 2]), bank[b][:], "x_copied")
            act.wait_ge(sem("par_turned"), 1)
            copy(par[:, 0:NPAR], bank[4][:, 0:NPAR], "par_copied")
            for i in range(4):
                act.wait_ge(sem("angle_ready"), i + 1)
                f(trig[:, i], trig[:, i], ACT.Sin, "trig_ready")
            act.wait_ge(sem("lbd_ready"), 1)
            f(lbc[:, GT:2 * GT], lbc[:, GT:2 * GT], ACT.Sigmoid, "lb_ready")

            for layer in range(DEPTH):
                def nth(per, i=0):
                    return layer * per + i + 1

                norm(2 * layer)

                def unit(u):
                    at = [J_R, J_K, J_V, J_X, J_HQ, J_HF, J_HI, J_HG, J_DQ, J_DK, J_DV, J_CQ, J_CKV][u]
                    b = bank[u % 2]
                    act.wait_ge(sem("unit_used"), layer * LU + u + 1)
                    if u < NU - 1:
                        copy(flat(proj[:, at:at + 2]), b[:], "unit_copied")
                    else:
                        copy(proj[:, at], b[:, 0:T])
                        copy(proj[HD:UQ, J_KR], b[HD:UQ, T:2 * T], "unit_copied")

                for u in range(6):
                    unit(u)
                act.wait_ge(sem("shifted"), nth(8, 6))
                f(tw[:], sh[0:HD, 6], ACT.Tanh, "tw_ready")
                act.wait_ge(sem("shifted"), nth(8, 7))
                f(sg[:], sh[:, 7], ACT.Sigmoid, "tw_ready")
                unit(6)
                unit(7)
                hflat = hs[:].rearrange("p a b -> p (a b)")
                f(hflat[:, 0:2 * T], flat(proj[:, J_HF:J_HF + 2]), ACT.Sigmoid, "hsig_ready")
                f(hflat[:, 2 * T:4 * T], flat(proj[:, J_HQ:J_HQ + 2]), ACT.Sigmoid, "hsig_ready")
                f(hx[:].rearrange("p a b -> p (a b)"), flat(proj[:, J_HG:J_HG + 2]), ACT.Sigmoid, "hsig_ready")
                for i, name in enumerate(("rwkv_w0", "rwkv_a0")):
                    act.wait_ge(sem("lora_ready"), nth(3, i))
                    for j in range(GT):
                        f(rw[:, (SW, SA)[i], j], bank[2 + i][:, j * T:(j + 1) * T], ACT.Sigmoid, "sig_ready",
                          bias=prm(name, layer, j))
                act.wait_ge(sem("lora_ready"), nth(3, 2))
                copy(flat(rw[:, GG]), bank[4][:], "sig_ready")
                act.wait_ge(sem("kkr_ready"), nth(1))
                f(flat(diff[:]), flat(rw[:, KK]), ACT.Square, "kksq_ready")
                for u in range(8, 11):
                    unit(u)
                act.wait_ge(sem("kkss_ready"), nth(1))
                f(flat(rw[:, BN]), bank[5][:], ACT.Sqrt, "kkstd_ready")
                act.wait_ge(sem("logs_ready"), nth(1))
                f(flat(rw[:, WT]), flat(rw[:, CS]), ACT.Exp, "decay_ready", -DECAY)
                f(flat(rw[:, WI]), flat(rw[:, CS]), ACT.Exp, "decay_ready", DECAY)
                f(flat(rw[:, CP]), flat(rw[:, CP]), ACT.Exp, "decay_ready", -DECAY)
                f(fac[:, 0:GT], fac[:, 0:GT], ACT.Exp, "decay_ready", -DECAY)
                act.wait_ge(sem("hgrn_crossed"), nth(1))
                for half in range(2):
                    copy(hx[:].rearrange("p (j h) b -> p h j b", h=2)[:, half],
                         bank[6 + half][:, 0:2 * P].rearrange("p (j b) -> p j b", b=P), "hx_copied" if half else "act_chain")
                for u in range(11, NU):
                    unit(u)
                act.wait_ge(sem("tok_turned"), nth(2))
                copy(flat(vtok[:]), bank[2][:], "tok_copied")
                act.wait_ge(sem("tok_turned"), nth(2, 1))
                f(btok[:, 0], bank[3][:, 0:G], ACT.Copy, scale=-1.0)
                copy(btok[:, 1], bank[3][:, G:2 * G], "tok_copied")
                for l in range(1, LEVELS):
                    for half in range(2):
                        act.wait_ge(sem("mx_ready"), nth(12, 2 * (l - 1) + half))
                        if l > 1:
                            act.wait_ge(sem("xmx_t_ready"), nth(12, 2 * (l - 2) + half))
                        copy(flat(pin[:, 4 * half:4 * half + 4]), bank[2 + half][:], "pin_ready")
                for c in range(TT):
                    act.wait_ge(sem("r_ready"), nth(2, c))
                    for half in range(2):
                        copy(rsol[:].rearrange("p (j h) v -> p h j v", h=2)[:, half],
                             bank[2 + half][:, 0:2 * HD].rearrange("p (j v) -> p j v", v=HD),
                             "rsol_ready" if half else "act_chain")
                    act.wait_ge(sem("u_ready"), nth(2, c))
                    copy(flat(usol[:, c]), bank[6][:, 0:G], "usol_ready")
                act.wait_ge(sem("y_ready"), nth(1))
                copy(flat(ysb[0:HD]), bank[5][0:HD, :])
                copy(flat(ysb[HD:P]), bank[4][HD:P, :], "ysb_ready")
                act.wait_ge(sem("yc_ready"), nth(1))
                f(flat(mtm[:, 0:4]), flat(ysb[:]), ACT.Square, "ysq_ready")
                act.wait_ge(sem("ho_ready"), nth(1))
                copy(hx[:].rearrange("p a b -> p (a b)"), bank[0][:], "ho_used")
                f(flat(pin[:, 0:4]), hx[:].rearrange("p a b -> p (a b)"), ACT.Square, "hosq_ready")
                act.wait_ge(sem("var_ready"), nth(1))
                f(flat(mtm[:, 4:8]), bank[7][:], ACT.Sqrt, "var_used", 1.0 / HD, cst("eps_ln"))
                act.wait_ge(sem("hoss_ready"), nth(1))
                f(flat(pin[:, 4:8]), bank[1][:], ACT.Sqrt, "hoss_used", 1.0 / HD, cst("eps_rms"))

                def softmax(n):
                    b = n % 2
                    act.wait_ge(sem("max_ready"), nth(2 * NH, n))
                    f(ssb[:, b, 0:P], ssb[:, b, 0:P], ACT.Exp, bias=mx[:, b, 0:1], accum=den[:, b, 0:1])
                    f(ssb[:, b, P:3 * P], ssb[:, b, P:3 * P], ACT.Exp, "exp_ready", bias=mx[:, b, 1:2],
                      accum=den[:, b, 1:2])

                def turned(n):
                    b = n % 2
                    act.wait_ge(sem("pts_turned"), nth(2 * NH, n))
                    if n >= 2:
                        act.wait_ge(sem("attended"), nth(2 * NH, n - 2))
                    copy(pts[:, b], bank[6 + b][:, 0:3 * P], "pts_ready")

                for kind in range(2):
                    if kind:
                        sq = mtm[:].rearrange("p a b -> p (a b)")
                        act.wait_ge(sem("ya_ready"), nth(2, 1))
                        f(sq[:, 0:2 * T], flat(proj[:, J_CQ:J_CQ + 2]), ACT.Square)
                        f(sq[:, 2 * T:3 * T], proj[:, J_CKV], ACT.Square, "latsq_ready")
                        act.wait_ge(sem("latss_ready"), nth(1))
                        f(rstd[:, 0], bank[1][:, 0:T], ACT.Sqrt, "latstd_ready", 1.0 / G, cst("eps_rms"))
                        f(rstd[:, 1], bank[1][:, T:2 * T], ACT.Sqrt, "latstd_ready", 1.0 / P, cst("eps_rms"))
                        for half in range(2):
                            act.wait_ge(sem("mlaq_ready"), nth(2, half))
                            copy(flat(qf[:, 2 * half:2 * half + 2]), bank[2 + half][0:UQ, :], "mlaq_copied")
                        for half in range(2):
                            act.wait_ge(sem("mlak_ready"), nth(2, half))
                            copy(flat(kf[0:HD, 2 * half:2 * half + 2]), bank[6 + half][0:HD, :], "mlakv_copied")
                        act.wait_ge(sem("mla_v_ready"), nth(1))
                        copy(flat(mtok), bank[2][:], "mlakv_copied")
                    for h in range(NH):
                        softmax(kind * NH + h)
                        if h:
                            turned(kind * NH + h - 1)
                    turned(kind * NH + NH - 1)
                    act.wait_ge(sem("attended"), nth(2 * NH, kind * NH + NH - 1))
                    copy(flat(yT[:, 2 + 2 * kind:4 + 2 * kind]), bank[0][:], "attn_copied")
                norm(2 * layer + 1)
                if layer == 0:
                    act_ffn_dense(act)
            act_moe(act, copy, f)
            norm(2 * DEPTH)
            for b in range(4):
                act.wait_ge(sem("out_turned"), b + 1)
                copy(wide[:].rearrange("p (a b) t -> p a (b t)", a=TT)[:, :, b * T:(b + 1) * T],
                     bank[b][:].rearrange("p (a t) -> p a t", a=TT), "out_ready")

        @block.vector
        def _(dve):
            settle = own(dve, "dve_chain")

            def tt_(o, a, b, op, sig="dve_chain"):
                settle(nc.vector.tensor_tensor(o, a, b, op), sig)

            def ts(o, a, s1, s2, op0, op1=ALU.bypass, sig="dve_chain"):
                settle(nc.vector.tensor_scalar(o, a, s1, s2, op0, op1), sig)

            def stt(o, a, s, b, op0, op1, sig="dve_chain"):
                settle(nc.vector.scalar_tensor_tensor(o, a, s, b, op0, op1), sig)

            def recip(o, a, sig="dve_chain"):
                settle(nc.vector.reciprocal(o, a), sig)

            def flat(a):
                return a.rearrange("p a t -> p (a t)")

            def norm(n, name, layer):
                dve.wait_ge(sem("std_ready"), n + 1)
                recip(rstd[:, 1], rstd[:, 0])
                for k in range(KT):
                    stt(hT[:, k], xT[:, k], prm(name, layer, k), rstd[:, 1], ALU.mult, ALU.mult, "hT_ready")

            settle(nc.vector.memset(zeros[:], 0.0), "gated")
            settle(nc.vector.memset(fac[:], 0.0), "gated")
            settle(nc.vector.memset(lbc[:], 0.0))
            dve.wait_ge(sem("const_in"), 16)
            dve.wait_ge(sem("pos_in"), 16)
            ts(diff[:, 0], posi, 1.0, None, ALU.mult)
            for i, (name, quarter) in enumerate((("f64", 0.25), ("f64", 0.0), ("f96", 0.25), ("f96", 0.0))):
                ang, turns = diff[:, 1], rtmp[:, 1]
                ts(ang, diff[:, 0], cst(name), None, ALU.mult)
                ts(turns, ang, float(1 / (2 * np.pi)), quarter, ALU.mult, ALU.add)
                ts(turns, turns, ROUND, ROUND, ALU.add, ALU.subtract)
                for part in TURN:
                    stt(ang, turns, -part, ang, ALU.mult, ALU.add)
                ts(ang, ang, float(np.pi / 2) if quarter else 0.0, float(np.float32(3.1415925)), ALU.add, ALU.min)
                ts(trig[:, i], ang, float(np.float32(-3.1415925)), None, ALU.max, sig="angle_ready")
            dve.wait_ge(sem("par_copied"), 1)
            ka = PCOL["rwkv_k_a"][0]
            ts(omka[:], par[:, ka:ka + DEPTH * GT], -1.0, 1.0, ALU.mult, ALU.add)
            lb = PCOL["hgrn_lb_logits"][0]
            tt_(lbc[:, GT:2 * GT], par[:, lb + GT:lb + 2 * GT], par[:, lb:lb + GT], ALU.subtract, "lbd_ready")
            dve.wait_ge(sem("lb_ready"), 1)
            ts(omlb[:], lbc[:], -1.0, 1.0, ALU.mult, ALU.add, "omlb_ready")

            for layer in range(DEPTH):
                def nth(per, i=0):
                    return layer * per + i + 1

                norm(2 * layer, "mix_norm", layer)
                for u in range(4):
                    dve.wait_ge(sem("unit_copied"), layer * NU + u + 1)
                    a = proj[:, 2 * u:2 * u + 2]
                    tt_(diff[:, :, 1:T], a[:, :, 0:T - 1], a[:, :, 1:T], ALU.subtract)
                    ts(diff[:, :, 0:1], a[:, :, 0:1], -1.0, None, ALU.mult)
                    for j in range(2):
                        stt(sh[:, 2 * u + j], diff[:, j], prm("rwkv_mu", layer, 2 * u + j), a[:, j], ALU.mult, ALU.add,
                            "shifted")
                for j in range(GT):
                    ts(rw[:, KK, j], sh[:, J_K + j], prm("rwkv_k_k", layer, j), None, ALU.mult,
                       sig="kkr_ready" if j else "dve_chain")
                dve.wait_ge(sem("sig_ready"), nth(5, 1))
                for j in range(GT):
                    for c in range(TT):
                        s = slice(c * P, (c + 1) * P)
                        settle(nc.vector.tensor_tensor_scan(rw[:, CS, j, s], cst("ones"), rw[:, SW, j, s], 0.0,
                                                            ALU.mult, ALU.add))
                for j in range(GT):
                    mid = [rw[:, CS, j, c * P + HD - 1:c * P + HD] for c in range(TT)]
                    tt_(fac[:, j:j + 1], rw[:, CS, j, P - 1:P], mid[0], ALU.subtract)
                    tt_(fac[:, j:j + 1], fac[:, j:j + 1], mid[1], ALU.add)
                    for c in range(TT):
                        settle(nc.vector.tensor_copy(fac[:, GT + c:GT + c + 1], mid[c]))
                        s = slice(c * P, (c + 1) * P)
                        ts(rw[:, CS, j, s], rw[:, CS, j, s], fac[:, GT + c:GT + c + 1], None, ALU.subtract)
                tt_(flat(rw[:, CP]), flat(rw[:, CS]), flat(rw[:, SW]), ALU.subtract, "logs_ready")
                dve.wait_ge(sem("kkstd_ready"), nth(1))
                ts(flat(rw[:, BN]), flat(rw[:, BN]), 1e-12, None, ALU.max)
                recip(flat(rw[:, BN]), flat(rw[:, BN]))
                tt_(flat(rw[:, KK]), flat(rw[:, KK]), flat(rw[:, BN]), ALU.mult)
                dve.wait_ge(sem("sig_ready"), nth(5, 3))
                for j in range(GT):
                    c = layer * GT + j
                    ts(rw[:, KM, j], rw[:, SA, j], prm("rwkv_k_a", layer, j), omka[:, c:c + 1], ALU.mult, ALU.add)
                tt_(flat(rw[:, KM]), flat(rw[:, KM]), flat(sh[:, J_K:J_K + 2]), ALU.mult)
                tt_(flat(rw[:, BN]), flat(sh[:, J_R:J_R + 2]), flat(rw[:, KM]), ALU.mult)
                for j in range(GT):
                    ts(diff[:, j], rw[:, BN, j], prm("rwkv_r_k", layer, j), None, ALU.mult,
                       sig="rkk_ready" if j else "dve_chain")
                tt_(flat(rw[:, SA]), flat(rw[:, KK]), flat(rw[:, SA]), ALU.mult)
                dve.wait_ge(sem("decay_ready"), nth(4, 3))
                tt_(flat(kap[:]), flat(rw[:, KK]), flat(rw[:, CP]), ALU.mult)
                tt_(flat(bet[:]), flat(rw[:, SA]), flat(rw[:, WI]), ALU.mult)
                tt_(flat(kha[:]), flat(rw[:, KM]), flat(rw[:, WI]), ALU.mult)
                tt_(flat(rha[:]), flat(sh[:, J_R:J_R + 2]), flat(rw[:, WT]), ALU.mult, "chunks_ready")
                for e in range(LEVELS + 1):
                    for half in range(2):
                        dve.wait_ge(sem("hgrn_scored"), nth(16, 2 * e + half))
                        o = hs[:, 4 * half:4 * half + 4]
                        i = bank[6 + half][:].rearrange("p (a b) -> p a b", b=P)
                        if e == 0:
                            tt_(o, i, over(cst("id"), 4), ALU.mult, "hgrn_masked")
                        else:
                            settle(nc.vector.copy_predicated(o, over(lvl(e - 1), 4).bitcast(I32), i), "hgrn_masked")
                dve.wait_ge(sem("bonus_ready"), nth(1))
                tt_(flat(rw[:, BN]), bank[5][:], flat(sh[:, J_V:J_V + 2]), ALU.mult, "bonus_used")
                for n, (o, mask, sign) in enumerate(((atm, "ups", 1.0), (btm, "ups", 1.0), (ctm, "upi", -1.0),
                                                     (dtm, "upi", 1.0))):
                    dve.wait_ge(sem("chunk_ready"), nth(4, n))
                    b = 4 if n % 2 == 0 else 6
                    for half in range(2):
                        stt(o[:, 4 * half:4 * half + 4], bank[b + half][:].rearrange("p (a b) -> p a b", b=P), sign,
                            over(cst(mask), 4), ALU.mult, ALU.mult, "chunk_masked" if half else "dve_chain")
                    if n == 0:
                        for half in range(2):
                            hv = slice(4 * half, 4 * half + 4)
                            tt_(xit[:, hv], atm[:, hv], over(lvl(0), 4), ALU.mult)
                            stt(xit[:, hv], xit[:, hv], -1.0, over(cst("id"), 4), ALU.mult, ALU.add, "xit_ready")
                for half in range(2):
                    dve.wait_ge(sem("xt_turned"), nth(2, half))
                    settle(nc.vector.tensor_copy(flat(xin[:, 4 * half:4 * half + 4]), bank[2 + half][:]), "xin_ready")
                for l in range(1, LEVELS):
                    for half in range(2):
                        hv = slice(4 * half, 4 * half + 4)
                        if l < LEVELS - 1:
                            dve.wait_ge(sem("xmx_ready"), nth(10, 2 * (l - 1) + half))
                            tt_(flat(xin[:, hv]), flat(xin[:, hv]), bank[4 + half][:], ALU.subtract, "xin_ready")
                        dve.wait_ge(sem("xmx_t_ready"), nth(12, 2 * (l - 1) + half))
                        tt_(flat(xit[:, hv]), flat(xit[:, hv]), bank[6 + half][:], ALU.subtract, "xit_ready")
                dve.wait_ge(sem("state_summed"), nth(1))
                for j in range(GT):
                    ts(st[:, j], bank[4][:, j * HD:(j + 1) * HD], fac[:, j:j + 1], None, ALU.mult,
                       sig="state_ready" if j else "dve_chain")
                dve.wait_ge(sem("mean_ready"), nth(1))
                stt(flat(ysb[:]), bank[6][:], -1.0 / HD, flat(ysb[:]), ALU.mult, ALU.add, "yc_ready")
                dve.wait_ge(sem("var_used"), nth(1))
                recip(flat(mtm[:, 4:8]), flat(mtm[:, 4:8]))
                tt_(flat(ysb[:]), flat(ysb[:]), flat(mtm[:, 4:8]), ALU.mult)
                for j in range(GT):
                    ts(ysb[:, j], ysb[:, j], prm("rwkv_ln_w", layer, j), prm("rwkv_ln_b", layer, j), ALU.mult, ALU.add)
                    tt_(ysb[:, j], ysb[:, j], rw[:, BN, j], ALU.add)
                    tt_(yT[:, j], ysb[:, j], rw[:, GG, j], ALU.mult, "ya_ready")
                dve.wait_ge(sem("hoss_used"), nth(1))
                recip(flat(pin[:, 4:8]), flat(pin[:, 4:8]))
                hxf = hx[:].rearrange("p a b -> p (a b)")
                tt_(hxf, hxf, flat(pin[:, 4:8]), ALU.mult)
                for j in range(GT):
                    stt(yT[:, 6 + j], hxf[:, j * T:(j + 1) * T], prm("hgrn_g_norm", layer, j), proj[:, J_HG + j],
                        ALU.mult, ALU.mult, "yd_ready")
                dve.wait_ge(sem("trig_ready"), 4)
                for i, at in enumerate((J_DQ, J_DK)):
                    dve.wait_ge(sem("partner_ready"), nth(2, i))
                    tt_(rtmp[:], bank[2 + i][:].rearrange("p (a t) -> p a t", t=T), over(trig[:, 1], 2), ALU.mult)
                    tt_(proj[:, at:at + 2], proj[:, at:at + 2], over(trig[:, 0], 2), ALU.mult)
                    tt_(proj[:, at:at + 2], proj[:, at:at + 2], rtmp[:], ALU.add, "rope_ready")

                def scores(n, scale, mask):
                    b = n % 2
                    dve.wait_ge(sem("scores_ready"), nth(2 * NH, n))
                    if n >= 2:
                        dve.wait_ge(sem("pts_turned"), nth(2 * NH, n - 2))
                    stt(ssb[:, b], bank[4 + b][:, 0:3 * P], scale, cst(mask), ALU.mult, ALU.add, "scores_used")
                    settle(nc.vector.tensor_reduce(mx[:, b, 0:1], ssb[:, b, 0:P], AX.X, ALU.max, negate=True))
                    settle(nc.vector.tensor_reduce(mx[:, b, 1:2], ssb[:, b, P:3 * P], AX.X, ALU.max, negate=True), "max_ready")

                def probs(n):
                    b = n % 2
                    dve.wait_ge(sem("exp_ready"), nth(2 * NH, n))
                    recip(den[:, b], den[:, b])
                    ts(ssb[:, b, 0:P], ssb[:, b, 0:P], den[:, b, 0:1], None, ALU.mult)
                    ts(ssb[:, b, P:3 * P], ssb[:, b, P:3 * P], den[:, b, 1:2], None, ALU.mult, sig="probs_ready")

                for kind in range(2):
                    if kind:
                        dve.wait_ge(sem("latstd_ready"), nth(2, 1))
                        recip(flat(rstd[:]), flat(rstd[:]))
                        for k in range(2):
                            stt(proj[:, J_CQ + k], proj[:, J_CQ + k], prm("mla_q_norm", layer, k), rstd[:, 0],
                                ALU.mult, ALU.mult, "lat_ready")
                        stt(proj[:, J_CKV], proj[:, J_CKV], prm("mla_kv_norm", layer, 0), rstd[:, 1],
                            ALU.mult, ALU.mult, "lat_ready")
                        r = slice(HD, UQ)
                        dve.wait_ge(sem("kr_partner"), nth(1))
                        tt_(rtmp[r, 0], bank[1][r, 0:T], trig[r, 3], ALU.mult)
                        tt_(proj[r, J_KR], proj[r, J_KR], trig[r, 2], ALU.mult)
                        tt_(kf[r], over(proj[r, J_KR], NH), over(rtmp[r, 0], NH), ALU.add, "kf_ready")
                        for half in range(2):
                            dve.wait_ge(sem("q_partner"), nth(2, half))
                            hv = slice(2 * half, 2 * half + 2)
                            tt_(rtmp[r], bank[4 + half][r, :].rearrange("p (a t) -> p a t", t=T), over(trig[r, 3], 2), ALU.mult)
                            tt_(qf[r, hv], qf[r, hv], over(trig[r, 2], 2), ALU.mult)
                            tt_(qf[r, hv], qf[r, hv], rtmp[r], ALU.add, "qf_ready" if half else "dve_chain")
                    scale = float(np.float32(HD ** -0.5 if kind == 0 else UQ ** -0.5))
                    for h in range(NH):
                        scores(kind * NH + h, scale, ("dil", "caus")[kind])
                        if h:
                            probs(kind * NH + h - 1)
                    probs(kind * NH + NH - 1)
                for u in range(NO):
                    dve.wait_ge(sem("unit_used"), layer * LU + NU + u + 1)
                    tt_(flat(xT[:, 2 * u:2 * u + 2]), flat(xT[:, 2 * u:2 * u + 2]), bank[2 + u][:], ALU.add,
                        "xT_ready" if u == NO - 1 else "dve_chain")
                norm(2 * layer + 1, "ffn_norm", layer)
                if layer == 0:
                    dve_ffn_dense(dve, tt_)
            dve_moe(dve, settle, tt_, ts, stt, recip)
            norm(2 * DEPTH, "final_norm", 0)


NAMES = ["x", "positions", "mix_norm", "w_in", "w_out", "rwkv_mu", "rwkv_w0", "rwkv_w2", "rwkv_a0", "rwkv_a2", "rwkv_g2",
         "rwkv_k_k", "rwkv_k_a", "rwkv_r_k", "rwkv_ln_w", "rwkv_ln_b", "mla_q_norm", "mla_w_uq", "mla_kv_norm",
         "mla_w_ukv", "hgrn_lb_logits", "hgrn_g_norm", "ffn_norm", "ffn_w1", "ffn_w3", "ffn_w2", "moe_router",
         "moe_w1", "moe_w3", "moe_w2", "final_norm"]


def kernel(**inputs):
    import concourse.bacc as bacc
    from concourse.bass_utils import run_bass_kernel_spmd

    nc = bacc.Bacc("TRN2", target_bir_lowering=False, num_devices=1)
    arrays = {f"in_{n}": np.ascontiguousarray(inputs[n]) for n in NAMES}
    arrays["in_const"] = constants()
    aps = {n[3:]: nc.dram_tensor(n, a.shape, mybir.dt.from_np(a.dtype), kind="ExternalInput").ap()
           for n, a in arrays.items()}
    out = nc.dram_tensor("out", (1, T, D), F32, kind="ExternalOutput").ap()
    program(nc, aps, out)
    r = run_bass_kernel_spmd(nc, [arrays], core_ids=[0])
    return r.results[0]["out"]
```

```python
from contextlib import ExitStack

import numpy as np

import concourse.bass as bass
from concourse import mybir

F32 = mybir.dt.float32
F32R = mybir.dt.float32r
I32 = mybir.dt.int32
U32 = mybir.dt.uint32
BF16 = mybir.dt.bfloat16
ALU = mybir.AluOpType
ACT = mybir.ActivationFunctionType
AX = mybir.AxisListType

P = 128
D = 1024
T = 256
DEPTH = 2
KT = D // P
TT = T // P
G = D // 4
GT = G // P
HD = 64
NH = G // HD
NM = NH * TT
N_IN = 3232
UQ = 96
FF = 2816
FE = 3584
NE = 8
C = P
MAXJOBS = 16
RWKV_EPS = 64e-5
RMS_EPS = 1e-6
DECAY = float(np.exp(np.float32(-0.5)))
NEG = -1e30
ROUND = 1.5 * 2.0 ** 23
TURN = (6.28125, 0.0019340515136718750, 1.2556659146e-06)
LEVELS = 7

UNITS = [(0, 256, False), (256, 256, False), (512, 256, False), (768, 256, False),
         (2208, 256, False), (2464, 256, False), (2720, 256, True), (2976, 256, False),
         (1024, 256, False), (1280, 256, False), (1536, 256, True),
         (1792, 256, False), (2048, 160, False)]
NU = len(UNITS)
J_R, J_K, J_V, J_X, J_HQ, J_HF, J_HI, J_HG, J_DQ, J_DK, J_DV, J_CQ, J_CKV, J_KR = \
    0, 2, 4, 6, 8, 10, 12, 14, 16, 18, 20, 22, 24, 25
NO = 4
LU = NU + NO
SLOTS = 6

PARAMS = [("mix_norm", 8), ("rwkv_mu", 8), ("rwkv_w0", 2), ("rwkv_a0", 2), ("rwkv_k_k", 2), ("rwkv_k_a", 2),
          ("rwkv_r_k", 2), ("rwkv_ln_w", 2), ("rwkv_ln_b", 2), ("mla_q_norm", 2), ("mla_kv_norm", 1),
          ("hgrn_g_norm", 2), ("hgrn_lb_logits", 2), ("ffn_norm", 8)]
PCOL, _at = {}, 0
for _name, _n in PARAMS:
    PCOL[_name] = (_at, _n)
    _at += DEPTH * _n
PCOL["final_norm"] = (_at, KT)
NPAR = _at + KT

CCOL, _at = {}, 0
for _name, _n in [("id", P), ("ones", P), ("blk", P), ("r64", P), ("r96", UQ), ("upi", P), ("ups", P),
                  ("lv", LEVELS * P), ("dil", 3 * P), ("caus", 3 * P), ("iota", P), ("f64", 1), ("f96", 1),
                  ("eps_rms", 1), ("eps_ln", 1), ("zero", 1)]:
    CCOL[_name] = (_at, _n)
    _at += _n
NCONST = _at


def constants():
    c = np.zeros((P, NCONST), np.float32)

    def put(name, a):
        at, n = CCOL[name]
        a = np.asarray(a, np.float32)
        c[:a.shape[0], at:at + n] = a.reshape(a.shape[0], n)

    i = np.arange(P)
    put("id", np.eye(P))
    put("ones", np.ones((P, P)))
    put("blk", (i[:, None] // HD == i[None, :] // HD))

    def rotate(lo, n, width):
        r = np.zeros((width, width))
        for b in range(lo, width, n):
            for q in range(n // 2):
                r[b + n // 2 + q, b + q] = -1.0
                r[b + q, b + n // 2 + q] = 1.0
        return r

    put("r64", rotate(0, HD, P))
    put("r96", rotate(HD, UQ - HD, UQ))
    put("upi", i[:, None] <= i[None, :])
    put("ups", i[:, None] < i[None, :])
    lv = np.zeros((P, LEVELS, P))
    for l in range(LEVELS):
        half = 1 << l
        same = i[:, None] // (2 * half) == i[None, :] // (2 * half)
        lv[:, l] = same & ((i[:, None] // half) % 2 == 0) & ((i[None, :] // half) % 2 == 1)
    put("lv", lv)
    q, k = np.arange(T)[:, None], np.arange(T)[None, :]
    d = q - k
    count = ((d >= 0) & (d <= 128)) + 0.0
    count += (d >= 0) & (d % 4 == 0) & (d // 4 <= 128)
    count += (d >= 0) & (d % 16 == 0) & (d // 16 <= 128)
    dil = np.where(count > 0, np.log(np.maximum(count, 1.0)), NEG)
    caus = np.where(d >= 0, 0.0, NEG)
    for name, m in (("dil", dil), ("caus", caus)):
        put(name, np.concatenate([m[:P, :P], m[P:, :]], axis=1))
    put("iota", np.broadcast_to(i, (P, P)))
    f64 = 1.0 / (np.float32(10000.0) ** (np.arange(0, HD, 2, dtype=np.float32) / np.float32(HD)))
    f32_ = 1.0 / (np.float32(10000.0) ** (np.arange(0, 32, 2, dtype=np.float32) / np.float32(32)))
    put("f64", f64[i % 32][:, None])
    put("f96", np.where((i >= HD) & (i < UQ), f32_[(i - HD) % 16], 0.0)[:, None])
    put("eps_rms", np.full((P, 1), RMS_EPS))
    put("eps_ln", np.full((P, 1), RWKV_EPS))
    put("zero", np.zeros((P, 1)))
    return c


def program(nc, A, out):
    ctx = ExitStack()
    with ctx:
        mixer = ExitStack()

        def sb(name, shape, dt=F32, where=ctx):
            return where.enter_context(nc.sbuf_tensor(name, shape, dt))

        def mx_sb(name, shape):
            return sb(name, shape, where=mixer)

        sems = {}

        def sem(name):
            if name not in sems:
                sems[name] = ctx.enter_context(nc.semaphore(name))
            return sems[name]

        ring = sb("ring", [P, SLOTS, KT, T])
        const = sb("const", [P, NCONST])
        prow = sb("prow", [P, P])
        par = sb("par", [P, P])
        omka = sb("omka", [P, DEPTH * GT])
        lbc = sb("lbc", [P, DEPTH * GT])
        omlb = sb("omlb", [P, DEPTH * GT])
        lora = sb("lora", [P, DEPTH, G])
        g2 = sb("g2", [P, DEPTH, G])
        wuq = sb("wuq", [P, 2, NH * UQ])
        wukv = sb("wukv", [P, NH, 2 * HD])
        router = sb("router", [P, KT, NE])
        trig = sb("trig", [P, 4, T])
        xT = sb("xT", [P, KT, T])
        hT = sb("hT", [P, KT, T])
        zeros = sb("zeros", [1, 640], BF16)
        wide = sb("wide", [P, KT, T])
        rstd = sb("rstd", [P, 2, T])
        proj = mx_sb("proj", [P, 26, T])
        diff = mx_sb("diff", [P, GT, T])
        tw = mx_sb("tw", [HD, T])
        sg = mx_sb("sg", [P, T])
        rw = mx_sb("rw", [P, 10, GT, T])
        kap, bet, kha, rha = (mx_sb(n, [P, GT, T]) for n in ("kap", "bet", "kha", "rha"))
        mtm = mx_sb("mtm", [P, NM, P])
        pin = mx_sb("pin", [P, NM, P])
        vtok = mx_sb("vtok", [P, TT, G])
        btok = mx_sb("btok", [P, 2, G])
        rsol = mx_sb("rsol", [P, NH, HD])
        usol = mx_sb("usol", [P, TT, NH, HD])
        st = mx_sb("st", [P, GT, HD])
        fac = mx_sb("fac", [P, 2 * GT])
        hq = mx_sb("hq", [P, 2, GT * T])
        hk = mx_sb("hk", [P, 2, GT * T])
        hend = mx_sb("hend", [P, GT * T])
        hs = mx_sb("hs", [P, NM, P])
        hx = mx_sb("hx", [P, NH, P])
        ssb = mx_sb("ssb", [P, 2, 3 * P])
        pts = mx_sb("pts", [P, 2, 3 * P])
        rtmp = mx_sb("rtmp", [P, 2, T])
        mx = mx_sb("mx", [P, 2, 2])
        den = mx_sb("den", [P, 2, 2])
        sh = wide
        yT = hT
        SW, SA, CS, CP, KK, KM, WT, WI, GG, BN = range(10)

        def pair(buf, at):
            return buf[:, at:at + 2].rearrange("p s a (b c) -> p (s a b) c", c=P)

        atm, btm, ctm, dtm = (pair(rw, 2 * i) for i in range(4))
        xin = proj[:, 0:4].rearrange("p a (b c) -> p (a b) c", c=P)
        xit = proj[:, 4:8].rearrange("p a (b c) -> p (a b) c", c=P)
        mtok = proj[:, J_HF:J_HF + 2]
        qf = hq[0:UQ].rearrange("p a (h t) -> p (a h) t", t=T)
        kf = hk[0:UQ].rearrange("p a (h t) -> p (a h) t", t=T)
        ysb = diff
        posi = rtmp[:, 0].bitcast(I32)
        mixer.close()
        wh = sb("wh", [P, 3, 8 * T], F32R)
        wl = sb("wl", [P, 3, 8 * T], F32R)
        xh = sb("xh", [P, KT, T], F32R)
        xl = sb("xl", [P, KT, T], F32R)
        gh = sb("gh", [P, 2, T], F32R)
        gl = sb("gl", [P, 2, T], F32R)
        silu = sb("silu", [P, 2, T])
        gate = sb("gate", [P, 2, T])
        yj = sb("yj", [P, D])
        sel = sb("sel", [P, TT, C])
        selg = sb("selg", [P, TT, C])
        selt = sb("selt", [P, TT, C])
        hit = sb("hit", [P, 2, TT, C])
        pgt = sb("pgt", [P, T])
        rt = sb("rt", [P, T])
        jt = sb("jt", [P, 2 * MAXJOBS], I32)
        idx = sb("idx", [P, 16], U32)

        bank = [ctx.enter_context(nc.psum_tensor(f"bank{i}", [P, 512], F32)) for i in range(8)]

        def cst(name, rows=P):
            at, n = CCOL[name]
            return const[0:rows, at:at + n]

        def lvl(l):
            at = CCOL["lv"][0] + l * P
            return const[:, at:at + P]

        def prm(name, layer, j, lo=0, hi=P):
            at, n = PCOL[name]
            return par[lo:hi, at + layer * n + j:at + layer * n + j + 1]

        def over(ap, n):
            return ap.unsqueeze(1).broadcast_to([ap.shape[0], n, ap.shape[1]])

        block = ctx.enter_context(nc.Block())

        CH_D, CH_E = FF // P, FE // P
        PAIRS_D, PAIRS_E = CH_D // 2, CH_E // 2

        def last_unit(s):
            return max(u for u in range(LU) if u % SLOTS == s)


        def own(eng, chain):
            count = {}

            def settle(ins, sig=chain):
                ins.then_inc(sem(sig), 1)
                count[sig] = count.get(sig, 0) + 1
                eng.wait_ge(sem(sig), count[sig])
            return settle

        def wait(eng, name, n):
            if not isinstance(n, int) or n > 0:
                eng.wait_ge(sem(name), n)

        unit_loads = [len([u for u in range(LU) if u % SLOTS == s]) for s in range(SLOTS)]
        dense_loads = [(PAIRS_D + (1 if s < 3 else 0)) // 2 for s in range(SLOTS)]

        def before(phase, s):
            return [0, unit_loads[s], unit_loads[s] + dense_loads[s], 2 * unit_loads[s] + dense_loads[s]][phase]

        class Run:
            def __init__(self, pairs, moe, stages, items, before_pairs, loads):
                self.pairs, self.moe = pairs, moe
                self.stages, self.items, self.before_pairs = stages, items, before_pairs
                self.loads = loads
                self.parts = 1 if moe else 2

            def up(self, m, part):
                if isinstance(m, int) and m == 0:
                    return self.stages + part, part
                return self.stages + 3 * m - 1 + part, (2, 0)[part]

            def down(self, m, last=False):
                if last:
                    return self.stages + 3 * self.pairs - 1, 2
                return self.stages + 3 * m + 4, 1

            def load(self, slot, half_m):
                return 16 * (self.loads(slot) + half_m + 1)

            def item(self, m):
                return self.items + self.parts * m

            def last_split(self, slot):
                m = max(q for q in range(self.pairs) if q % 2 == slot // 3)
                return 1 + (self.down(m, m == self.pairs - 1)[0] if slot % 3 == 2 else self.up(m, 1)[0])

        dense = Run(PAIRS_D, False, 0, 0, 0, lambda s: before(1, s))

        def job(j):
            return Run(PAIRS_E, True, 3 * PAIRS_D + 3 * PAIRS_E * j, 2 * PAIRS_D + PAIRS_E * j,
                       PAIRS_D + PAIRS_E * j, lambda s: before(3, s) + PAIRS_E // 2 * j)

        TURNS = 4

        def up_bank(run, par, item):
            return bank[par if run.moe else 6 * par + item]

        def pe_up(pe, run, m, par, part, before_last=None):
            stage, buf = run.up(m, part)
            pe.wait_ge(sem("w_split"), stage + 1)
            if part == 0:
                wait(pe, "gated", run.item(m - 1))
            w = [b[:, buf].rearrange("p (k n) -> p k n", n=2 * T) for b in (wh, wl)]
            for item in range(run.parts):
                for kind in range(1 if run.moe else 2):
                    for k in range(4):
                        for n, (a, b) in enumerate(((0, 0), (0, 1), (1, 0))):
                            x = (xh, xl)[a][:, 4 * part + k]
                            kw = {"start": part == kind == k == n == 0, "stop": part == 1 and k == 3 and n == 2,
                                  "skip_group_check": True}
                            if before_last and k == 3 and n == 2:
                                pe.wait_ge(sem(before_last[0]), before_last[1])
                            if run.moe:
                                ins = nc.tensor.matmul(up_bank(run, par, 0)[:], x[:, 0:C], w[b][:, k], **kw)
                            else:
                                at = kind * T + item * P
                                ins = nc.tensor.matmul(up_bank(run, par, item)[:, kind * T:(kind + 1) * T],
                                                       w[b][:, k, at:at + P], x, **kw)
            ins.then_inc(sem("stage_used"), 1)

        def pe_turn_gated(pe, run, m):
            if run.moe:
                pe.wait_ge(sem("gated"), run.item(m) + 1)
                pe.wait_ge(sem("g_split"), run.before_pairs + m)
                for a in range(2):
                    ins = nc.tensor.transpose(bank[TURNS][:, a * P:(a + 1) * P], gate[:, 0, a * P:(a + 1) * P], cst("id"))
                ins.then_inc(sem("g_turned"), 1)

        def pe_down(pe, run, m, last=False):
            stage, buf = run.down(m, last)
            pe.wait_ge(sem("w_split"), stage + 1)
            pe.wait_ge(sem("g_split"), run.before_pairs + m + 1)
            w = [b[:, buf].rearrange("p (a n) -> p a n", a=2) for b in (wh, wl)]
            for o in range(2 if run.moe else KT):
                for a in range(2):
                    for g, b in ((gh, 0), (gh, 1), (gl, 0)):
                        if run.moe:
                            ins = nc.tensor.matmul(bank[2 + o][:], g[:, a, 0:C], w[b][:, a, o * 512:(o + 1) * 512],
                                                   start=False, stop=False, skip_group_check=True)
                        else:
                            ins = nc.tensor.matmul(bank[2 + o // 2][:, o % 2 * T:(o % 2 + 1) * T],
                                                   w[b][:, a, o * P:(o + 1) * P], g[:, a],
                                                   start=False, stop=False, skip_group_check=True)
            ins.then_inc(sem("stage_used"), 1)

        def pe_steps(pe, run):
            def step(m, par):
                pe_up(pe, run, m, par, 0)
                pe_turn_gated(pe, run, m - 1)
                pe_up(pe, run, m, par, 1)
                pe_down(pe, run, m - 1)

            n = run.pairs - 1
            with pe.Fori(0, n // 2) as i:
                step(2 * i + 1, 1)
                step(2 * i + 2, 0)
            if n % 2:
                step(n, 1)

        def zero_acc(banks_):
            for b in banks_:
                nc.tensor.matmul(bank[b][:], zeros[:, 0:P], zeros[:, P:P + 512], start=True, stop=True)

        def split_high(act, stage, buf, src, split):
            wait(act, "stage_used", stage - 2)
            for slot, n in src[1]:
                act.wait_ge(sem(f"w_ready{slot}"), n)
            o = split(wh[:, buf])
            nc.scalar.activation(o, src[0], ACT.Copy).then_inc(sem("w_high"), 1)

        def split_low(dve, stage, buf, src, split):
            dve.wait_ge(sem("w_high"), stage + 1)
            nc.vector.tensor_tensor(split(wl[:, buf]), src[0], split(wh[:, buf]).bitcast(F32), ALU.subtract
                                    ).then_inc(sem("w_split"), 1)

        def splitter(eng, fn, run):
            def up(m, half_m, par, part):
                s0 = 3 * par
                src = ring[:, s0:s0 + 2, 4 * part:4 * part + 4]
                fn(eng, *run.up(m, part), (src, [(s0 + i, run.load(s0 + i, half_m)) for i in range(2)]),
                   lambda w: w.rearrange("p (k a n) -> p a k n", a=2, n=T))

            def down(m, half_m, par, last=False):
                s = 3 * par + 2
                fn(eng, *run.down(m, last), (ring[:, s].rearrange("p a t -> p (a t)"), [(s, run.load(s, half_m))]),
                   lambda w: w)
            return up, down

        def act_split(act, run):
            return splitter(act, split_high, run)

        def act_silu(act, run, m, par):
            for item in range(run.parts):
                act.wait_ge(sem("stage_used"), run.up(m, 1)[0] + 1)
                wait(act, "gated", run.item(m - 1) + item + 1)
                nc.scalar.activation(silu[:, item], up_bank(run, par, item)[:, 0:T], ACT.Silu, bias=cst("zero")
                                     ).then_inc(sem("silu_done"), 1)

        def act_gated_high(act, run, m):
            if run.moe:
                act.wait_ge(sem("g_turned"), run.before_pairs - PAIRS_D + m + 1)
                o, i = gh[:, :, 0:C], bank[TURNS][:, 0:2 * C].rearrange("p (a c) -> p a c", c=C)
            else:
                act.wait_ge(sem("gated"), run.item(m) + 2)
                o, i = gh[:], gate[:]
            prev = run.stages if isinstance(m, int) and m == 0 else run.down(m - 1)[0] + 1
            wait(act, "stage_used", prev)
            nc.scalar.activation(o, i, ACT.Copy).then_inc(sem("g_high"), 1)

        def act_first_splits(act, run):
            up, down = act_split(act, run)
            up(0, 0, 0, 0)
            up(0, 0, 0, 1)
            up(1, 0, 1, 0)

        def act_start(act, run):
            up, down = act_split(act, run)
            up(1, 0, 1, 1)
            act_silu(act, run, 0, 0)
            down(0, 0, 0)

        def steps(eng, run, body):
            n = run.pairs - 2
            with eng.Fori(0, n // 2) as i:
                body(2 * i + 1, i, i + 1, 1)
                body(2 * i + 2, i + 1, i + 1, 0)
            if n % 2:
                body(n, n // 2, n // 2 + 1, 1)

        def act_steps(act, run):
            up, down = act_split(act, run)

            def step(m, half_m, half_next, par):
                act_gated_high(act, run, m - 1)
                up(m + 1, half_next, 1 - par, 0)
                act_silu(act, run, m, par)
                up(m + 1, half_next, 1 - par, 1)
                down(m, half_m, par)

            steps(act, run, step)

        def act_end_a(act, run):
            m, par = run.pairs - 1, (run.pairs - 1) % 2
            act_gated_high(act, run, m - 1)
            act_split(act, run)[1](m, m // 2, par, True)
            act_silu(act, run, m, par)

        def dve_gate(dve, run, m, par):
            for item in range(run.parts):
                dve.wait_ge(sem("silu_done"), run.item(m) + item + 1)
                wait(dve, "g_split", run.before_pairs + m)
                nc.vector.tensor_tensor(gate[:, item], up_bank(run, par, item)[:, T:2 * T], silu[:, item], ALU.mult
                                        ).then_inc(sem("gated"), 1)

        def dve_gated_low(dve, run, m):
            dve.wait_ge(sem("g_high"), run.before_pairs + m + 1)
            if run.moe:
                o, i, h = gl[:, :, 0:C], bank[TURNS][:, 0:2 * C].rearrange("p (a c) -> p a c", c=C), gh[:, :, 0:C]
            else:
                o, i, h = gl[:], gate[:], gh[:]
            nc.vector.tensor_tensor(o, i, h.bitcast(F32), ALU.subtract).then_inc(sem("g_split"), 1)

        def dve_first_splits(dve, run):
            up, down = splitter(dve, split_low, run)
            up(0, 0, 0, 0)
            up(0, 0, 0, 1)
            up(1, 0, 1, 0)

        def dve_start(dve, run):
            up, down = splitter(dve, split_low, run)
            up(1, 0, 1, 1)
            dve_gate(dve, run, 0, 0)
            down(0, 0, 0)

        def dve_steps(dve, run):
            up, down = splitter(dve, split_low, run)

            def step(m, half_m, half_next, par):
                dve_gated_low(dve, run, m - 1)
                up(m + 1, half_next, 1 - par, 0)
                dve_gate(dve, run, m, par)
                up(m + 1, half_next, 1 - par, 1)
                down(m, half_m, par)

            steps(dve, run, step)

        def dve_end_a(dve, run):
            m, par = run.pairs - 1, (run.pairs - 1) % 2
            dve_gated_low(dve, run, m - 1)
            splitter(dve, split_low, run)[1](m, m // 2, par, True)
            dve_gate(dve, run, m, par)

        def pe_ffn_dense(pe):
            zero_acc((2, 3, 4, 5))
            pe.wait_ge(sem("x_split"), 2)
            pe_up(pe, dense, 0, 0, 0)
            pe_up(pe, dense, 0, 0, 1)
            pe_steps(pe, dense)
            pe_down(pe, dense, PAIRS_D - 1, True)

        def act_ffn_dense(act):
            for half in range(2):
                hv = slice(4 * half, 4 * half + 4)
                act.wait_ge(sem("hT_ready"), KT + 4 * half + 4)
                nc.scalar.activation(xh[:, hv], hT[:, hv], ACT.Copy).then_inc(sem("x_high"), 1)
            act_start(act, dense)
            act_steps(act, dense)
            act_end_a(act, dense)
            act_gated_high(act, dense, PAIRS_D - 1)

        def dve_ffn_dense(dve, tt_):
            for half in range(2):
                hv = slice(4 * half, 4 * half + 4)
                dve.wait_ge(sem("x_high"), half + 1)
                nc.vector.tensor_tensor(xl[:, hv], hT[:, hv], xh[:, hv].bitcast(F32), ALU.subtract
                                        ).then_inc(sem("x_split"), 1)
            dve_start(dve, dense)
            dve_steps(dve, dense)
            dve_end_a(dve, dense)
            dve_gated_low(dve, dense, PAIRS_D - 1)
            dve.wait_ge(sem("stage_used"), 3 * PAIRS_D)
            for u in range(NO):
                x = xT[:, 2 * u:2 * u + 2].rearrange("p a t -> p (a t)")
                tt_(x, x, bank[2 + u][:], ALU.add, "xT_ready" if u == NO - 1 else "dve_chain")

        rtc = {}
        _c = 0
        for _n, _w in (("logit", 16), ("top", 16), ("idx", 16), ("oh1", 16), ("oh2", 16), ("sel", 16), ("e", 2),
                       ("gate", 4), ("slot", 4), ("pos", 16), ("cnt", 8), ("blk", 8), ("cum", 8), ("start", 8),
                       ("tmp", 16), ("job", MAXJOBS + 2)):
            rtc[_n] = (_c, _w)
            _c += _w
        assert _c <= T

        def R(name, i=0, n=None):
            at, w = rtc[name]
            return rt[:, at + i:at + (w if n is None else i + n)]

        def jobs_of(eng):
            eng.wait_ge(sem("jobs_ready"), 1)
            return eng.value_load(jt[0:1, MAXJOBS:MAXJOBS + 1], min_val=1, max_val=MAXJOBS - 1)

        def last_job(eng):
            return eng.value_load(jt[0:1, MAXJOBS + 1:MAXJOBS + 2], min_val=0, max_val=MAXJOBS - 2)

        def hrows():
            return wide[:].rearrange("p (a b) t -> p a (b t)", a=TT)

        def pe_moe(pe, mm, turn):
            pe.wait_ge(sem("hT_ready"), 4 * KT)
            pe.wait_ge(sem("router_in"), 16)
            for tt in range(TT):
                for k in range(KT):
                    mm(bank[7][:, tt * NE:(tt + 1) * NE], hT[:, k, tt * P:(tt + 1) * P], router[:, k], k == 0, k == KT - 1,
                       "logits_ready" if tt and k == KT - 1 else None)
            for b in range(4):
                for k in range(2):
                    for tt in range(TT):
                        turn(bank[b][:, tt * T + k * P:tt * T + (k + 1) * P], hT[:, 2 * b + k, tt * P:(tt + 1) * P],
                             sig="h_turned" if k and tt else None)
            pe.wait_ge(sem("sel_ready"), 1)
            mm(bank[6][:, 0:NE], cst("ups"), R("sel", 0, NE))
            mm(bank[6][:, NE:2 * NE], cst("ups"), R("sel", NE, NE), True, False)
            mm(bank[6][:, NE:2 * NE], cst("ones"), R("sel", 0, NE), False, True)
            mm(bank[6][:, 2 * NE:3 * NE], cst("ones"), R("sel", 0, NE), True, False)
            mm(bank[6][:, 2 * NE:3 * NE], cst("ones"), R("sel", NE, NE), False, True, "pos_ready")
            pe.wait_ge(sem("h_copied"), 4)

            def gather(j):
                pe.wait_ge(sem("sel_built"), j + 1)
                for half in range(2):
                    for d in range(4):
                        for tt in range(TT):
                            k = 4 * half + d
                            mm(bank[5 + half][:, d * C:(d + 1) * C], hrows()[:, tt, k * P:(k + 1) * P], sel[:, tt],
                               tt == 0, tt == 1, "gathered" if d == 3 and tt else None)

            def turn_gates(j):
                pe.wait_ge(sem("selg_built"), j + 1)
                for tt in range(TT):
                    turn(bank[7][:, tt * P:(tt + 1) * P], selg[:, tt], sig="gates_turned" if tt else None)

            def scatter(j):
                pe.wait_ge(sem("gates_copied"), j + 1)
                pe.wait_ge(sem("acc_copied"), 2 * j + 2)
                for b in range(4):
                    for k in range(2):
                        dt = 2 * b + k
                        mm(bank[4 + b][:, k * T:(k + 1) * T], yj[:, dt * P:(dt + 1) * P], pgt[:],
                           sig="scattered" if k else None)

            last = PAIRS_E - 1
            gather(0)
            zero_acc((2, 3))
            run = job(0)
            pe.wait_ge(sem("x_split"), 4)
            pe_up(pe, run, 0, 0, 0)
            pe_up(pe, run, 0, 0, 1)
            pe_steps(pe, run)
            n_jobs = jobs_of(pe)
            with pe.Fori(1, n_jobs) as j:
                run, nxt = job(j - 1), job(j)
                pe_turn_gated(pe, run, last)
                gather(j)
                turn_gates(j - 1)
                pe_down(pe, run, last, True)
                pe.wait_ge(sem("x_split"), 2 * j + 4)
                pe_up(pe, nxt, 0, 0, 0)
                scatter(j - 1)
                zero_acc((2, 3))
                pe_up(pe, nxt, 0, 0, 1, ("scatter_added", 4 * j))
                pe_steps(pe, nxt)
            j = last_job(pe)
            run = job(j)
            pe_turn_gated(pe, run, last)
            turn_gates(j)
            pe_down(pe, run, last, True)
            scatter(j)

        def act_moe(act, copy, f):
            for b in range(4):
                act.wait_ge(sem("h_turned"), b + 1)
                copy(hrows()[:, :, b * T:(b + 1) * T], bank[b][:].rearrange("p (a t) -> p a t", a=TT), "h_copied")
            act.wait_ge(sem("gate_logit"), 1)
            f(R("e"), R("e"), ACT.Exp, "gate_exp")

            def gathered(j):
                for half in range(2):
                    act.wait_ge(sem("gathered"), 2 * j + half + 1)
                    nc.scalar.activation(xh[:, 4 * half:4 * half + 4, 0:C],
                                         bank[5 + half][:].rearrange("p (k c) -> p k c", c=C), ACT.Copy
                                         ).then_inc(sem("x_high"), 1)

            def gates(j):
                act.wait_ge(sem("gates_turned"), j + 1)
                nc.scalar.copy(pgt[:], bank[7][:, 0:T]).then_inc(sem("gates_copied"), 1)

            def acc(j):
                act.wait_ge(sem("stage_used"), job(j).down(0, True)[0] + 1)
                for half in range(2):
                    nc.scalar.copy(yj[:, half * 512:(half + 1) * 512], bank[2 + half][:]).then_inc(sem("acc_copied"), 1)

            last = PAIRS_E - 1
            gathered(0)
            act_start(act, job(0))
            act_steps(act, job(0))
            n_jobs = jobs_of(act)
            with act.Fori(1, n_jobs) as j:
                run, nxt = job(j - 1), job(j)
                up, down = act_split(act, nxt)
                act_end_a(act, run)
                up(0, 0, 0, 0)
                act_gated_high(act, run, last)
                up(0, 0, 0, 1)
                gathered(j)
                gates(j - 1)
                acc(j - 1)
                up(1, 0, 1, 0)
                act_start(act, nxt)
                act_steps(act, nxt)
            j = last_job(act)
            run = job(j)
            act_end_a(act, run)
            act_gated_high(act, run, last)
            gates(j)
            acc(j)

        def dve_moe(dve, settle, tt_, ts, stt, recip):
            iota8 = cst("iota")[:, 0:NE]
            dve.wait_ge(sem("logits_ready"), 1)
            settle(nc.vector.tensor_copy(R("logit"), bank[7][:, 0:TT * NE]))
            for tt in range(TT):
                settle(nc.vector.max(R("top", tt * 8, 8), R("logit", tt * NE, NE)))
                settle(nc.vector.max_index(idx[:, tt * 8:(tt + 1) * 8], R("top", tt * 8, 8), R("logit", tt * NE, NE)))
            settle(nc.vector.tensor_copy(R("idx"), idx[:]))
            for tt in range(TT):
                ts(R("oh1", tt * NE, NE), iota8, R("idx", tt * 8, 1), None, ALU.is_equal)
                ts(R("oh2", tt * NE, NE), iota8, R("idx", tt * 8 + 1, 1), None, ALU.is_equal)
                tt_(R("e", tt, 1), R("top", tt * 8 + 1, 1), R("top", tt * 8, 1), ALU.subtract,
                    "gate_logit" if tt else "dve_chain")
            tt_(R("sel"), R("oh1"), R("oh2"), ALU.add, "sel_ready")
            dve.wait_ge(sem("gate_exp"), 1)
            for tt in range(TT):
                ts(R("gate", 2 * tt, 1), R("e", tt, 1), 1.0, None, ALU.add)
                recip(R("gate", 2 * tt, 1), R("gate", 2 * tt, 1))
                tt_(R("gate", 2 * tt + 1, 1), R("gate", 2 * tt, 1), R("e", tt, 1), ALU.mult)
            dve.wait_ge(sem("pos_ready"), 1)
            settle(nc.vector.tensor_copy(R("pos"), bank[6][:, 0:2 * NE]))
            settle(nc.vector.tensor_copy(R("cnt"), bank[6][:, 2 * NE:3 * NE]))
            ts(R("blk", 0, 1), R("cnt", 0, 1), -1.0, None, ALU.is_gt)
            ts(R("blk", 1, NE - 1), R("cnt", 1, NE - 1), 0.0, None, ALU.is_gt)
            for b in range(1, -(-T // C)):
                stt(R("blk"), R("cnt"), float(b * C), R("blk"), ALU.is_gt, ALU.add)
            settle(nc.vector.tensor_tensor_scan(R("cum"), cst("ones")[:, 0:NE], R("blk"), 0.0, ALU.mult, ALU.add))
            tt_(R("start"), R("cum"), R("blk"), ALU.subtract)
            ts(R("start"), R("start"), float(C), None, ALU.mult)
            for tt in range(TT):
                tt_(R("pos", tt * NE, NE), R("pos", tt * NE, NE), R("start"), ALU.add)
                for i, oh in enumerate(("oh1", "oh2")):
                    tt_(R("tmp", 0, NE), R(oh, tt * NE, NE), R("pos", tt * NE, NE), ALU.mult)
                    settle(nc.vector.tensor_reduce(R("slot", 2 * tt + i, 1), R("tmp", 0, NE), AX.X, ALU.add))
            iota16 = cst("iota")[:, 0:MAXJOBS]
            ts(R("job", 0, MAXJOBS), iota16, R("cum", 0, 1), None, ALU.is_ge)
            for e in range(1, NE):
                stt(R("job", 0, MAXJOBS), iota16, R("cum", e, 1), R("job", 0, MAXJOBS), ALU.is_ge, ALU.add)
            settle(nc.vector.tensor_copy(R("job", MAXJOBS, 1), R("cum", NE - 1, 1)))
            ts(R("job", MAXJOBS + 1, 1), R("cum", NE - 1, 1), -1.0, None, ALU.add)
            settle(nc.vector.tensor_copy(jt[:, 0:MAXJOBS + 2], R("job")), "jobs_ready")
            def gathered(j):
                for half in range(2):
                    dve.wait_ge(sem("x_high"), 2 * j + half + 3)
                    hv = slice(4 * half, 4 * half + 4)
                    nc.vector.tensor_tensor(xl[:, hv, 0:C], bank[5 + half][:].rearrange("p (k c) -> p k c", c=C),
                                            xh[:, hv, 0:C].bitcast(F32), ALU.subtract).then_inc(sem("x_split"), 1)

            def scattered(j):
                for b in range(4):
                    dve.wait_ge(sem("scattered"), 4 * j + b + 1)
                    x = xT[:, 2 * b:2 * b + 2].rearrange("p a t -> p (a t)")
                    nc.vector.tensor_tensor(x, x, bank[4 + b][:], ALU.add).then_inc(sem("scatter_added"), 1)
                dve.wait_ge(sem("scatter_added"), 4 * j + 4)

            def compare_slots(j):
                wait(dve, "slots_compared", 3 * j)
                wait(dve, "selg_built", j)
                for i in range(2):
                    nc.vector.tensor_tensor(hit[:, i], cst("iota").unsqueeze(1).broadcast_to([P, TT, C]),
                                            choice("slot")[:, i].unsqueeze(2).broadcast_to([P, TT, C]), ALU.is_equal
                                            ).then_inc(sem("slots_compared"), 1)
                dve.wait_ge(sem("slots_compared"), 3 * j + 2)
                nc.vector.tensor_scalar(R("slot"), R("slot"), -float(C), None, ALU.add).then_inc(sem("slots_compared"), 1)

            last = PAIRS_E - 1
            compare_slots(0)
            gathered(0)
            dve_start(dve, job(0))
            compare_slots(1)
            dve_steps(dve, job(0))
            n_jobs = jobs_of(dve)
            with dve.Fori(1, n_jobs) as j:
                run, nxt = job(j - 1), job(j)
                up, down = splitter(dve, split_low, nxt)
                dve_end_a(dve, run)
                up(0, 0, 0, 0)
                dve_gated_low(dve, run, last)
                up(0, 0, 0, 1)
                gathered(j)
                up(1, 0, 1, 0)
                up(1, 0, 1, 1)
                scattered(j - 1)
                dve_gate(dve, nxt, 0, 0)
                down(0, 0, 0)
                compare_slots(j + 1)
                dve_steps(dve, nxt)
            j = last_job(dve)
            run = job(j)
            dve_end_a(dve, run)
            dve_gated_low(dve, run, last)
            scattered(j)
            settle(nc.vector.memset(mx[:, 0, 0:1], 0.0), "xT_ready")

        def choice(name):
            return R(name).rearrange("p (t i) -> p i t", i=2)

        def pool_moe(pool):
            def job_matrices(j):
                pool.wait_ge(sem("slots_compared"), 3 * j + 2)
                wait(pool, "gathered", 2 * j)
                nc.gpsimd.tensor_tensor(sel[:], hit[:, 0], hit[:, 1], ALU.add).then_inc(sem("sel_built"), 1)
                wait(pool, "gates_turned", j)
                for i in range(2):
                    nc.gpsimd.tensor_tensor((selg, selt)[i][:], hit[:, i],
                                            choice("gate")[:, i].unsqueeze(2).broadcast_to([P, TT, C]), ALU.mult
                                            ).then_inc(sem("gates_chain"), 1)
                pool.wait_ge(sem("gates_chain"), 2 * j + 2)
                nc.gpsimd.tensor_tensor(selg[:], selg[:], selt[:], ALU.add).then_inc(sem("selg_built"), 1)

            pool.wait_ge(sem("jobs_ready"), 1)
            job_matrices(0)
            n_jobs = jobs_of(pool)
            with pool.Fori(1, n_jobs) as j:
                job_matrices(j)

        @block.sync
        def _(sp):
            def load(slot, dst, src):
                sp.dma_start(dst, src).then_inc(sem(f"w_ready{slot}"), 16)

            def columns(slot, w, at, n):
                load(slot, ring[:, slot, :, 0:n], w[:, at:at + n].rearrange("(k p) n -> p k n", p=P))

            def mixer_unit(layer, u):
                if u < NU:
                    columns(u % SLOTS, A["w_in"][layer], UNITS[u][0], UNITS[u][1])
                else:
                    columns(u % SLOTS, A["w_out"][layer], (u - NU) * T, T)

            def rows(slot, w, at):
                load(slot, ring[:, slot].rearrange("p (a b) t -> p a (b t)", a=2),
                     w[at:at + 2 * P, :].rearrange("(a p) d -> p a d", p=P))

            def sp_ffn(run, w1, w3, w2, row13, row2, after_mixer):
                def free(slot, first, n):
                    if first and after_mixer:
                        sp.wait_ge(sem("unit_used"), (after_mixer - 1) * LU + last_unit(slot) + 1)
                    else:
                        sp.wait_ge(sem("w_split"), run.stages + n)

                def up(m, par, first, n):
                    for kind, w in enumerate((w1, w3)):
                        free(3 * par + kind, first, n)
                        load(3 * par + kind, ring[:, 3 * par + kind],
                             w[bass.ds(row13, D), bass.ds(m * T, T)].rearrange("(k p) n -> p k n", p=P))

                def down(m, par, first, n):
                    free(3 * par + 2, first, n)
                    load(3 * par + 2, ring[:, 3 * par + 2].rearrange("p (a b) t -> p a (b t)", a=2),
                         w2[bass.ds(row2 + m * T, T), :].rearrange("(a p) d -> p a d", p=P))

                up(0, 0, True, -5)
                up(1, 1, True, -2)
                down(0, 0, True, -1)
                up(2, 0, False, 2)
                down(1, 1, True, 0)
                with sp.Fori(0, (run.pairs - 3) // 2) as i:
                    for par in (1, 0):
                        m = 2 * i + (3 if par else 4)
                        up(m, par, False, 3 * m - 5)
                        down(m - 1, 1 - par, False, 3 * m - 4)
                if run.pairs % 2 == 0:
                    m = run.pairs - 1
                    up(m, 1, False, 3 * m - 5)
                    down(m - 1, 0, False, 3 * m - 4)
                down(run.pairs - 1, (run.pairs - 1) % 2, False, 3 * run.pairs - 4)

            sp.dma_start(const[:], A["const"]).then_inc(sem("const_in"), 16)
            sp.dma_start(wide[:].rearrange("p (a b) t -> p a (b t)", a=TT),
                         A["x"][0].rearrange("(a p) d -> p a d", p=P)).then_inc(sem("x_in"), 16)
            for layer in range(DEPTH):
                for u in range(LU):
                    slot = u % SLOTS
                    if u >= SLOTS:
                        sp.wait_ge(sem("unit_used"), layer * LU + u - SLOTS + 1)
                    elif layer:
                        sp.wait_ge(sem("w_split"), dense.last_split(slot))
                    mixer_unit(layer, u)
                if layer == 0:
                    sp_ffn(dense, A["ffn_w1"][0], A["ffn_w3"][0], A["ffn_w2"][0], 0, 0, 1)

            w1, w3 = (A[n][0].rearrange("e d f -> (e d) f") for n in ("moe_w1", "moe_w3"))
            w2 = A["moe_w2"][0].rearrange("e f d -> (e f) d")
            sp_ffn(job(0), w1, w3, w2, 0, 0, 2)
            n_jobs = jobs_of(sp)
            with sp.Fori(1, n_jobs) as j:
                e = sp.value_load(jt[0:1, bass.ds(j, 1)], min_val=0, max_val=NE - 1)
                sp_ffn(job(j), w1, w3, w2, e * D, e * FE, 0)
            sp.wait_ge(sem("out_ready"), KT // 2)
            sp.dma_start(out[0].rearrange("(a p) d -> p a d", p=P),
                         wide[:].rearrange("p (a b) t -> p a (b t)", a=TT)).then_inc(sem("out_stored"), 16)
            sp.wait_ge(sem("out_stored"), 16)

        @block.gpsimd
        def _(pool):
            settle = own(pool, "pool_chain")
            for name, n in PARAMS:
                at = PCOL[name][0]
                pool.dma_start(prow[at:at + DEPTH * n, :], A[name].rearrange("l (t p) -> (l t) p", p=P)
                               ).then_inc(sem("prow_in"), 16)
            at = PCOL["final_norm"][0]
            pool.dma_start(prow[at:at + KT, :], A["final_norm"].rearrange("(t p) -> t p", p=P)
                           ).then_inc(sem("prow_in"), 16)
            pool.dma_start(posi, A["positions"].broadcast_to([P, T])).then_inc(sem("pos_in"), 16)
            pool.dma_start(lora[0:HD], A["rwkv_w2"].rearrange("l r g -> r l g")).then_inc(sem("lora_in"), 16)
            pool.dma_start(lora[HD:P], A["rwkv_a2"].rearrange("l r g -> r l g")).then_inc(sem("lora_in"), 16)
            pool.dma_start(g2[:], A["rwkv_g2"].rearrange("l r g -> r l g")).then_inc(sem("lora_in"), 16)
            pool.dma_start(router[:], A["moe_router"][0].rearrange("(k p) e -> p k e", p=P)
                           ).then_inc(sem("router_in"), 16)

            def mla_weights(layer):
                pool.dma_start(wuq[:], A["mla_w_uq"][layer].rearrange("(k p) n -> p k n", p=P)
                               ).then_inc(sem("mla_w_in"), 16)
                pool.dma_start(wukv[:].rearrange("p h n -> p (h n)"), A["mla_w_ukv"][layer]
                               ).then_inc(sem("mla_w_in"), 16)

            mla_weights(0)
            pool.wait_ge(sem("omlb_ready"), 1)
            for layer in range(DEPTH):
                if layer:
                    pool.wait_ge(sem("mla_v_ready"), layer)
                    mla_weights(layer)
                pool.wait_ge(sem("hsig_ready"), 3 * layer + 3)
                fq = proj[:, J_HQ:J_HQ + 2].rearrange("p a t -> p (a t)")
                ff = proj[:, J_HF:J_HF + 2].rearrange("p a t -> p (a t)")
                fg = proj[:, J_HG:J_HG + 2].rearrange("p a t -> p (a t)")
                flat = hs[:].rearrange("p a b -> p (a b)")
                sf, sq = flat[:, 0:2 * T], flat[:, 2 * T:4 * T]
                sgt = hx[:].rearrange("p a b -> p (a b)")
                settle(nc.gpsimd.tensor_tensor(fq, fq, sq, ALU.mult))
                settle(nc.gpsimd.tensor_tensor(fg, fg, sgt, ALU.mult))
                for j in range(GT):
                    c = layer * GT + j
                    settle(nc.gpsimd.tensor_scalar(ff[:, j * T:(j + 1) * T], sf[:, j * T:(j + 1) * T],
                                                   omlb[:, c:c + 1], lbc[:, c:c + 1], ALU.mult, ALU.add))
                settle(nc.gpsimd.tensor_scalar(hk[:, 0], ff, -1.0, 1.0, ALU.mult, ALU.add), "hgrn_level")
                ends = ff
                for l in range(LEVELS + 1):
                    n = 1 << l
                    new, old = l % 2, (l + 1) % 2
                    if l == 0:
                        settle(nc.gpsimd.tensor_tensor(hq[:, 0], fq, ff, ALU.mult), "hgrn_level")
                        continue
                    half = n // 2
                    nb = GT * T // n
                    qo = hq[:, old].rearrange("p (b h i) -> p b h i", h=2, i=half)
                    qn = hq[:, new].rearrange("p (b h i) -> p b h i", h=2, i=half)
                    ko = hk[:, old].rearrange("p (b h i) -> p b h i", h=2, i=half)
                    kn = hk[:, new].rearrange("p (b h i) -> p b h i", h=2, i=half)
                    ev = ends.rearrange("p (b h) -> p b h", h=2)
                    if l >= 2:
                        pool.wait_ge(sem("hgrn_scored"), layer * 16 + 2 * l)
                    else:
                        pool.wait_ge(sem("hgrn_scored"), layer * 16 + 2)
                    nxt = hend[:, GT * T - 2 * nb:GT * T - nb]
                    e1 = ev[:, :, 0:1].broadcast_to([P, nb, half])
                    e2 = ev[:, :, 1:2].broadcast_to([P, nb, half])
                    settle(nc.gpsimd.tensor_tensor(qn[:, :, 1], qo[:, :, 1], e1, ALU.mult))
                    settle(nc.gpsimd.tensor_copy(qn[:, :, 0], qo[:, :, 0]))
                    settle(nc.gpsimd.tensor_tensor(kn[:, :, 0], ko[:, :, 0], e2, ALU.mult))
                    settle(nc.gpsimd.tensor_tensor(nxt, ev[:, :, 0], ev[:, :, 1], ALU.mult))
                    settle(nc.gpsimd.tensor_copy(kn[:, :, 1], ko[:, :, 1]), "hgrn_level")
                    ends = nxt
                pool.wait_ge(sem("chunk_masked"), 4 * layer + 1)
                for l in range(1, LEVELS):
                    for half in range(2):
                        if l > 1:
                            pool.wait_ge(sem("mx_ready"), 12 * layer + 2 * (l - 2) + half + 1)
                        hv = slice(4 * half, 4 * half + 4)
                        settle(nc.gpsimd.tensor_tensor(mtm[:, hv], atm[:, hv], over(lvl(l), 4), ALU.mult), "level_masked")
            pool_moe(pool)

        @block.tensor
        def _(pe):
            def mm(o, l, r, start=True, stop=True, sig=None):
                ins = nc.tensor.matmul(o, l, r, start=start, stop=stop)
                if sig:
                    ins.then_inc(sem(sig), 1)

            def turn(o, i, rows=P, sig=None):
                ins = nc.tensor.transpose(o, i, cst("id")[0:rows, 0:rows])
                if sig:
                    ins.then_inc(sem(sig), 1)

            def w_wait(slot, n):
                pe.wait_ge(sem(f"w_ready{slot}"), 16 * n)

            def norm(n):
                for half in range(2):
                    pe.wait_ge(sem("sq_ready"), 2 * n + half + 1)
                    for k in range(4 * half, 4 * half + 4):
                        mm(bank[7][:, 0:T], cst("ones"), wide[:, k], k == 0, k == KT - 1,
                           "ss_ready" if k == KT - 1 else None)

            pe.wait_ge(sem("const_in"), 16)
            pe.wait_ge(sem("x_in"), 16)
            xr = wide[:].rearrange("p (a b) t -> p a (b t)", a=TT)
            for b in range(4):
                for k in range(2):
                    for tt in range(TT):
                        turn(bank[b][:, k * T + tt * P:k * T + (tt + 1) * P],
                             xr[:, tt, (2 * b + k) * P:(2 * b + k + 1) * P],
                             sig="x_turned" if k == 1 and tt == TT - 1 else None)
            pe.wait_ge(sem("prow_in"), 16 * (len(PARAMS) + 1))
            turn(bank[4][:, 0:NPAR], prow[0:NPAR, :], NPAR, "par_turned")

            def unit(layer, u):
                slot, b = u % SLOTS, u % 2
                _, cols, token_major = UNITS[u]
                w_wait(slot, before(2 * layer, slot) + u // SLOTS + 1)
                if u >= 2:
                    pe.wait_ge(sem("unit_copied"), layer * NU + u - 1)
                if token_major:
                    for tt in range(TT):
                        for k in range(KT):
                            mm(bank[b][:, tt * G:(tt + 1) * G], hT[:, k, tt * P:(tt + 1) * P],
                               ring[:, slot, k, 0:G], k == 0, k == KT - 1,
                               "unit_used" if tt == 1 and k == KT - 1 else None)
                    return
                for ct in range(2):
                    n = min(P, cols - ct * P)
                    lo = HD if n < P else 0
                    for k in range(KT):
                        if u == 0 and ct == 0:
                            pe.wait_ge(sem("hT_ready"), 2 * layer * KT + k + 1)
                        mm(bank[b][lo:lo + n, ct * T:(ct + 1) * T], ring[:, slot, k, ct * P:ct * P + n], hT[:, k],
                           k == 0, k == KT - 1, "unit_used" if ct == 1 and k == KT - 1 else None)

            def rows(h):
                lo = HD * (h % 2)
                return lo, lo + HD, h // 2

            def mat(h, c):
                return 4 * (h % 2) + 2 * (h // 2) + c

            for layer in range(DEPTH):
                def nth(per, i=0):
                    return layer * per + i + 1

                norm(2 * layer)
                for u in range(8):
                    unit(layer, u)
                if layer == 0:
                    pe.wait_ge(sem("lora_in"), 48)
                pe.wait_ge(sem("tw_ready"), nth(2))
                for j in range(GT):
                    mm(bank[2][:, j * T:(j + 1) * T], lora[0:HD, layer, j * P:(j + 1) * P], tw[:],
                       sig="lora_ready" if j else None)
                for j in range(GT):
                    mm(bank[3][:, j * T:(j + 1) * T], lora[HD:P, layer, j * P:(j + 1) * P], sh[HD:P, 6],
                       sig="lora_ready" if j else None)
                pe.wait_ge(sem("tw_ready"), nth(2, 1))
                for j in range(GT):
                    mm(bank[4][:, j * T:(j + 1) * T], g2[:, layer, j * P:(j + 1) * P], sg[:],
                       sig="lora_ready" if j else None)
                pe.wait_ge(sem("kksq_ready"), nth(1))
                mm(bank[5][:], cst("blk"), diff[:].rearrange("p a t -> p (a t)"), sig="kkss_ready")
                for u in range(8, 11):
                    unit(layer, u)
                for e in range(LEVELS + 1):
                    pe.wait_ge(sem("hgrn_level"), nth(9, 0 if e == 0 else e))
                    for half in range(2):
                        if e or layer:
                            pe.wait_ge(sem("hgrn_masked"), layer * 16 + 2 * e + half - 1)
                        for m in range(4):
                            h, c = 2 * (m // 2) + half, m % 2
                            lo, hi, j = rows(h)
                            s = slice(j * T + c * P, j * T + (c + 1) * P)
                            src = hk[lo:hi, 0 if e == 0 else (e - 1) % 2, s]
                            qry = (proj[lo:hi, J_HQ + j, c * P:(c + 1) * P] if e == 0
                                   else hq[lo:hi, (e - 1) % 2, s])
                            mm(bank[6 + half][:, m * P:(m + 1) * P], src, qry, sig="hgrn_scored" if m == 3 else None)
                pe.wait_ge(sem("hgrn_level"), nth(9, 8))
                pe.wait_ge(sem("hgrn_masked"), nth(16, 14))
                pe.wait_ge(sem("hgrn_masked"), nth(16, 15))
                for h in range(NH):
                    lo, hi, j = rows(h)
                    mm(bank[6 + h % 2][:, j * P:(j + 1) * P], hk[lo:hi, 1, j * T:j * T + P],
                       hq[lo:hi, 1, j * T + P:j * T + T], sig="hgrn_crossed" if h == NH - 1 else None)
                for u in range(11, NU):
                    unit(layer, u)
                pe.wait_ge(sem("rkk_ready"), nth(1))
                mm(bank[5][:], cst("blk"), diff[:].rearrange("p a t -> p (a t)"), sig="bonus_ready")
                pe.wait_ge(sem("sig_ready"), nth(5, 4))
                for c in range(TT):
                    for j in range(GT):
                        turn(bank[2][:, c * G + j * P:c * G + (j + 1) * P], sh[:, J_V + j, c * P:(c + 1) * P],
                             sig="tok_turned" if c and j else None)
                pe.wait_ge(sem("chunks_ready"), nth(1))
                for i, a in enumerate((bet, kha)):
                    for j in range(GT):
                        turn(bank[3][:, i * G + j * P:i * G + (j + 1) * P], a[:, j, 0:P],
                             sig="tok_turned" if i and j else None)
                for n, (a, b, bk) in enumerate(((bet, kap, 4), (kha, kap, 6), (bet, rha, 4), (kha, rha, 6))):
                    if n == 0:
                        pe.wait_ge(sem("bonus_used"), nth(1))
                    elif n == 1:
                        pe.wait_ge(sem("hgrn_masked"), nth(16, 15))
                        pe.wait_ge(sem("hx_copied"), nth(1))
                    else:
                        pe.wait_ge(sem("chunk_masked"), nth(4, n - 2))
                    for m in range(NM):
                        h, c = 2 * (m // 2 % 2) + m // 4, m % 2
                        lo, hi, j = rows(h)
                        mm(bank[bk + m // 4][:, m % 4 * P:(m % 4 + 1) * P], a[lo:hi, j, c * P:(c + 1) * P],
                           b[lo:hi, j, c * P:(c + 1) * P], sig="chunk_ready" if m == NM - 1 else None)
                pe.wait_ge(sem("xit_ready"), nth(2 * LEVELS, 1))
                pe.wait_ge(sem("tok_copied"), nth(2, 1))
                for half in range(2):
                    for m in range(4):
                        turn(bank[2 + half][:, m * P:(m + 1) * P], xit[:, 4 * half + m], sig="xt_turned" if m == 3 else None)
                for l in range(1, LEVELS):
                    last = l == LEVELS - 1
                    for half in range(2):
                        pe.wait_ge(sem("level_masked"), nth(2 * (LEVELS - 1), 2 * (l - 1) + half))
                        pe.wait_ge(sem("xin_ready"), nth(2 * (LEVELS - 1), 2 * (l - 1) + half))
                        for m in range(4):
                            mm(bank[2 + half][:, m * P:(m + 1) * P], mtm[:, 4 * half + m], xin[:, 4 * half + m],
                               sig="mx_ready" if m == 3 else None)
                    for half in range(2):
                        pe.wait_ge(sem("pin_ready"), nth(2 * (LEVELS - 1), 2 * (l - 1) + half))
                        if l == 1 and half == 0:
                            pe.wait_ge(sem("chunk_masked"), nth(4, 3))
                        pe.wait_ge(sem("xit_ready"), nth(2 * LEVELS, 2 * (l - 1) + half))
                        if not last:
                            for m in range(4):
                                mm(bank[4 + half][:, m * P:(m + 1) * P], xit[:, 4 * half + m], pin[:, 4 * half + m],
                                   sig="xmx_ready" if m == 3 else None)
                        for m in range(4):
                            mm(bank[6 + half][:, m * P:(m + 1) * P], pin[:, 4 * half + m], xit[:, 4 * half + m],
                               sig="xmx_t_ready" if m == 3 else None)
                pe.wait_ge(sem("xit_ready"), nth(2 * LEVELS, 2 * LEVELS - 1))
                for c in range(TT):
                    for h in range(NH):
                        lo, hi, j = rows(h)
                        o = bank[2 + h % 2][:, j * HD:(j + 1) * HD]
                        if c:
                            if h == 0:
                                pe.wait_ge(sem("state_ready"), nth(1))
                            mm(o, kap[lo:hi, j, P:T], st[lo:hi, j], True, False)
                        mm(o, btm[:, mat(h, c)], vtok[:, c, h * HD:(h + 1) * HD], c == 0, True,
                           "r_ready" if h == NH - 1 else None)
                    pe.wait_ge(sem("rsol_ready"), nth(2, c))
                    for h in range(NH):
                        mm(bank[6][:, h * HD:(h + 1) * HD], xit[:, mat(h, c)], rsol[:, h],
                           sig="u_ready" if h == NH - 1 else None)
                    pe.wait_ge(sem("usol_ready"), nth(2, c))
                    if c == 0:
                        for h in range(NH):
                            lo, hi, j = rows(h)
                            o = bank[4][lo:hi, j * HD:(j + 1) * HD]
                            mm(o, btok[:, 0, h * HD:(h + 1) * HD], usol[:, 0, h], True, False)
                            mm(o, btok[:, 1, h * HD:(h + 1) * HD], vtok[:, 0, h * HD:(h + 1) * HD], False, True,
                               "state_summed" if h == NH - 1 else None)
                for h in range(NH):
                    lo, hi, j = rows(h)
                    for c in range(TT):
                        o = bank[5 - h % 2][lo:hi, j * T + c * P:j * T + (c + 1) * P]
                        if c:
                            mm(o, st[lo:hi, j], rha[lo:hi, j, P:T], True, False)
                        mm(o, usol[:, c, h], ctm[:, mat(h, c)], c == 0, False)
                        mm(o, vtok[:, c, h * HD:(h + 1) * HD], dtm[:, mat(h, c)], False, True,
                           "y_ready" if c and h == NH - 1 else None)
                pe.wait_ge(sem("ysb_ready"), nth(1))
                mm(bank[6][:], cst("blk"), ysb[:].rearrange("p a t -> p (a t)"), sig="mean_ready")
                pe.wait_ge(sem("ysq_ready"), nth(1))
                mm(bank[7][:], cst("blk"), mtm[:, 0:4].rearrange("p a t -> p (a t)"), sig="var_ready")
                pe.wait_ge(sem("unit_copied"), nth(NU, NU - 1))
                for h in range(NH):
                    lo, hi, j = rows(h)
                    it = [proj[:, J_HI + c, h * HD:(h + 1) * HD] for c in range(TT)]
                    mm(bank[0][lo:hi, j * T:j * T + P], it[0], hs[:, mat(h, 0)])
                    mm(bank[0][lo:hi, j * T + P:j * T + T], it[0], hx[:, h], True, False)
                    mm(bank[0][lo:hi, j * T + P:j * T + T], it[1], hs[:, mat(h, 1)], False, True,
                       "ho_ready" if h == NH - 1 else None)
                pe.wait_ge(sem("hosq_ready"), nth(1))
                mm(bank[1][:], cst("blk"), pin[:, 0:4].rearrange("p a t -> p (a t)"), sig="hoss_ready")
                for i, at in enumerate((J_DQ, J_DK)):
                    mm(bank[2 + i][:], cst("r64"), proj[:, at:at + 2].rearrange("p a t -> p (a t)"), sig="partner_ready")

                def attend(kind, h, query, key, value, ready):
                    lo, hi, j = rows(h)
                    n = kind * NH + h
                    b = n % 2
                    pe.wait_ge(sem(ready[0]), ready[1])
                    if n >= 2:
                        pe.wait_ge(sem("scores_used"), nth(2 * NH, n - 2))
                    mm(bank[4 + b][:, 0:P], query(0), key(0, P))
                    mm(bank[4 + b][:, P:3 * P], query(1), key(0, T), sig="scores_ready")

                def attend2(kind, h, value):
                    lo, hi, j = rows(h)
                    n = kind * NH + h
                    b = n % 2
                    pe.wait_ge(sem("probs_ready"), nth(2 * NH, n))
                    if n >= 2:
                        pe.wait_ge(sem("pts_ready"), nth(2 * NH, n - 2))
                    elif n == 0:
                        pe.wait_ge(sem("var_used"), nth(1))
                    turn(bank[6 + b][:, 0:P], ssb[:, b, 0:P])
                    turn(bank[6 + b][:, P:T], ssb[:, b, P:2 * P])
                    turn(bank[6 + b][:, T:3 * P], ssb[:, b, 2 * P:3 * P], sig="pts_turned")
                    pe.wait_ge(sem("pts_ready"), nth(2 * NH, n))
                    if n == 0:
                        pe.wait_ge(sem("ho_used"), nth(1))
                    if n == NH:
                        pe.wait_ge(sem("attn_copied"), nth(2))
                    o = bank[0]
                    mm(o[lo:hi, j * T:(j + 1) * T], value(0), pts[:, b, 0:T], True, False)
                    mm(o[lo:hi, j * T + P:(j + 1) * T], value(1), pts[:, b, T:3 * P], False, True, "attended")

                def dq(h):
                    lo, hi, j = rows(h)
                    return lambda qt: proj[lo:hi, J_DQ + j, qt * P:(qt + 1) * P]

                def dk(h):
                    lo, hi, j = rows(h)
                    return lambda a, b: proj[lo:hi, J_DK + j, a:b]

                for h in range(NH):
                    attend(0, h, dq(h), dk(h), None, ("rope_ready", nth(2, 1)))
                    if h:
                        attend2(0, h - 1, lambda kt, h=h - 1: proj[:, J_DV + kt, h * HD:(h + 1) * HD])
                attend2(0, NH - 1, lambda kt: proj[:, J_DV + kt, (NH - 1) * HD:NH * HD])
                pe.wait_ge(sem("latsq_ready"), nth(1))
                pe.wait_ge(sem("hoss_used"), nth(1))
                sq = mtm[:].rearrange("p a b -> p (a b)")
                mm(bank[1][:, 0:T], cst("ones"), sq[:, 0:T], True, False)
                mm(bank[1][:, 0:T], cst("ones"), sq[:, T:2 * T], False, True)
                mm(bank[1][:, T:2 * T], cst("ones"), sq[:, 2 * T:3 * T], sig="latss_ready")
                pe.wait_ge(sem("lat_ready"), nth(3, 2))
                pe.wait_ge(sem("mla_w_in"), 32 * (layer + 1))
                for h in range(NH):
                    for k in range(2):
                        mm(bank[2 + h // 2][0:UQ, h % 2 * T:(h % 2 + 1) * T], wuq[:, k, h * UQ:(h + 1) * UQ],
                           proj[:, J_CQ + k], k == 0, k == 1, "mlaq_ready" if k and h % 2 else None)
                mm(bank[1][HD:UQ, 0:T], cst("r96")[HD:UQ, HD:UQ], proj[HD:UQ, J_KR], sig="kr_partner")
                pe.wait_ge(sem("pts_ready"), nth(2 * NH, NH - 1))
                for h in range(NH):
                    mm(bank[6 + h // 2][0:HD, h % 2 * T:(h % 2 + 1) * T], wukv[:, h, 0:HD], proj[:, J_CKV],
                       sig="mlak_ready" if h % 2 else None)
                pe.wait_ge(sem("scores_used"), nth(2 * NH, NH - 1))
                pe.wait_ge(sem("mlaq_copied"), nth(2, 1))
                for half in range(2):
                    mm(bank[4 + half][0:UQ, :], cst("r96")[0:UQ, :], qf[:, 2 * half:2 * half + 2].rearrange("p a t -> p (a t)"),
                       sig="q_partner")
                for tt in range(TT):
                    mm(bank[2][:, tt * G:(tt + 1) * G], proj[:, J_CKV, tt * P:(tt + 1) * P], wukv[:, :, HD:2 * HD],
                       sig="mla_v_ready" if tt else None)
                for h in range(NH):
                    if h == 0:
                        pe.wait_ge(sem("mlakv_copied"), nth(3, 2))
                        pe.wait_ge(sem("kf_ready"), nth(1))
                    attend(1, h, lambda qt, h=h: qf[:, h, qt * P:(qt + 1) * P], lambda a, b, h=h: kf[:, h, a:b], None,
                           ("qf_ready", nth(1)))
                    if h:
                        attend2(1, h - 1, lambda kt, h=h - 1: mtok[:, kt, h * HD:(h + 1) * HD])
                attend2(1, NH - 1, lambda kt: mtok[:, kt, (NH - 1) * HD:NH * HD])
                for name, n in (("ya_ready", 2), ("yd_ready", 2)):
                    pe.wait_ge(sem(name), n * (layer + 1))
                pe.wait_ge(sem("attn_copied"), nth(2, 1))
                for u in range(NU, LU):
                    slot, b = u % SLOTS, 2 + u - NU
                    w_wait(slot, before(2 * layer, slot) + u // SLOTS + 1)
                    for ct in range(2):
                        for k in range(KT):
                            mm(bank[b][:, ct * T:(ct + 1) * T], ring[:, slot, k, ct * P:(ct + 1) * P], yT[:, k],
                               k == 0, k == KT - 1, "unit_used" if ct and k == KT - 1 else None)
                norm(2 * layer + 1)
                if layer == 0:
                    pe_ffn_dense(pe)
            pe_moe(pe, mm, turn)
            norm(2 * DEPTH)
            for k in range(KT):
                pe.wait_ge(sem("hT_ready"), 2 * DEPTH * KT + k + 1)
                for tt in range(TT):
                    turn(bank[k // 2][:, tt * T + k % 2 * P:tt * T + (k % 2 + 1) * P], hT[:, k, tt * P:(tt + 1) * P],
                         sig="out_turned" if k % 2 and tt else None)

        @block.scalar
        def _(act):
            settle = own(act, "act_chain")

            def f(o, i, func, sig="act_chain", scale=1.0, bias=None, accum=None):
                if bias is None and func != ACT.Copy:
                    bias = cst("zero", o.shape[0])
                kw = {"scale": scale}
                if bias is not None:
                    kw["bias"] = bias
                if accum is not None:
                    kw["accum_out"] = accum
                settle(nc.scalar.activation(o, i, func, **kw), sig)

            def copy(o, i, sig="act_chain"):
                settle(nc.scalar.copy(o, i), sig)

            def flat(a):
                return a.rearrange("p a t -> p (a t)")

            def norm(n):
                if n:
                    act.wait_ge(sem("xT_ready"), n)
                for half in range(2):
                    f(flat(wide[:, 4 * half:4 * half + 4]), flat(xT[:, 4 * half:4 * half + 4]), ACT.Square, "sq_ready")
                act.wait_ge(sem("ss_ready"), n + 1)
                f(rstd[:, 0], bank[7][:, 0:T], ACT.Sqrt, "std_ready", 1.0 / D, cst("eps_rms"))

            act.wait_ge(sem("const_in"), 16)
            for b in range(4):
                act.wait_ge(sem("x_turned"), b + 1)
                copy(flat(xT[:, 2 * b:2 * b + 2]), bank[b][:], "x_copied")
            act.wait_ge(sem("par_turned"), 1)
            copy(par[:, 0:NPAR], bank[4][:, 0:NPAR], "par_copied")
            for i in range(4):
                act.wait_ge(sem("angle_ready"), i + 1)
                f(trig[:, i], trig[:, i], ACT.Sin, "trig_ready")
            act.wait_ge(sem("lbd_ready"), 1)
            f(lbc[:, GT:2 * GT], lbc[:, GT:2 * GT], ACT.Sigmoid, "lb_ready")

            for layer in range(DEPTH):
                def nth(per, i=0):
                    return layer * per + i + 1

                norm(2 * layer)

                def unit(u):
                    at = [J_R, J_K, J_V, J_X, J_HQ, J_HF, J_HI, J_HG, J_DQ, J_DK, J_DV, J_CQ, J_CKV][u]
                    b = bank[u % 2]
                    act.wait_ge(sem("unit_used"), layer * LU + u + 1)
                    if u < NU - 1:
                        copy(flat(proj[:, at:at + 2]), b[:], "unit_copied")
                    else:
                        copy(proj[:, at], b[:, 0:T])
                        copy(proj[HD:UQ, J_KR], b[HD:UQ, T:2 * T], "unit_copied")

                for u in range(6):
                    unit(u)
                act.wait_ge(sem("shifted"), nth(8, 6))
                f(tw[:], sh[0:HD, 6], ACT.Tanh, "tw_ready")
                act.wait_ge(sem("shifted"), nth(8, 7))
                f(sg[:], sh[:, 7], ACT.Sigmoid, "tw_ready")
                unit(6)
                unit(7)
                hflat = hs[:].rearrange("p a b -> p (a b)")
                f(hflat[:, 0:2 * T], flat(proj[:, J_HF:J_HF + 2]), ACT.Sigmoid, "hsig_ready")
                f(hflat[:, 2 * T:4 * T], flat(proj[:, J_HQ:J_HQ + 2]), ACT.Sigmoid, "hsig_ready")
                f(hx[:].rearrange("p a b -> p (a b)"), flat(proj[:, J_HG:J_HG + 2]), ACT.Sigmoid, "hsig_ready")
                for i, name in enumerate(("rwkv_w0", "rwkv_a0")):
                    act.wait_ge(sem("lora_ready"), nth(3, i))
                    for j in range(GT):
                        f(rw[:, (SW, SA)[i], j], bank[2 + i][:, j * T:(j + 1) * T], ACT.Sigmoid, "sig_ready",
                          bias=prm(name, layer, j))
                act.wait_ge(sem("lora_ready"), nth(3, 2))
                copy(flat(rw[:, GG]), bank[4][:], "sig_ready")
                act.wait_ge(sem("kkr_ready"), nth(1))
                f(flat(diff[:]), flat(rw[:, KK]), ACT.Square, "kksq_ready")
                for u in range(8, 11):
                    unit(u)
                act.wait_ge(sem("kkss_ready"), nth(1))
                f(flat(rw[:, BN]), bank[5][:], ACT.Sqrt, "kkstd_ready")
                act.wait_ge(sem("logs_ready"), nth(1))
                f(flat(rw[:, WT]), flat(rw[:, CS]), ACT.Exp, "decay_ready", -DECAY)
                f(flat(rw[:, WI]), flat(rw[:, CS]), ACT.Exp, "decay_ready", DECAY)
                f(flat(rw[:, CP]), flat(rw[:, CP]), ACT.Exp, "decay_ready", -DECAY)
                f(fac[:, 0:GT], fac[:, 0:GT], ACT.Exp, "decay_ready", -DECAY)
                act.wait_ge(sem("hgrn_crossed"), nth(1))
                for half in range(2):
                    copy(hx[:].rearrange("p (j h) b -> p h j b", h=2)[:, half],
                         bank[6 + half][:, 0:2 * P].rearrange("p (j b) -> p j b", b=P), "hx_copied" if half else "act_chain")
                for u in range(11, NU):
                    unit(u)
                act.wait_ge(sem("tok_turned"), nth(2))
                copy(flat(vtok[:]), bank[2][:], "tok_copied")
                act.wait_ge(sem("tok_turned"), nth(2, 1))
                f(btok[:, 0], bank[3][:, 0:G], ACT.Copy, scale=-1.0)
                copy(btok[:, 1], bank[3][:, G:2 * G], "tok_copied")
                for l in range(1, LEVELS):
                    for half in range(2):
                        act.wait_ge(sem("mx_ready"), nth(12, 2 * (l - 1) + half))
                        if l > 1:
                            act.wait_ge(sem("xmx_t_ready"), nth(12, 2 * (l - 2) + half))
                        copy(flat(pin[:, 4 * half:4 * half + 4]), bank[2 + half][:], "pin_ready")
                for c in range(TT):
                    act.wait_ge(sem("r_ready"), nth(2, c))
                    for half in range(2):
                        copy(rsol[:].rearrange("p (j h) v -> p h j v", h=2)[:, half],
                             bank[2 + half][:, 0:2 * HD].rearrange("p (j v) -> p j v", v=HD),
                             "rsol_ready" if half else "act_chain")
                    act.wait_ge(sem("u_ready"), nth(2, c))
                    copy(flat(usol[:, c]), bank[6][:, 0:G], "usol_ready")
                act.wait_ge(sem("y_ready"), nth(1))
                copy(flat(ysb[0:HD]), bank[5][0:HD, :])
                copy(flat(ysb[HD:P]), bank[4][HD:P, :], "ysb_ready")
                act.wait_ge(sem("yc_ready"), nth(1))
                f(flat(mtm[:, 0:4]), flat(ysb[:]), ACT.Square, "ysq_ready")
                act.wait_ge(sem("ho_ready"), nth(1))
                copy(hx[:].rearrange("p a b -> p (a b)"), bank[0][:], "ho_used")
                f(flat(pin[:, 0:4]), hx[:].rearrange("p a b -> p (a b)"), ACT.Square, "hosq_ready")
                act.wait_ge(sem("var_ready"), nth(1))
                f(flat(mtm[:, 4:8]), bank[7][:], ACT.Sqrt, "var_used", 1.0 / HD, cst("eps_ln"))
                act.wait_ge(sem("hoss_ready"), nth(1))
                f(flat(pin[:, 4:8]), bank[1][:], ACT.Sqrt, "hoss_used", 1.0 / HD, cst("eps_rms"))

                def softmax(n):
                    b = n % 2
                    act.wait_ge(sem("max_ready"), nth(2 * NH, n))
                    f(ssb[:, b, 0:P], ssb[:, b, 0:P], ACT.Exp, bias=mx[:, b, 0:1], accum=den[:, b, 0:1])
                    f(ssb[:, b, P:3 * P], ssb[:, b, P:3 * P], ACT.Exp, "exp_ready", bias=mx[:, b, 1:2],
                      accum=den[:, b, 1:2])

                def turned(n):
                    b = n % 2
                    act.wait_ge(sem("pts_turned"), nth(2 * NH, n))
                    if n >= 2:
                        act.wait_ge(sem("attended"), nth(2 * NH, n - 2))
                    copy(pts[:, b], bank[6 + b][:, 0:3 * P], "pts_ready")

                for kind in range(2):
                    if kind:
                        sq = mtm[:].rearrange("p a b -> p (a b)")
                        act.wait_ge(sem("ya_ready"), nth(2, 1))
                        f(sq[:, 0:2 * T], flat(proj[:, J_CQ:J_CQ + 2]), ACT.Square)
                        f(sq[:, 2 * T:3 * T], proj[:, J_CKV], ACT.Square, "latsq_ready")
                        act.wait_ge(sem("latss_ready"), nth(1))
                        f(rstd[:, 0], bank[1][:, 0:T], ACT.Sqrt, "latstd_ready", 1.0 / G, cst("eps_rms"))
                        f(rstd[:, 1], bank[1][:, T:2 * T], ACT.Sqrt, "latstd_ready", 1.0 / P, cst("eps_rms"))
                        for half in range(2):
                            act.wait_ge(sem("mlaq_ready"), nth(2, half))
                            copy(flat(qf[:, 2 * half:2 * half + 2]), bank[2 + half][0:UQ, :], "mlaq_copied")
                        for half in range(2):
                            act.wait_ge(sem("mlak_ready"), nth(2, half))
                            copy(flat(kf[0:HD, 2 * half:2 * half + 2]), bank[6 + half][0:HD, :], "mlakv_copied")
                        act.wait_ge(sem("mla_v_ready"), nth(1))
                        copy(flat(mtok), bank[2][:], "mlakv_copied")
                    for h in range(NH):
                        softmax(kind * NH + h)
                        if h:
                            turned(kind * NH + h - 1)
                    turned(kind * NH + NH - 1)
                    act.wait_ge(sem("attended"), nth(2 * NH, kind * NH + NH - 1))
                    copy(flat(yT[:, 2 + 2 * kind:4 + 2 * kind]), bank[0][:], "attn_copied")
                act.wait_ge(sem("unit_used"), layer * LU + NU + 1)
                act_first_splits(act, (dense, job(0))[layer])
                norm(2 * layer + 1)
                if layer == 0:
                    act_ffn_dense(act)
            act_moe(act, copy, f)
            norm(2 * DEPTH)
            for b in range(4):
                act.wait_ge(sem("out_turned"), b + 1)
                copy(wide[:].rearrange("p (a b) t -> p a (b t)", a=TT)[:, :, b * T:(b + 1) * T],
                     bank[b][:].rearrange("p (a t) -> p a t", a=TT), "out_ready")

        @block.vector
        def _(dve):
            settle = own(dve, "dve_chain")

            def tt_(o, a, b, op, sig="dve_chain"):
                settle(nc.vector.tensor_tensor(o, a, b, op), sig)

            def ts(o, a, s1, s2, op0, op1=ALU.bypass, sig="dve_chain"):
                settle(nc.vector.tensor_scalar(o, a, s1, s2, op0, op1), sig)

            def stt(o, a, s, b, op0, op1, sig="dve_chain"):
                settle(nc.vector.scalar_tensor_tensor(o, a, s, b, op0, op1), sig)

            def recip(o, a, sig="dve_chain"):
                settle(nc.vector.reciprocal(o, a), sig)

            def flat(a):
                return a.rearrange("p a t -> p (a t)")

            def norm(n, name, layer):
                dve.wait_ge(sem("std_ready"), n + 1)
                recip(rstd[:, 1], rstd[:, 0])
                for k in range(KT):
                    stt(hT[:, k], xT[:, k], prm(name, layer, k), rstd[:, 1], ALU.mult, ALU.mult, "hT_ready")

            settle(nc.vector.memset(zeros[:], 0.0))
            settle(nc.vector.memset(fac[:], 0.0))
            settle(nc.vector.memset(lbc[:], 0.0))
            dve.wait_ge(sem("const_in"), 16)
            dve.wait_ge(sem("pos_in"), 16)
            ts(diff[:, 0], posi, 1.0, None, ALU.mult)
            for i, (name, quarter) in enumerate((("f64", 0.25), ("f64", 0.0), ("f96", 0.25), ("f96", 0.0))):
                ang, turns = diff[:, 1], rtmp[:, 1]
                ts(ang, diff[:, 0], cst(name), None, ALU.mult)
                ts(turns, ang, float(1 / (2 * np.pi)), quarter, ALU.mult, ALU.add)
                ts(turns, turns, ROUND, ROUND, ALU.add, ALU.subtract)
                for part in TURN:
                    stt(ang, turns, -part, ang, ALU.mult, ALU.add)
                ts(ang, ang, float(np.pi / 2) if quarter else 0.0, float(np.float32(3.1415925)), ALU.add, ALU.min)
                ts(trig[:, i], ang, float(np.float32(-3.1415925)), None, ALU.max, sig="angle_ready")
            dve.wait_ge(sem("par_copied"), 1)
            ka = PCOL["rwkv_k_a"][0]
            ts(omka[:], par[:, ka:ka + DEPTH * GT], -1.0, 1.0, ALU.mult, ALU.add)
            lb = PCOL["hgrn_lb_logits"][0]
            tt_(lbc[:, GT:2 * GT], par[:, lb + GT:lb + 2 * GT], par[:, lb:lb + GT], ALU.subtract, "lbd_ready")
            dve.wait_ge(sem("lb_ready"), 1)
            ts(omlb[:], lbc[:], -1.0, 1.0, ALU.mult, ALU.add, "omlb_ready")

            for layer in range(DEPTH):
                def nth(per, i=0):
                    return layer * per + i + 1

                norm(2 * layer, "mix_norm", layer)
                for u in range(4):
                    dve.wait_ge(sem("unit_copied"), layer * NU + u + 1)
                    a = proj[:, 2 * u:2 * u + 2]
                    tt_(diff[:, :, 1:T], a[:, :, 0:T - 1], a[:, :, 1:T], ALU.subtract)
                    ts(diff[:, :, 0:1], a[:, :, 0:1], -1.0, None, ALU.mult)
                    for j in range(2):
                        stt(sh[:, 2 * u + j], diff[:, j], prm("rwkv_mu", layer, 2 * u + j), a[:, j], ALU.mult, ALU.add,
                            "shifted")
                for j in range(GT):
                    ts(rw[:, KK, j], sh[:, J_K + j], prm("rwkv_k_k", layer, j), None, ALU.mult,
                       sig="kkr_ready" if j else "dve_chain")
                dve.wait_ge(sem("sig_ready"), nth(5, 1))
                for j in range(GT):
                    for c in range(TT):
                        s = slice(c * P, (c + 1) * P)
                        settle(nc.vector.tensor_tensor_scan(rw[:, CS, j, s], cst("ones"), rw[:, SW, j, s], 0.0,
                                                            ALU.mult, ALU.add))
                for j in range(GT):
                    mid = [rw[:, CS, j, c * P + HD - 1:c * P + HD] for c in range(TT)]
                    tt_(fac[:, j:j + 1], rw[:, CS, j, P - 1:P], mid[0], ALU.subtract)
                    tt_(fac[:, j:j + 1], fac[:, j:j + 1], mid[1], ALU.add)
                    for c in range(TT):
                        settle(nc.vector.tensor_copy(fac[:, GT + c:GT + c + 1], mid[c]))
                        s = slice(c * P, (c + 1) * P)
                        ts(rw[:, CS, j, s], rw[:, CS, j, s], fac[:, GT + c:GT + c + 1], None, ALU.subtract)
                tt_(flat(rw[:, CP]), flat(rw[:, CS]), flat(rw[:, SW]), ALU.subtract, "logs_ready")
                dve.wait_ge(sem("kkstd_ready"), nth(1))
                ts(flat(rw[:, BN]), flat(rw[:, BN]), 1e-12, None, ALU.max)
                recip(flat(rw[:, BN]), flat(rw[:, BN]))
                tt_(flat(rw[:, KK]), flat(rw[:, KK]), flat(rw[:, BN]), ALU.mult)
                dve.wait_ge(sem("sig_ready"), nth(5, 3))
                for j in range(GT):
                    c = layer * GT + j
                    ts(rw[:, KM, j], rw[:, SA, j], prm("rwkv_k_a", layer, j), omka[:, c:c + 1], ALU.mult, ALU.add)
                tt_(flat(rw[:, KM]), flat(rw[:, KM]), flat(sh[:, J_K:J_K + 2]), ALU.mult)
                tt_(flat(rw[:, BN]), flat(sh[:, J_R:J_R + 2]), flat(rw[:, KM]), ALU.mult)
                for j in range(GT):
                    ts(diff[:, j], rw[:, BN, j], prm("rwkv_r_k", layer, j), None, ALU.mult,
                       sig="rkk_ready" if j else "dve_chain")
                tt_(flat(rw[:, SA]), flat(rw[:, KK]), flat(rw[:, SA]), ALU.mult)
                dve.wait_ge(sem("decay_ready"), nth(4, 3))
                tt_(flat(kap[:]), flat(rw[:, KK]), flat(rw[:, CP]), ALU.mult)
                tt_(flat(bet[:]), flat(rw[:, SA]), flat(rw[:, WI]), ALU.mult)
                tt_(flat(kha[:]), flat(rw[:, KM]), flat(rw[:, WI]), ALU.mult)
                tt_(flat(rha[:]), flat(sh[:, J_R:J_R + 2]), flat(rw[:, WT]), ALU.mult, "chunks_ready")
                for e in range(LEVELS + 1):
                    for half in range(2):
                        dve.wait_ge(sem("hgrn_scored"), nth(16, 2 * e + half))
                        o = hs[:, 4 * half:4 * half + 4]
                        i = bank[6 + half][:].rearrange("p (a b) -> p a b", b=P)
                        if e == 0:
                            tt_(o, i, over(cst("id"), 4), ALU.mult, "hgrn_masked")
                        else:
                            settle(nc.vector.copy_predicated(o, over(lvl(e - 1), 4).bitcast(I32), i), "hgrn_masked")
                dve.wait_ge(sem("bonus_ready"), nth(1))
                tt_(flat(rw[:, BN]), bank[5][:], flat(sh[:, J_V:J_V + 2]), ALU.mult, "bonus_used")
                for n, (o, mask, sign) in enumerate(((atm, "ups", 1.0), (btm, "ups", 1.0), (ctm, "upi", -1.0),
                                                     (dtm, "upi", 1.0))):
                    dve.wait_ge(sem("chunk_ready"), nth(4, n))
                    b = 4 if n % 2 == 0 else 6
                    for half in range(2):
                        stt(o[:, 4 * half:4 * half + 4], bank[b + half][:].rearrange("p (a b) -> p a b", b=P), sign,
                            over(cst(mask), 4), ALU.mult, ALU.mult, "chunk_masked" if half else "dve_chain")
                    if n == 0:
                        for half in range(2):
                            hv = slice(4 * half, 4 * half + 4)
                            tt_(xit[:, hv], atm[:, hv], over(lvl(0), 4), ALU.mult)
                            stt(xit[:, hv], xit[:, hv], -1.0, over(cst("id"), 4), ALU.mult, ALU.add, "xit_ready")
                for half in range(2):
                    dve.wait_ge(sem("xt_turned"), nth(2, half))
                    settle(nc.vector.tensor_copy(flat(xin[:, 4 * half:4 * half + 4]), bank[2 + half][:]), "xin_ready")
                for l in range(1, LEVELS):
                    for half in range(2):
                        hv = slice(4 * half, 4 * half + 4)
                        if l < LEVELS - 1:
                            dve.wait_ge(sem("xmx_ready"), nth(10, 2 * (l - 1) + half))
                            tt_(flat(xin[:, hv]), flat(xin[:, hv]), bank[4 + half][:], ALU.subtract, "xin_ready")
                        dve.wait_ge(sem("xmx_t_ready"), nth(12, 2 * (l - 1) + half))
                        tt_(flat(xit[:, hv]), flat(xit[:, hv]), bank[6 + half][:], ALU.subtract, "xit_ready")
                dve.wait_ge(sem("state_summed"), nth(1))
                for j in range(GT):
                    ts(st[:, j], bank[4][:, j * HD:(j + 1) * HD], fac[:, j:j + 1], None, ALU.mult,
                       sig="state_ready" if j else "dve_chain")
                dve.wait_ge(sem("mean_ready"), nth(1))
                stt(flat(ysb[:]), bank[6][:], -1.0 / HD, flat(ysb[:]), ALU.mult, ALU.add, "yc_ready")
                dve.wait_ge(sem("var_used"), nth(1))
                recip(flat(mtm[:, 4:8]), flat(mtm[:, 4:8]))
                tt_(flat(ysb[:]), flat(ysb[:]), flat(mtm[:, 4:8]), ALU.mult)
                for j in range(GT):
                    ts(ysb[:, j], ysb[:, j], prm("rwkv_ln_w", layer, j), prm("rwkv_ln_b", layer, j), ALU.mult, ALU.add)
                    tt_(ysb[:, j], ysb[:, j], rw[:, BN, j], ALU.add)
                    tt_(yT[:, j], ysb[:, j], rw[:, GG, j], ALU.mult, "ya_ready")
                dve.wait_ge(sem("hoss_used"), nth(1))
                recip(flat(pin[:, 4:8]), flat(pin[:, 4:8]))
                hxf = hx[:].rearrange("p a b -> p (a b)")
                tt_(hxf, hxf, flat(pin[:, 4:8]), ALU.mult)
                for j in range(GT):
                    stt(yT[:, 6 + j], hxf[:, j * T:(j + 1) * T], prm("hgrn_g_norm", layer, j), proj[:, J_HG + j],
                        ALU.mult, ALU.mult, "yd_ready")
                dve.wait_ge(sem("trig_ready"), 4)
                for i, at in enumerate((J_DQ, J_DK)):
                    dve.wait_ge(sem("partner_ready"), nth(2, i))
                    tt_(rtmp[:], bank[2 + i][:].rearrange("p (a t) -> p a t", t=T), over(trig[:, 1], 2), ALU.mult)
                    tt_(proj[:, at:at + 2], proj[:, at:at + 2], over(trig[:, 0], 2), ALU.mult)
                    tt_(proj[:, at:at + 2], proj[:, at:at + 2], rtmp[:], ALU.add, "rope_ready")

                def scores(n, scale, mask):
                    b = n % 2
                    dve.wait_ge(sem("scores_ready"), nth(2 * NH, n))
                    if n >= 2:
                        dve.wait_ge(sem("pts_turned"), nth(2 * NH, n - 2))
                    stt(ssb[:, b], bank[4 + b][:, 0:3 * P], scale, cst(mask), ALU.mult, ALU.add, "scores_used")
                    settle(nc.vector.tensor_reduce(mx[:, b, 0:1], ssb[:, b, 0:P], AX.X, ALU.max, negate=True))
                    settle(nc.vector.tensor_reduce(mx[:, b, 1:2], ssb[:, b, P:3 * P], AX.X, ALU.max, negate=True), "max_ready")

                def probs(n):
                    b = n % 2
                    dve.wait_ge(sem("exp_ready"), nth(2 * NH, n))
                    recip(den[:, b], den[:, b])
                    ts(ssb[:, b, 0:P], ssb[:, b, 0:P], den[:, b, 0:1], None, ALU.mult)
                    ts(ssb[:, b, P:3 * P], ssb[:, b, P:3 * P], den[:, b, 1:2], None, ALU.mult, sig="probs_ready")

                for kind in range(2):
                    if kind:
                        dve.wait_ge(sem("latstd_ready"), nth(2, 1))
                        recip(flat(rstd[:]), flat(rstd[:]))
                        for k in range(2):
                            stt(proj[:, J_CQ + k], proj[:, J_CQ + k], prm("mla_q_norm", layer, k), rstd[:, 0],
                                ALU.mult, ALU.mult, "lat_ready")
                        stt(proj[:, J_CKV], proj[:, J_CKV], prm("mla_kv_norm", layer, 0), rstd[:, 1],
                            ALU.mult, ALU.mult, "lat_ready")
                        r = slice(HD, UQ)
                        dve.wait_ge(sem("kr_partner"), nth(1))
                        tt_(rtmp[r, 0], bank[1][r, 0:T], trig[r, 3], ALU.mult)
                        tt_(proj[r, J_KR], proj[r, J_KR], trig[r, 2], ALU.mult)
                        tt_(kf[r], over(proj[r, J_KR], NH), over(rtmp[r, 0], NH), ALU.add, "kf_ready")
                        for half in range(2):
                            dve.wait_ge(sem("q_partner"), nth(2, half))
                            hv = slice(2 * half, 2 * half + 2)
                            tt_(rtmp[r], bank[4 + half][r, :].rearrange("p (a t) -> p a t", t=T), over(trig[r, 3], 2), ALU.mult)
                            tt_(qf[r, hv], qf[r, hv], over(trig[r, 2], 2), ALU.mult)
                            tt_(qf[r, hv], qf[r, hv], rtmp[r], ALU.add, "qf_ready" if half else "dve_chain")
                    scale = float(np.float32(HD ** -0.5 if kind == 0 else UQ ** -0.5))
                    for h in range(NH):
                        scores(kind * NH + h, scale, ("dil", "caus")[kind])
                        if h:
                            probs(kind * NH + h - 1)
                    probs(kind * NH + NH - 1)
                for u in range(NO):
                    dve.wait_ge(sem("unit_used"), layer * LU + NU + u + 1)
                    tt_(flat(xT[:, 2 * u:2 * u + 2]), flat(xT[:, 2 * u:2 * u + 2]), bank[2 + u][:], ALU.add,
                        "xT_ready" if u == NO - 1 else "dve_chain")
                dve_first_splits(dve, (dense, job(0))[layer])
                norm(2 * layer + 1, "ffn_norm", layer)
                if layer == 0:
                    dve_ffn_dense(dve, tt_)
            dve_moe(dve, settle, tt_, ts, stt, recip)
            norm(2 * DEPTH, "final_norm", 0)


NAMES = ["x", "positions", "mix_norm", "w_in", "w_out", "rwkv_mu", "rwkv_w0", "rwkv_w2", "rwkv_a0", "rwkv_a2", "rwkv_g2",
         "rwkv_k_k", "rwkv_k_a", "rwkv_r_k", "rwkv_ln_w", "rwkv_ln_b", "mla_q_norm", "mla_w_uq", "mla_kv_norm",
         "mla_w_ukv", "hgrn_lb_logits", "hgrn_g_norm", "ffn_norm", "ffn_w1", "ffn_w3", "ffn_w2", "moe_router",
         "moe_w1", "moe_w3", "moe_w2", "final_norm"]


def kernel(**inputs):
    import concourse.bacc as bacc
    from concourse.bass_utils import run_bass_kernel_spmd

    nc = bacc.Bacc("TRN2", target_bir_lowering=False, num_devices=1)
    arrays = {f"in_{n}": np.ascontiguousarray(inputs[n]) for n in NAMES}
    arrays["in_const"] = constants()
    aps = {n[3:]: nc.dram_tensor(n, a.shape, mybir.dt.from_np(a.dtype), kind="ExternalInput").ap()
           for n, a in arrays.items()}
    out = nc.dram_tensor("out", (1, T, D), F32, kind="ExternalOutput").ap()
    program(nc, aps, out)
    r = run_bass_kernel_spmd(nc, [arrays], core_ids=[0])
    return r.results[0]["out"]
```

```python
from contextlib import ExitStack

import numpy as np

import concourse.bass as bass
from concourse import mybir

F32 = mybir.dt.float32
F32R = mybir.dt.float32r
I32 = mybir.dt.int32
U32 = mybir.dt.uint32
BF16 = mybir.dt.bfloat16
ALU = mybir.AluOpType
ACT = mybir.ActivationFunctionType
AX = mybir.AxisListType

P = 128
D = 1024
T = 256
DEPTH = 2
KT = D // P
TT = T // P
G = D // 4
GT = G // P
HD = 64
NH = G // HD
NM = NH * TT
UQ = 96
FF = 2816
FE = 3584
NE = 8
C = P
MAXJOBS = 16
RWKV_EPS = 64e-5
RMS_EPS = 1e-6
DECAY = float(np.exp(np.float32(-0.5)))
NEG = -1e30
ROUND = 1.5 * 2.0 ** 23
TURN = (6.28125, 0.0019340515136718750, 1.2556659146e-06)
LEVELS = 7

UNITS = [(0, 256, False), (256, 256, False), (512, 256, False), (768, 256, False),
         (2208, 256, False), (2464, 256, False), (2720, 256, True), (2976, 256, False),
         (1024, 256, False), (1280, 256, False), (1536, 256, True),
         (1792, 256, False), (2048, 160, False)]
NU = len(UNITS)
J_R, J_K, J_V, J_X, J_HQ, J_HF, J_HI, J_HG, J_DQ, J_DK, J_DV, J_CQ, J_CKV, J_KR = \
    0, 2, 4, 6, 8, 10, 12, 14, 16, 18, 20, 22, 24, 25
NO = 4
LU = NU + NO
RING_M = 4
SLOTS = 6
UP, DOWN = ((4, 5), (2, 3)), (1, 0)

PARAMS = [("mix_norm", 8), ("rwkv_mu", 8), ("rwkv_w0", 2), ("rwkv_a0", 2), ("rwkv_k_k", 2), ("rwkv_k_a", 2),
          ("rwkv_r_k", 2), ("rwkv_ln_w", 2), ("rwkv_ln_b", 2), ("mla_q_norm", 2), ("mla_kv_norm", 1),
          ("hgrn_g_norm", 2), ("hgrn_lb_logits", 2), ("ffn_norm", 8)]
PCOL, _at = {}, 0
for _name, _n in PARAMS:
    PCOL[_name] = (_at, _n)
    _at += DEPTH * _n
PCOL["final_norm"] = (_at, KT)
NPAR = _at + KT

CCOL, _at = {}, 0
for _name, _n in [("id", P), ("ones", P), ("blk", P), ("r64", P), ("r96", UQ), ("upi", P), ("ups", P),
                  ("lv", LEVELS * P), ("dil", 3 * P), ("caus", 3 * P), ("iota", P), ("f64", 1), ("f96", 1),
                  ("eps_rms", 1), ("eps_ln", 1), ("zero", 1)]:
    CCOL[_name] = (_at, _n)
    _at += _n
NCONST = _at


def constants():
    c = np.zeros((P, NCONST), np.float32)

    def put(name, a):
        at, n = CCOL[name]
        a = np.asarray(a, np.float32)
        c[:a.shape[0], at:at + n] = a.reshape(a.shape[0], n)

    i = np.arange(P)
    put("id", np.eye(P))
    put("ones", np.ones((P, P)))
    put("blk", (i[:, None] // HD == i[None, :] // HD))

    def rotate(lo, n, width):
        r = np.zeros((width, width))
        for b in range(lo, width, n):
            for q in range(n // 2):
                r[b + n // 2 + q, b + q] = -1.0
                r[b + q, b + n // 2 + q] = 1.0
        return r

    put("r64", rotate(0, HD, P))
    put("r96", rotate(HD, UQ - HD, UQ))
    put("upi", i[:, None] <= i[None, :])
    put("ups", i[:, None] < i[None, :])
    lv = np.zeros((P, LEVELS, P))
    for l in range(LEVELS):
        half = 1 << l
        same = i[:, None] // (2 * half) == i[None, :] // (2 * half)
        lv[:, l] = same & ((i[:, None] // half) % 2 == 0) & ((i[None, :] // half) % 2 == 1)
    put("lv", lv)
    q, k = np.arange(T)[:, None], np.arange(T)[None, :]
    d = q - k
    count = ((d >= 0) & (d <= 128)) + 0.0
    count += (d >= 0) & (d % 4 == 0) & (d // 4 <= 128)
    count += (d >= 0) & (d % 16 == 0) & (d // 16 <= 128)
    dil = np.where(count > 0, np.log(np.maximum(count, 1.0)), NEG)
    caus = np.where(d >= 0, 0.0, NEG)
    for name, m in (("dil", dil), ("caus", caus)):
        put(name, np.concatenate([m[:P, :P], m[P:, :]], axis=1))
    put("iota", np.broadcast_to(i, (P, P)))
    f64 = 1.0 / (np.float32(10000.0) ** (np.arange(0, HD, 2, dtype=np.float32) / np.float32(HD)))
    f32_ = 1.0 / (np.float32(10000.0) ** (np.arange(0, 32, 2, dtype=np.float32) / np.float32(32)))
    put("f64", f64[i % 32][:, None])
    put("f96", np.where((i >= HD) & (i < UQ), f32_[(i - HD) % 16], 0.0)[:, None])
    put("eps_rms", np.full((P, 1), RMS_EPS))
    put("eps_ln", np.full((P, 1), RWKV_EPS))
    put("zero", np.zeros((P, 1)))
    return c


def program(nc, A, out):
    ctx = ExitStack()
    with ctx:
        mixer = ExitStack()

        def sb(name, shape, dt=F32, where=ctx):
            return where.enter_context(nc.sbuf_tensor(name, shape, dt))

        def mx_sb(name, shape):
            return sb(name, shape, where=mixer)

        sems = {}

        def sem(name):
            if name not in sems:
                sems[name] = ctx.enter_context(nc.semaphore(name))
            return sems[name]

        ring = sb("ring", [P, RING_M, KT, T])
        const = sb("const", [P, NCONST])
        par = sb("par", [P, NPAR])
        omka = sb("omka", [P, DEPTH * GT])
        lbc = sb("lbc", [P, DEPTH * GT])
        omlb = sb("omlb", [P, DEPTH * GT])
        lora = sb("lora", [P, DEPTH, G])
        g2 = sb("g2", [P, DEPTH, G])
        wuq = sb("wuq", [P, 2, NH * UQ])
        wukv = sb("wukv", [P, NH, 2 * HD])
        router = sb("router", [P, KT, NE])
        trig = sb("trig", [P, 4, T])
        xT = sb("xT", [P, KT, T])
        hT = sb("hT", [P, KT, T])
        zeros = sb("zeros", [1, 640], BF16)
        tiny = sb("tiny", [P, 1])
        wide = sb("wide", [P, KT, T])
        rstd = sb("rstd", [P, 2, T])
        xh = sb("xh", [P, KT, T], F32R)
        xl = sb("xl", [P, KT, T], F32R)
        proj = mx_sb("proj", [P, 26, T])
        diff = mx_sb("diff", [P, GT, T])
        tw = mx_sb("tw", [HD, T])
        sg = mx_sb("sg", [P, T])
        rw = mx_sb("rw", [P, 10, GT, T])
        kap, bet, kha, rha = (mx_sb(n, [P, GT, T]) for n in ("kap", "bet", "kha", "rha"))
        st = mx_sb("st", [P, GT, HD])
        fac = mx_sb("fac", [P, 2 * GT])
        hq = mx_sb("hq", [P, 2, GT * T])
        hk = mx_sb("hk", [P, 2, GT * T])
        hend = mx_sb("hend", [P, GT * T])
        hs = mx_sb("hs", [P, NM, P])
        hx = mx_sb("hx", [P, NH, P])
        ssb = mx_sb("ssb", [P, 3, 3 * P])
        pts = mx_sb("pts", [P, 2, 3 * P])
        rtmp = mx_sb("rtmp", [P, 2, T])
        mx = mx_sb("mx", [P, 3, 2])
        den = mx_sb("den", [P, 3, 2])
        projecting = ExitStack()
        mh, ml = (sb(n, [P, 2, 4, T], F32R, projecting) for n in ("mh", "ml"))
        projecting.close()
        mtm = mx_sb("mtm", [P, NM, P])
        pin = mx_sb("pin", [P, NM, P])
        vtok = mx_sb("vtok", [P, TT, G])
        btok = mx_sb("btok", [P, 2, G])
        rsol = mx_sb("rsol", [P, NH, HD])
        usol = mx_sb("usol", [P, TT, NH, HD])
        sh = wide
        yT = hT
        SW, SA, CS, CP, KK, KM, WT, WI, GG, BN = range(10)

        def pair(buf, at):
            return buf[:, at:at + 2].rearrange("p s a (b c) -> p (s a b) c", c=P)

        atm, btm, ctm, dtm = (pair(rw, 2 * i) for i in range(4))
        xin = proj[:, 0:4].rearrange("p a (b c) -> p (a b) c", c=P)
        xit = proj[:, 4:8].rearrange("p a (b c) -> p (a b) c", c=P)
        mtok = proj[:, J_HF:J_HF + 2]
        qf = hq[0:UQ].rearrange("p a (h t) -> p (a h) t", t=T)
        kf = hk[0:UQ].rearrange("p a (h t) -> p (a h) t", t=T)
        ysb = diff
        posi = rtmp[:, 0].bitcast(I32)
        mixer.close()
        ring2 = sb("ring2", [P, SLOTS - RING_M, KT, T])
        wh = sb("wh", [P, 3, 8 * T], F32R)
        wl = sb("wl", [P, 3, 8 * T], F32R)
        gh = sb("gh", [P, 2, T], F32R)
        gl = sb("gl", [P, 2, T], F32R)
        silu = sb("silu", [P, 2, T])
        gate = sb("gate", [P, 2, T])
        yj = sb("yj", [P, D])
        sel = sb("sel", [P, TT, C])
        selg = sb("selg", [P, TT, C])
        selt = sb("selt", [P, TT, C])
        hit = sb("hit", [P, 2, TT, C])
        pgt = sb("pgt", [P, T])
        rt = sb("rt", [P, T])
        jt = sb("jt", [P, 2 * MAXJOBS], I32)
        idx = sb("idx", [P, 16], U32)

        bank = [ctx.enter_context(nc.psum_tensor(f"bank{i}", [P, 512], F32)) for i in range(8)]

        def cst(name, rows=P):
            at, n = CCOL[name]
            return const[0:rows, at:at + n]

        def lvl(l):
            at = CCOL["lv"][0] + l * P
            return const[:, at:at + P]

        def prm(name, layer, j, lo=0, hi=P):
            at, n = PCOL[name]
            return par[lo:hi, at + layer * n + j:at + layer * n + j + 1]

        def over(ap, n):
            return ap.unsqueeze(1).broadcast_to([ap.shape[0], n, ap.shape[1]])

        block = ctx.enter_context(nc.Block())

        CH_D, CH_E = FF // P, FE // P
        PAIRS_D, PAIRS_E = CH_D // 2, CH_E // 2

        def last_unit(s):
            return max(u for u in range(LU) if u % RING_M == s)


        def own(eng, chain):
            count = {}

            def settle(ins, sig=chain):
                ins.then_inc(sem(sig), 1)
                count[sig] = count.get(sig, 0) + 1
                eng.wait_ge(sem(sig), count[sig])
            return settle

        SUMS = [7] * (2 * DEPTH) + [0]

        def wait(eng, name, n):
            if not isinstance(n, int) or n > 0:
                eng.wait_ge(sem(name), n)

        def parity(slot):
            return 0 if slot in (*UP[0], DOWN[0]) else 1

        def slot_of(slot):
            return ring[:, slot] if slot < RING_M else ring2[:, slot - RING_M]

        unit_loads = [len([u for u in range(LU) if u % RING_M == s]) if s < RING_M else 0 for s in range(SLOTS)]
        dense_loads = [(PAIRS_D + 1 - parity(s)) // 2 for s in range(SLOTS)]

        def before(phase, s):
            return [0, unit_loads[s], unit_loads[s] + dense_loads[s], 2 * unit_loads[s] + dense_loads[s]][phase]

        class Run:
            def __init__(self, pairs, moe, stages, items, before_pairs, loads):
                self.pairs, self.moe = pairs, moe
                self.stages, self.items, self.before_pairs = stages, items, before_pairs
                self.loads = loads
                self.parts = 1 if moe else 2

            def up(self, m, part):
                if isinstance(m, int) and m == 0:
                    return self.stages + part, part
                return self.stages + 3 * m - 1 + part, (2, 0)[part]

            def down(self, m, last=False):
                if last:
                    return self.stages + 3 * self.pairs - 1, 2
                return self.stages + 3 * m + 4, 1

            def load(self, slot, half_m):
                return 16 * (self.loads(slot) + half_m + 1)

            def item(self, m):
                return self.items + self.parts * m

            def last_split(self, slot):
                m = max(q for q in range(self.pairs) if q % 2 == parity(slot))
                return 1 + (self.down(m, m == self.pairs - 1)[0] if slot in DOWN else self.up(m, 1)[0])

        dense = Run(PAIRS_D, False, 0, 0, 0, lambda s: before(1, s))

        def job(j):
            return Run(PAIRS_E, True, 3 * PAIRS_D + 3 * PAIRS_E * j, 2 * PAIRS_D + PAIRS_E * j,
                       PAIRS_D + PAIRS_E * j, lambda s: before(3, s) + PAIRS_E // 2 * j)

        TURNS = 4
        SCATTER = (2, 3, 5, 6)

        def up_bank(run, par, item):
            return bank[par if run.moe else 6 * par + item]

        def pe_up(pe, run, m, par, part):
            stage, buf = run.up(m, part)
            pe.wait_ge(sem("w_split"), stage + 1)
            if part == 0:
                wait(pe, "gated", run.item(m - 1))
            w = [b[:, buf].rearrange("p (k n) -> p k n", n=2 * T) for b in (wh, wl)]
            for item in range(run.parts):
                for kind in range(1 if run.moe else 2):
                    for k in range(4):
                        for n, (a, b) in enumerate(((0, 0), (0, 1), (1, 0))):
                            x = (xh, xl)[a][:, 4 * part + k]
                            kw = {"start": part == kind == k == n == 0, "stop": part == 1 and k == 3 and n == 2,
                                  "skip_group_check": True}
                            if run.moe:
                                ins = nc.tensor.matmul(up_bank(run, par, 0)[:], x[:, 0:C], w[b][:, k], **kw)
                            else:
                                at = kind * T + item * P
                                ins = nc.tensor.matmul(up_bank(run, par, item)[:, kind * T:(kind + 1) * T],
                                                       w[b][:, k, at:at + P], x, **kw)
            ins.then_inc(sem("stage_used"), 1)

        def pe_turn_gated(pe, run, m):
            if run.moe:
                pe.wait_ge(sem("gated"), run.item(m) + 1)
                pe.wait_ge(sem("g_split"), run.before_pairs + m)
                for a in range(2):
                    ins = nc.tensor.transpose(bank[TURNS][:, a * P:(a + 1) * P], gate[:, 0, a * P:(a + 1) * P], cst("id"))
                ins.then_inc(sem("g_turned"), 1)

        def pe_down(pe, run, m, last=False):
            stage, buf = run.down(m, last)
            pe.wait_ge(sem("w_split"), stage + 1)
            pe.wait_ge(sem("g_split"), run.before_pairs + m + 1)
            w = [b[:, buf].rearrange("p (a n) -> p a n", a=2) for b in (wh, wl)]
            for o in range(2 if run.moe else KT):
                for a in range(2):
                    for g, b in ((gh, 0), (gh, 1), (gl, 0)):
                        if run.moe:
                            ins = nc.tensor.matmul(bank[2 + o][:], g[:, a, 0:C], w[b][:, a, o * 512:(o + 1) * 512],
                                                   start=False, stop=False, skip_group_check=True)
                        else:
                            ins = nc.tensor.matmul(bank[2 + o // 2][:, o % 2 * T:(o % 2 + 1) * T],
                                                   w[b][:, a, o * P:(o + 1) * P], g[:, a],
                                                   start=False, stop=False, skip_group_check=True)
                if last and not run.moe and o % 2 and o < KT - 1:
                    ins.then_inc(sem("acc_ready"), 1)
            ins.then_inc(sem("stage_used"), 1)

        def pe_steps(pe, run):
            def step(m, par):
                pe_up(pe, run, m, par, 0)
                pe_turn_gated(pe, run, m - 1)
                pe_up(pe, run, m, par, 1)
                pe_down(pe, run, m - 1)

            n = run.pairs - 1
            with pe.Fori(0, n // 2) as i:
                step(2 * i + 1, 1)
                step(2 * i + 2, 0)
            if n % 2:
                step(n, 1)

        def zero_acc(banks_):
            for b in banks_:
                nc.tensor.matmul(bank[b][:], zeros[:, 0:P], zeros[:, P:P + 512], start=True, stop=True)

        def split_high(act, stage, buf, src, split):
            wait(act, "stage_used", stage - 2)
            for slot, n in src[1]:
                act.wait_ge(sem(f"w_ready{slot}"), n)
            o = split(wh[:, buf])
            nc.scalar.activation(o, src[0], ACT.Copy).then_inc(sem("w_high"), 1)

        def split_low(dve, stage, buf, src, split):
            dve.wait_ge(sem("w_high"), stage + 1)
            nc.vector.tensor_tensor(split(wl[:, buf]), src[0], split(wh[:, buf]).bitcast(F32), ALU.subtract
                                    ).then_inc(sem("w_split"), 1)

        def splitter(eng, fn, run):
            def up(m, half_m, par, part):
                slots = UP[par]
                src = (ring[:, slots[0]:slots[0] + 2] if slots[0] < RING_M else ring2[:])[:, :, 4 * part:4 * part + 4]
                fn(eng, *run.up(m, part), (src, [(s, run.load(s, half_m)) for s in slots]),
                   lambda w: w.rearrange("p (k a n) -> p a k n", a=2, n=T))

            def down(m, half_m, par, last=False):
                s = DOWN[par]
                fn(eng, *run.down(m, last), (slot_of(s).rearrange("p a t -> p (a t)"), [(s, run.load(s, half_m))]),
                   lambda w: w)
            return up, down

        def act_split(act, run):
            return splitter(act, split_high, run)

        def act_silu(act, run, m, par):
            for item in range(run.parts):
                act.wait_ge(sem("stage_used"), run.up(m, 1)[0] + 1)
                wait(act, "gated", run.item(m - 1) + item + 1)
                nc.scalar.activation(silu[:, item], up_bank(run, par, item)[:, 0:T], ACT.Silu, bias=cst("zero")
                                     ).then_inc(sem("silu_done"), 1)

        def act_gated_high(act, run, m):
            if run.moe:
                act.wait_ge(sem("g_turned"), run.before_pairs - PAIRS_D + m + 1)
                o, i = gh[:, :, 0:C], bank[TURNS][:, 0:2 * C].rearrange("p (a c) -> p a c", c=C)
            else:
                act.wait_ge(sem("gated"), run.item(m) + 2)
                o, i = gh[:], gate[:]
            prev = run.stages if isinstance(m, int) and m == 0 else run.down(m - 1)[0] + 1
            wait(act, "stage_used", prev)
            nc.scalar.activation(o, i, ACT.Copy).then_inc(sem("g_high"), 1)

        def act_start(act, run):
            up, down = act_split(act, run)
            up(1, 0, 1, 1)
            act_silu(act, run, 0, 0)
            down(0, 0, 0)

        def steps(eng, run, body):
            n = run.pairs - 2
            with eng.Fori(0, n // 2) as i:
                body(2 * i + 1, i, i + 1, 1)
                body(2 * i + 2, i + 1, i + 1, 0)
            if n % 2:
                body(n, n // 2, n // 2 + 1, 1)

        def act_steps(act, run):
            up, down = act_split(act, run)

            def step(m, half_m, half_next, par):
                act_gated_high(act, run, m - 1)
                up(m + 1, half_next, 1 - par, 0)
                act_silu(act, run, m, par)
                up(m + 1, half_next, 1 - par, 1)
                down(m, half_m, par)

            steps(act, run, step)

        def act_end_a(act, run):
            m, par = run.pairs - 1, (run.pairs - 1) % 2
            act_gated_high(act, run, m - 1)
            act_split(act, run)[1](m, m // 2, par, True)
            act_silu(act, run, m, par)

        def dve_gate(dve, run, m, par):
            for item in range(run.parts):
                dve.wait_ge(sem("silu_done"), run.item(m) + item + 1)
                wait(dve, "g_split", run.before_pairs + m)
                nc.vector.tensor_tensor(gate[:, item], up_bank(run, par, item)[:, T:2 * T], silu[:, item], ALU.mult
                                        ).then_inc(sem("gated"), 1)

        def dve_gated_low(dve, run, m):
            dve.wait_ge(sem("g_high"), run.before_pairs + m + 1)
            if run.moe:
                o, i, h = gl[:, :, 0:C], bank[TURNS][:, 0:2 * C].rearrange("p (a c) -> p a c", c=C), gh[:, :, 0:C]
            else:
                o, i, h = gl[:], gate[:], gh[:]
            nc.vector.tensor_tensor(o, i, h.bitcast(F32), ALU.subtract).then_inc(sem("g_split"), 1)

        def dve_start(dve, run):
            up, down = splitter(dve, split_low, run)
            up(1, 0, 1, 1)
            dve_gate(dve, run, 0, 0)
            down(0, 0, 0)

        def dve_steps(dve, run):
            up, down = splitter(dve, split_low, run)

            def step(m, half_m, half_next, par):
                dve_gated_low(dve, run, m - 1)
                up(m + 1, half_next, 1 - par, 0)
                dve_gate(dve, run, m, par)
                up(m + 1, half_next, 1 - par, 1)
                down(m, half_m, par)

            steps(dve, run, step)

        def dve_end_a(dve, run):
            m, par = run.pairs - 1, (run.pairs - 1) % 2
            dve_gated_low(dve, run, m - 1)
            splitter(dve, split_low, run)[1](m, m // 2, par, True)
            dve_gate(dve, run, m, par)

        def pe_ffn_dense(pe):
            zero_acc((2, 3, 4, 5))
            for part in range(2):
                pe.wait_ge(sem("x_split"), x_before(0, 2) + part + 1)
                pe_up(pe, dense, 0, 0, part)
            pe_steps(pe, dense)
            pe_down(pe, dense, PAIRS_D - 1, True)

        def x_before(layer, i):
            return 2 * (3 * layer + i)

        def act_split_x(act, norm, halves=(0, 1)):
            for half in halves:
                hv = slice(4 * half, 4 * half + 4)
                if norm is not None:
                    act.wait_ge(sem("hT_ready"), norm * KT + 4 * half + 4)
                nc.scalar.activation(xh[:, hv], hT[:, hv], ACT.Copy).then_inc(sem("x_high"), 1)

        def act_ffn_dense(act):
            act_start(act, dense)
            act_steps(act, dense)
            act_end_a(act, dense)
            act_gated_high(act, dense, PAIRS_D - 1)

        def dve_split_x(dve, n, halves=(0, 1)):
            for half in halves:
                hv = slice(4 * half, 4 * half + 4)
                dve.wait_ge(sem("x_high"), n + half + 1)
                nc.vector.tensor_tensor(xl[:, hv], hT[:, hv], xh[:, hv].bitcast(F32), ALU.subtract
                                        ).then_inc(sem("x_split"), 1)

        def dve_ffn_dense(dve, tt_):
            dve_start(dve, dense)
            dve_steps(dve, dense)
            dve_end_a(dve, dense)
            dve_gated_low(dve, dense, PAIRS_D - 1)
            for u in range(NO):
                if u < NO - 1:
                    dve.wait_ge(sem("acc_ready"), u + 1)
                else:
                    dve.wait_ge(sem("stage_used"), 3 * PAIRS_D)
                x = xT[:, 2 * u:2 * u + 2].rearrange("p a t -> p (a t)")
                tt_(x, x, bank[2 + u][:], ALU.add, "xT_ready")

        def unit_columns(u):
            return P if u == NU - 1 else T

        def act_unit_split(act, layer, u, part):
            slot, n = u % RING_M, unit_columns(u)
            act.wait_ge(sem(f"w_ready{slot}"), 16 * (before(2 * layer, slot) + u // RING_M + 1))
            wait(act, ("half_used", "unit_used")[part], layer * LU + u)
            nc.scalar.activation(mh[:, part, :, 0:n], ring[:, slot, 4 * part:4 * part + 4, 0:n], ACT.Copy
                                 ).then_inc(sem("unit_high"), 1)

        def dve_unit_split(dve, layer, u, part):
            slot, n = u % RING_M, unit_columns(u)
            dve.wait_ge(sem("unit_high"), 2 * (layer * LU + u) + part + 1)
            nc.vector.tensor_tensor(ml[:, part, :, 0:n], ring[:, slot, 4 * part:4 * part + 4, 0:n],
                                    mh[:, part, :, 0:n].bitcast(F32), ALU.subtract).then_inc(sem("unit_split"), 1)

        def pe_unit_half(pe, layer, u, part, o, lhs_is_weight):
            pe.wait_ge(sem("unit_split"), 2 * (layer * LU + u) + part + 1)
            groups = unit_columns(u) // P if lhs_is_weight else TT
            for c in range(groups):
                for k in range(4):
                    for n, (a, b) in enumerate(((0, 0), (0, 1), (1, 0))):
                        x, w = (xh, xl)[a][:, 4 * part + k], (mh, ml)[b][:, part, k]
                        l, r = (w[:, c * P:(c + 1) * P], x) if lhs_is_weight else (x[:, c * P:(c + 1) * P], w)
                        ins = nc.tensor.matmul(o[:, c * T:(c + 1) * T], l, r, start=part == c == k == n == 0,
                                               stop=part == 1 and k == 3 and n == 2, skip_group_check=True)
            return ins

        rtc = {}
        _c = 0
        for _n, _w in (("logit", 16), ("top", 16), ("idx", 16), ("oh1", 16), ("oh2", 16), ("sel", 16), ("e", 2),
                       ("gate", 4), ("slot", 4), ("pos", 16), ("cnt", 8), ("blk", 8), ("cum", 8), ("start", 8),
                       ("tmp", 16), ("job", MAXJOBS + 2)):
            rtc[_n] = (_c, _w)
            _c += _w
        assert _c <= T

        def R(name, i=0, n=None):
            at, w = rtc[name]
            return rt[:, at + i:at + (w if n is None else i + n)]

        def choice(name):
            return R(name).rearrange("p (t i) -> p i t", i=2)

        def jobs_of(eng):
            eng.wait_ge(sem("jobs_ready"), 1)
            return eng.value_load(jt[0:1, MAXJOBS:MAXJOBS + 1], min_val=1, max_val=MAXJOBS - 1)

        def last_job(eng):
            return eng.value_load(jt[0:1, MAXJOBS + 1:MAXJOBS + 2], min_val=0, max_val=MAXJOBS - 2)

        def hrows():
            return wide[:].rearrange("p (a b) t -> p a (b t)", a=TT)

        def pe_moe(pe, mm, turn):
            pe.wait_ge(sem("router_in"), 16)
            for k in range(KT):
                pe.wait_ge(sem("hT_ready"), 3 * KT + k + 1)
                for tt in range(TT):
                    ins = nc.tensor.matmul(bank[6][:, tt * NE:(tt + 1) * NE], hT[:, k, tt * P:(tt + 1) * P], router[:, k],
                                           start=k == tt == 0, stop=k == KT - 1, skip_group_check=True)
            ins.then_inc(sem("logits_ready"), 1)
            for b in range(4):
                for k in range(2):
                    for tt in range(TT):
                        turn(bank[b][:, tt * T + k * P:tt * T + (k + 1) * P], hT[:, 2 * b + k, tt * P:(tt + 1) * P],
                             sig="h_turned" if k and tt else None)
            pe.wait_ge(sem("sel_ready"), 1)
            mm(bank[7][:, 0:NE], cst("ups"), R("sel", 0, NE))
            mm(bank[7][:, NE:2 * NE], cst("ups"), R("sel", NE, NE), True, False)
            mm(bank[7][:, NE:2 * NE], cst("ones"), R("sel", 0, NE), False, True)
            mm(bank[7][:, 2 * NE:3 * NE], cst("ones"), R("sel", 0, NE), True, False)
            mm(bank[7][:, 2 * NE:3 * NE], cst("ones"), R("sel", NE, NE), False, True, "pos_ready")
            pe.wait_ge(sem("h_copied"), 4)

            def gather(j):
                pe.wait_ge(sem("sel_built"), j + 1)
                for half in range(2):
                    for d in range(4):
                        for tt in range(TT):
                            k = 4 * half + d
                            mm(bank[5 + half][:, d * C:(d + 1) * C], hrows()[:, tt, k * P:(k + 1) * P], sel[:, tt],
                               tt == 0, tt == 1, "gathered" if d == 3 and tt else None)

            def turn_gates(j):
                pe.wait_ge(sem("selg_built"), j + 1)
                for tt in range(TT):
                    turn(bank[7][:, tt * P:(tt + 1) * P], selg[:, tt], sig="gates_turned" if tt else None)

            def scatter(j):
                pe.wait_ge(sem("gates_copied"), j + 1)
                pe.wait_ge(sem("acc_copied"), 2 * j + 2)
                for b in range(4):
                    for k in range(2):
                        dt = 2 * b + k
                        mm(bank[SCATTER[b]][:, k * T:(k + 1) * T], yj[:, dt * P:(dt + 1) * P], pgt[:],
                           sig="scattered" if k else None)

            last = PAIRS_E - 1
            gather(0)
            zero_acc((2, 3))
            run = job(0)
            pe.wait_ge(sem("x_split"), x_before(1, 2) + 2)
            pe_up(pe, run, 0, 0, 0)
            pe_up(pe, run, 0, 0, 1)
            pe_steps(pe, run)
            n_jobs = jobs_of(pe)
            with pe.Fori(1, n_jobs) as j:
                run, nxt = job(j - 1), job(j)
                pe_turn_gated(pe, run, last)
                gather(j)
                turn_gates(j - 1)
                pe_down(pe, run, last, True)
                pe.wait_ge(sem("x_split"), x_before(1, 2) + 2 * j + 2)
                pe_up(pe, nxt, 0, 0, 0)
                pe_up(pe, nxt, 0, 0, 1)
                scatter(j - 1)
                pe.wait_ge(sem("scatter_added"), 4 * (j - 1) + 2)
                zero_acc((2, 3))
                pe_steps(pe, nxt)
            j = last_job(pe)
            run = job(j)
            pe_turn_gated(pe, run, last)
            turn_gates(j)
            pe_down(pe, run, last, True)
            scatter(j)

        def act_moe(act, copy, f, square):
            for b in range(4):
                act.wait_ge(sem("h_turned"), b + 1)
                copy(hrows()[:, :, b * T:(b + 1) * T], bank[b][:].rearrange("p (a t) -> p a t", a=TT), "h_copied")
            act.wait_ge(sem("gate_logit"), 1)
            f(R("e"), R("e"), ACT.Exp, "gate_exp")

            def gathered(j):
                for half in range(2):
                    act.wait_ge(sem("gathered"), 2 * j + half + 1)
                    nc.scalar.activation(xh[:, 4 * half:4 * half + 4, 0:C],
                                         bank[5 + half][:].rearrange("p (k c) -> p k c", c=C), ACT.Copy
                                         ).then_inc(sem("x_high"), 1)

            def gates(j):
                act.wait_ge(sem("gates_turned"), j + 1)
                nc.scalar.copy(pgt[:], bank[7][:, 0:T]).then_inc(sem("gates_copied"), 1)

            def acc(j):
                act.wait_ge(sem("stage_used"), job(j).down(0, True)[0] + 1)
                for half in range(2):
                    nc.scalar.copy(yj[:, half * 512:(half + 1) * 512], bank[2 + half][:]).then_inc(sem("acc_copied"), 1)

            last = PAIRS_E - 1
            gathered(0)
            act_start(act, job(0))
            act_steps(act, job(0))
            n_jobs = jobs_of(act)
            with act.Fori(1, n_jobs) as j:
                run, nxt = job(j - 1), job(j)
                up, down = act_split(act, nxt)
                act_end_a(act, run)
                up(0, 0, 0, 0)
                act_gated_high(act, run, last)
                up(0, 0, 0, 1)
                gathered(j)
                gates(j - 1)
                acc(j - 1)
                up(1, 0, 1, 0)
                act_start(act, nxt)
                act_steps(act, nxt)
            j = last_job(act)
            run = job(j)
            act_end_a(act, run)
            act_gated_high(act, run, last)
            gates(j)
            acc(j)
            for b in range(4):
                act.wait_ge(sem("scatter_added"), 4 * j + b + 1)
                square(2 * DEPTH, b)

        def dve_moe(dve, settle, tt_, ts, stt, recip):
            iota8 = cst("iota")[:, 0:NE]
            dve.wait_ge(sem("logits_ready"), 1)
            settle(nc.vector.tensor_copy(R("logit"), bank[6][:, 0:TT * NE]))
            for tt in range(TT):
                settle(nc.vector.max(R("top", tt * 8, 8), R("logit", tt * NE, NE)))
                settle(nc.vector.max_index(idx[:, tt * 8:(tt + 1) * 8], R("top", tt * 8, 8), R("logit", tt * NE, NE)))
            settle(nc.vector.tensor_copy(R("idx"), idx[:]))
            for tt in range(TT):
                ts(R("oh1", tt * NE, NE), iota8, R("idx", tt * 8, 1), None, ALU.is_equal)
                ts(R("oh2", tt * NE, NE), iota8, R("idx", tt * 8 + 1, 1), None, ALU.is_equal)
                tt_(R("e", tt, 1), R("top", tt * 8 + 1, 1), R("top", tt * 8, 1), ALU.subtract,
                    "gate_logit" if tt else "dve_chain")
            tt_(R("sel"), R("oh1"), R("oh2"), ALU.add, "sel_ready")
            def gates():
                dve.wait_ge(sem("gate_exp"), 1)
                ts(choice("gate")[:, 0], R("e"), 1.0, None, ALU.add)
                recip(choice("gate")[:, 0], choice("gate")[:, 0])
                tt_(choice("gate")[:, 1], choice("gate")[:, 0], R("e"), ALU.mult, "gates_ready")

            dve.wait_ge(sem("pos_ready"), 1)
            pos, cnt = rtc["pos"][0], rtc["cnt"][0]
            assert cnt == pos + 2 * NE
            settle(nc.vector.tensor_copy(rt[:, pos:cnt + NE], bank[7][:, 0:3 * NE]))
            ts(R("blk", 0, 1), R("cnt", 0, 1), -1.0, None, ALU.is_gt)
            ts(R("blk", 1, NE - 1), R("cnt", 1, NE - 1), 0.0, None, ALU.is_gt)
            for b in range(1, -(-T // C)):
                stt(R("blk"), R("cnt"), float(b * C), R("blk"), ALU.is_gt, ALU.add)
            settle(nc.vector.tensor_tensor_scan(R("cum"), cst("ones")[:, 0:NE], R("blk"), 0.0, ALU.mult, ALU.add))
            tt_(R("start"), R("cum"), R("blk"), ALU.subtract)
            ts(R("start"), R("start"), float(C), None, ALU.mult)

            def by_tile(name):
                return R(name).rearrange("p (t e) -> p t e", e=NE)

            tt_(by_tile("pos"), by_tile("pos"), R("start").unsqueeze(1).broadcast_to([P, TT, NE]), ALU.add)
            for i, oh in enumerate(("oh1", "oh2")):
                tt_(R("tmp"), R(oh), R("pos"), ALU.mult)
                settle(nc.vector.tensor_reduce(choice("slot")[:, i], by_tile("tmp"), AX.X, ALU.add))

            def gathered(j):
                for half in range(2):
                    dve.wait_ge(sem("x_high"), x_before(1, 2) + 2 * j + half + 1)
                    hv = slice(4 * half, 4 * half + 4)
                    nc.vector.tensor_tensor(xl[:, hv, 0:C], bank[5 + half][:].rearrange("p (k c) -> p k c", c=C),
                                            xh[:, hv, 0:C].bitcast(F32), ALU.subtract).then_inc(sem("x_split"), 1)

            def scattered(j):
                for b in range(4):
                    dve.wait_ge(sem("scattered"), 4 * j + b + 1)
                    x = xT[:, 2 * b:2 * b + 2].rearrange("p a t -> p (a t)")
                    nc.vector.tensor_tensor(x, x, bank[SCATTER[b]][:], ALU.add).then_inc(sem("scatter_added"), 1)
                dve.wait_ge(sem("scatter_added"), 4 * j + 4)

            def compare_slots(j):
                wait(dve, "slots_compared", 3 * j)
                wait(dve, "selg_built", j)
                for i in range(2):
                    nc.vector.tensor_tensor(hit[:, i], cst("iota").unsqueeze(1).broadcast_to([P, TT, C]),
                                            choice("slot")[:, i].unsqueeze(2).broadcast_to([P, TT, C]), ALU.is_equal
                                            ).then_inc(sem("slots_compared"), 1)
                dve.wait_ge(sem("slots_compared"), 3 * j + 2)
                nc.vector.tensor_scalar(R("slot"), R("slot"), -float(C), None, ALU.add).then_inc(sem("slots_compared"), 1)

            last = PAIRS_E - 1
            compare_slots(0)
            gates()
            iota16 = cst("iota")[:, 0:MAXJOBS]
            ts(R("job", 0, MAXJOBS), iota16, R("cum", 0, 1), None, ALU.is_ge)
            for e in range(1, NE):
                stt(R("job", 0, MAXJOBS), iota16, R("cum", e, 1), R("job", 0, MAXJOBS), ALU.is_ge, ALU.add)
            settle(nc.vector.tensor_copy(R("job", MAXJOBS, 1), R("cum", NE - 1, 1)))
            ts(R("job", MAXJOBS + 1, 1), R("cum", NE - 1, 1), -1.0, None, ALU.add)
            settle(nc.vector.tensor_copy(jt[:, 0:MAXJOBS + 2], R("job")), "jobs_ready")
            gathered(0)
            dve_start(dve, job(0))
            compare_slots(1)
            dve_steps(dve, job(0))
            n_jobs = jobs_of(dve)
            with dve.Fori(1, n_jobs) as j:
                run, nxt = job(j - 1), job(j)
                up, down = splitter(dve, split_low, nxt)
                dve_end_a(dve, run)
                up(0, 0, 0, 0)
                dve_gated_low(dve, run, last)
                up(0, 0, 0, 1)
                gathered(j)
                up(1, 0, 1, 0)
                up(1, 0, 1, 1)
                dve_gate(dve, nxt, 0, 0)
                scattered(j - 1)
                down(0, 0, 0)
                compare_slots(j + 1)
                dve_steps(dve, nxt)
            j = last_job(dve)
            run = job(j)
            dve_end_a(dve, run)
            dve_gated_low(dve, run, last)
            scattered(j)
        def pool_moe(pool):
            def job_matrices(j):
                pool.wait_ge(sem("slots_compared"), 3 * j + 2)
                wait(pool, "gathered", 2 * j)
                nc.gpsimd.tensor_tensor(sel[:], hit[:, 0], hit[:, 1], ALU.add).then_inc(sem("sel_built"), 1)
                wait(pool, "gates_turned", j)
                if isinstance(j, int):
                    pool.wait_ge(sem("gates_ready"), 1)
                for i in range(2):
                    nc.gpsimd.tensor_tensor((selg, selt)[i][:], hit[:, i],
                                            choice("gate")[:, i].unsqueeze(2).broadcast_to([P, TT, C]), ALU.mult
                                            ).then_inc(sem("gates_chain"), 1)
                pool.wait_ge(sem("gates_chain"), 2 * j + 2)
                nc.gpsimd.tensor_tensor(selg[:], selg[:], selt[:], ALU.add).then_inc(sem("selg_built"), 1)

            job_matrices(0)
            n_jobs = jobs_of(pool)
            with pool.Fori(1, n_jobs) as j:
                job_matrices(j)

        @block.sync
        def _(sp):
            def load(slot, dst, src):
                sp.dma_start(dst, src).then_inc(sem(f"w_ready{slot}"), 16)

            def columns(slot, w, at, n):
                load(slot, ring[:, slot, :, 0:n], w[:, at:at + n].rearrange("(k p) n -> p k n", p=P))

            def mixer_unit(layer, u):
                if u < NU:
                    columns(u % RING_M, A["w_in"][layer], UNITS[u][0], UNITS[u][1])
                else:
                    columns(u % RING_M, A["w_out"][layer], (u - NU) * T, T)

            def rows(slot, w, at):
                load(slot, ring[:, slot].rearrange("p (a b) t -> p a (b t)", a=2),
                     w[at:at + 2 * P, :].rearrange("(a p) d -> p a d", p=P))

            def sp_ffn(run, w1, w3, w2, row13, row2, after_mixer):
                def free(slot, first, n):
                    if first and after_mixer:
                        last = last_unit(slot) if slot < RING_M else NU
                        sp.wait_ge(sem("unit_used"), (after_mixer - 1) * LU + last + 1)
                    else:
                        sp.wait_ge(sem("w_split"), run.stages + n)

                def up(m, par, first, n):
                    for slot, w in zip(UP[par], (w1, w3)):
                        free(slot, first, n)
                        load(slot, slot_of(slot), w[bass.ds(row13, D), bass.ds(m * T, T)].rearrange("(k p) n -> p k n", p=P))

                def down(m, par, first, n):
                    free(DOWN[par], first, n)
                    load(DOWN[par], slot_of(DOWN[par]).rearrange("p (a b) t -> p a (b t)", a=2),
                         w2[bass.ds(row2 + m * T, T), :].rearrange("(a p) d -> p a d", p=P))

                up(0, 0, True, -5)
                up(1, 1, True, -2)
                down(0, 0, True, -1)
                up(2, 0, False, 2)
                down(1, 1, True, 0)
                with sp.Fori(0, (run.pairs - 3) // 2) as i:
                    for par in (1, 0):
                        m = 2 * i + (3 if par else 4)
                        up(m, par, False, 3 * m - 5)
                        down(m - 1, 1 - par, False, 3 * m - 4)
                if run.pairs % 2 == 0:
                    m = run.pairs - 1
                    up(m, 1, False, 3 * m - 5)
                    down(m - 1, 0, False, 3 * m - 4)
                down(run.pairs - 1, (run.pairs - 1) % 2, False, 3 * run.pairs - 4)

            sp.dma_start(const[:, 0:P], A["const"][:, 0:P]).then_inc(sem("x_in"), 16)
            sp.dma_start(proj[:, 0:KT].rearrange("p (a b) t -> p a (b t)", a=TT),
                         A["x"][0].rearrange("(a p) d -> p a d", p=P)).then_inc(sem("x_in"), 16)
            sp.dma_start(const[:, P:NCONST], A["const"][:, P:NCONST]).then_inc(sem("const_in"), 16)
            for layer in range(DEPTH):
                for u in range(LU):
                    slot = u % RING_M
                    if u >= RING_M:
                        sp.wait_ge(sem("unit_used"), layer * LU + u - RING_M + 1)
                    elif layer:
                        sp.wait_ge(sem("w_split"), dense.last_split(slot))
                    mixer_unit(layer, u)
                if layer == 0:
                    sp_ffn(dense, A["ffn_w1"][0], A["ffn_w3"][0], A["ffn_w2"][0], 0, 0, 1)

            w1, w3 = (A[n][0].rearrange("e d f -> (e d) f") for n in ("moe_w1", "moe_w3"))
            w2 = A["moe_w2"][0].rearrange("e f d -> (e f) d")
            sp_ffn(job(0), w1, w3, w2, 0, 0, 2)
            n_jobs = jobs_of(sp)
            with sp.Fori(1, n_jobs) as j:
                e = sp.value_load(jt[0:1, bass.ds(j, 1)], min_val=0, max_val=NE - 1)
                sp_ffn(job(j), w1, w3, w2, e * D, e * FE, 0)
            sp.wait_ge(sem("out_ready"), KT // 2)
            sp.dma_start(out[0].rearrange("(a p) d -> p a d", p=P),
                         wide[:].rearrange("p (a b) t -> p a (b t)", a=TT)).then_inc(sem("out_stored"), 16)
            sp.wait_ge(sem("out_stored"), 16)

        @block.gpsimd
        def _(pool):
            settle = own(pool, "pool_chain")
            pool.dma_start(posi, A["positions"].broadcast_to([P, T])).then_inc(sem("pos_in"), 16)
            pool.dma_start(lora[0:HD], A["rwkv_w2"].rearrange("l r g -> r l g")).then_inc(sem("lora_in"), 16)
            pool.dma_start(lora[HD:P], A["rwkv_a2"].rearrange("l r g -> r l g")).then_inc(sem("lora_in"), 16)
            pool.dma_start(g2[:], A["rwkv_g2"].rearrange("l r g -> r l g")).then_inc(sem("lora_in"), 16)
            pool.dma_start(router[:], A["moe_router"][0].rearrange("(k p) e -> p k e", p=P)
                           ).then_inc(sem("router_in"), 16)

            def mla_weights(layer):
                pool.dma_start(wuq[:], A["mla_w_uq"][layer].rearrange("(k p) n -> p k n", p=P)
                               ).then_inc(sem("mla_w_in"), 16)
                pool.dma_start(wukv[:].rearrange("p h n -> p (h n)"), A["mla_w_ukv"][layer]
                               ).then_inc(sem("mla_w_in"), 16)

            mla_weights(0)
            pool.wait_ge(sem("omlb_ready"), 1)
            for layer in range(DEPTH):
                if layer:
                    pool.wait_ge(sem("mla_v_ready"), layer)
                    mla_weights(layer)
                pool.wait_ge(sem("hsig_ready"), 3 * layer + 3)
                fq = proj[:, J_HQ:J_HQ + 2].rearrange("p a t -> p (a t)")
                ff = proj[:, J_HF:J_HF + 2].rearrange("p a t -> p (a t)")
                fg = proj[:, J_HG:J_HG + 2].rearrange("p a t -> p (a t)")
                flat = hs[:].rearrange("p a b -> p (a b)")
                sf, sq = flat[:, 0:2 * T], flat[:, 2 * T:4 * T]
                sgt = hx[:].rearrange("p a b -> p (a b)")
                settle(nc.gpsimd.tensor_tensor(fq, fq, sq, ALU.mult))
                settle(nc.gpsimd.tensor_tensor(fg, fg, sgt, ALU.mult))
                for j in range(GT):
                    c = layer * GT + j
                    settle(nc.gpsimd.tensor_scalar(ff[:, j * T:(j + 1) * T], sf[:, j * T:(j + 1) * T],
                                                   omlb[:, c:c + 1], lbc[:, c:c + 1], ALU.mult, ALU.add))
                settle(nc.gpsimd.tensor_scalar(hk[:, 0], ff, -1.0, 1.0, ALU.mult, ALU.add), "hgrn_level")
                ends = ff
                for l in range(LEVELS + 1):
                    n = 1 << l
                    new, old = l % 2, (l + 1) % 2
                    if l == 0:
                        settle(nc.gpsimd.tensor_tensor(hq[:, 0], fq, ff, ALU.mult), "hgrn_level")
                        continue
                    half = n // 2
                    nb = GT * T // n
                    qo = hq[:, old].rearrange("p (b h i) -> p b h i", h=2, i=half)
                    qn = hq[:, new].rearrange("p (b h i) -> p b h i", h=2, i=half)
                    ko = hk[:, old].rearrange("p (b h i) -> p b h i", h=2, i=half)
                    kn = hk[:, new].rearrange("p (b h i) -> p b h i", h=2, i=half)
                    ev = ends.rearrange("p (b h) -> p b h", h=2)
                    if l >= 2:
                        pool.wait_ge(sem("hgrn_scored"), layer * 16 + 2 * l)
                    else:
                        pool.wait_ge(sem("hgrn_scored"), layer * 16 + 2)
                    nxt = hend[:, GT * T - 2 * nb:GT * T - nb]
                    e1 = ev[:, :, 0:1].broadcast_to([P, nb, half])
                    e2 = ev[:, :, 1:2].broadcast_to([P, nb, half])
                    settle(nc.gpsimd.tensor_tensor(qn[:, :, 1], qo[:, :, 1], e1, ALU.mult))
                    settle(nc.gpsimd.tensor_copy(qn[:, :, 0], qo[:, :, 0]))
                    settle(nc.gpsimd.tensor_tensor(kn[:, :, 0], ko[:, :, 0], e2, ALU.mult))
                    settle(nc.gpsimd.tensor_tensor(nxt, ev[:, :, 0], ev[:, :, 1], ALU.mult))
                    settle(nc.gpsimd.tensor_copy(kn[:, :, 1], ko[:, :, 1]), "hgrn_level")
                    ends = nxt
                pool.wait_ge(sem("chunk_masked"), 4 * layer + 1)
                for l in range(1, LEVELS):
                    for half in range(2):
                        if l > 1:
                            pool.wait_ge(sem("mx_ready"), 12 * layer + 2 * (l - 2) + half + 1)
                        hv = slice(4 * half, 4 * half + 4)
                        settle(nc.gpsimd.tensor_tensor(mtm[:, hv], atm[:, hv], over(lvl(l), 4), ALU.mult), "level_masked")
            pool_moe(pool)

        @block.tensor
        def _(pe):
            def mm(o, l, r, start=True, stop=True, sig=None):
                ins = nc.tensor.matmul(o, l, r, start=start, stop=stop)
                if sig:
                    ins.then_inc(sem(sig), 1)

            def turn(o, i, rows=P, sig=None):
                ins = nc.tensor.transpose(o, i, cst("id")[0:rows, 0:rows])
                if sig:
                    ins.then_inc(sem(sig), 1)

            def norm_part(n, q):
                pe.wait_ge(sem("sq_ready"), NO * n + q + 1)
                for k in (2 * q, 2 * q + 1):
                    mm(bank[SUMS[n]][:, 0:T], cst("ones"), wide[:, k], k == 0, k == KT - 1,
                       "ss_ready" if k == KT - 1 else None)

            def norm(n):
                for q in range(NO):
                    norm_part(n, q)

            pe.wait_ge(sem("x_in"), 32)
            xr = proj[:, 0:KT].rearrange("p (a b) t -> p a (b t)", a=TT)
            for b in range(4):
                for k in range(2):
                    for tt in range(TT):
                        turn(bank[b][:, k * T + tt * P:k * T + (tt + 1) * P],
                             xr[:, tt, (2 * b + k) * P:(2 * b + k + 1) * P],
                             sig="x_turned" if k == 1 and tt == TT - 1 else None)
            pe.wait_ge(sem("const_in"), 16)

            def unit(layer, u):
                slot, b = u % RING_M, u % 2
                _, cols, token_major = UNITS[u]
                if u >= 2:
                    pe.wait_ge(sem("unit_copied"), layer * NU + u - 1)
                for part in range(2):
                    if u == 0:
                        pe.wait_ge(sem("x_split"), x_before(layer, 0) + part + 1)
                    ins = pe_unit_half(pe, layer, u, part, bank[b], not token_major)
                    if part == 0:
                        ins.then_inc(sem("half_used"), 1)
                if u == NU - 1:
                    for k in range(KT):
                        ins = nc.tensor.matmul(bank[b][HD:UQ, T:2 * T], ring[:, slot, k, P:cols], hT[:, k],
                                               start=k == 0, stop=k == KT - 1)
                ins.then_inc(sem("unit_used"), 1)

            def rows(h):
                lo = HD * (h % 2)
                return lo, lo + HD, h // 2

            def mat(h, c):
                return 4 * (h % 2) + 2 * (h // 2) + c

            for layer in range(DEPTH):
                def nth(per, i=0):
                    return layer * per + i + 1

                norm(2 * layer)
                for u in range(8):
                    unit(layer, u)
                if layer == 0:
                    pe.wait_ge(sem("lora_in"), 48)
                pe.wait_ge(sem("tw_ready"), nth(2))
                for j in range(GT):
                    mm(bank[2][:, j * T:(j + 1) * T], lora[0:HD, layer, j * P:(j + 1) * P], tw[:],
                       sig="lora_ready" if j else None)
                for j in range(GT):
                    mm(bank[3][:, j * T:(j + 1) * T], lora[HD:P, layer, j * P:(j + 1) * P], sh[HD:P, 6],
                       sig="lora_ready" if j else None)
                pe.wait_ge(sem("tw_ready"), nth(2, 1))
                for j in range(GT):
                    mm(bank[4][:, j * T:(j + 1) * T], g2[:, layer, j * P:(j + 1) * P], sg[:],
                       sig="lora_ready" if j else None)
                unit(layer, 8)
                pe.wait_ge(sem("kksq_ready"), nth(1))
                mm(bank[5][:], cst("blk"), diff[:].rearrange("p a t -> p (a t)"), sig="kkss_ready")
                def hgrn_scores(e):
                    pe.wait_ge(sem("hgrn_level"), nth(9, 0 if e == 0 else e))
                    for half in range(2):
                        if e or layer:
                            pe.wait_ge(sem("hgrn_masked"), layer * 16 + 2 * e + half - 1)
                        for m in range(4):
                            h, c = 2 * (m // 2) + half, m % 2
                            lo, hi, j = rows(h)
                            s = slice(j * T + c * P, j * T + (c + 1) * P)
                            src = hk[lo:hi, 0 if e == 0 else (e - 1) % 2, s]
                            qry = (proj[lo:hi, J_HQ + j, c * P:(c + 1) * P] if e == 0
                                   else hq[lo:hi, (e - 1) % 2, s])
                            mm(bank[6 + half][:, m * P:(m + 1) * P], src, qry, sig="hgrn_scored" if m == 3 else None)

                hgrn_scores(0)
                for u, levels in ((9, (1, 2)), (10, (3, 4)), (11, (5, 6)), (12, (7,))):
                    unit(layer, u)
                    for e in levels:
                        hgrn_scores(e)
                    if u == 9:
                        pe.wait_ge(sem("unit_copied"), nth(NU, 9))
                        pe.wait_ge(sem("sig_ready"), nth(5, 4))
                        for i, at in enumerate((J_DQ, J_DK)):
                            mm(bank[2 + i][:], cst("r64"), proj[:, at:at + 2].rearrange("p a t -> p (a t)"),
                               sig="partner_ready")
                pe.wait_ge(sem("hgrn_level"), nth(9, 8))
                pe.wait_ge(sem("hgrn_masked"), nth(16, 14))
                pe.wait_ge(sem("hgrn_masked"), nth(16, 15))
                for h in range(NH):
                    lo, hi, j = rows(h)
                    mm(bank[6 + h % 2][:, j * P:(j + 1) * P], hk[lo:hi, 1, j * T:j * T + P],
                       hq[lo:hi, 1, j * T + P:j * T + T], sig="hgrn_crossed" if h == NH - 1 else None)
                pe.wait_ge(sem("rkk_ready"), nth(1))
                mm(bank[5][:], cst("blk"), diff[:].rearrange("p a t -> p (a t)"), sig="bonus_ready")
                pe.wait_ge(sem("rope_ready"), nth(2, 1))
                for c in range(TT):
                    for j in range(GT):
                        turn(bank[2][:, c * G + j * P:c * G + (j + 1) * P], sh[:, J_V + j, c * P:(c + 1) * P],
                             sig="tok_turned" if c and j else None)
                pe.wait_ge(sem("chunks_ready"), nth(1))
                for i, a in enumerate((bet, kha)):
                    for j in range(GT):
                        turn(bank[3][:, i * G + j * P:i * G + (j + 1) * P], a[:, j, 0:P],
                             sig="tok_turned" if i and j else None)
                for n, (a, b, bk) in enumerate(((bet, kap, 4), (kha, kap, 6), (bet, rha, 4), (kha, rha, 6))):
                    if n == 3:
                        pe.wait_ge(sem("latsq_ready"), nth(1))
                        sq = ssb[:].rearrange("p a b -> p (a b)")
                        mm(bank[1][:, 0:T], cst("ones"), sq[:, 0:T], True, False)
                        mm(bank[1][:, 0:T], cst("ones"), sq[:, T:2 * T], False, True)
                        mm(bank[1][:, T:2 * T], cst("ones"), sq[:, 2 * T:3 * T], sig="latss_ready")
                        for h in range(NH):
                            lo, hi, j = rows(h)
                            it = [proj[:, J_HI + c, h * HD:(h + 1) * HD] for c in range(TT)]
                            mm(bank[0][lo:hi, j * T:j * T + P], it[0], hs[:, mat(h, 0)])
                            mm(bank[0][lo:hi, j * T + P:j * T + T], it[0], hx[:, h], True, False)
                            mm(bank[0][lo:hi, j * T + P:j * T + T], it[1], hs[:, mat(h, 1)], False, True,
                               "ho_ready" if h == NH - 1 else None)
                    if n == 0:
                        pe.wait_ge(sem("bonus_used"), nth(1))
                    elif n == 1:
                        pe.wait_ge(sem("hgrn_masked"), nth(16, 15))
                        pe.wait_ge(sem("hx_copied"), nth(1))
                    else:
                        pe.wait_ge(sem("chunk_masked"), nth(4, n - 2))
                    for m in range(NM):
                        h, c = 2 * (m // 2 % 2) + m // 4, m % 2
                        lo, hi, j = rows(h)
                        mm(bank[bk + m // 4][:, m % 4 * P:(m % 4 + 1) * P], a[lo:hi, j, c * P:(c + 1) * P],
                           b[lo:hi, j, c * P:(c + 1) * P], sig="chunk_ready" if m == NM - 1 else None)
                pe.wait_ge(sem("hosq_ready"), nth(1))
                mm(bank[0][:], cst("blk"), pts[:].rearrange("p a b -> p (a b)")[:, 0:2 * T], sig="hoss_ready")

                def mla_step(step):
                    if step == 1:
                        pe.wait_ge(sem("hoss_used"), nth(1))
                        pe.wait_ge(sem("lat_ready"), nth(3, 2))
                        pe.wait_ge(sem("mla_w_in"), 32 * (layer + 1))
                        for h in range(NH):
                            for k in range(2):
                                mm(bank[h // 2][0:UQ, h % 2 * T:(h % 2 + 1) * T], wuq[:, k, h * UQ:(h + 1) * UQ],
                                   proj[:, J_CQ + k], k == 0, k == 1, "mlaq_ready" if k and h % 2 else None)
                    if step == 2:
                        for half in range(2):
                            pe.wait_ge(sem("mlaq_copied"), nth(2, half))
                            mm(bank[half][0:UQ, :], cst("r96")[0:UQ, :],
                               qf[:, 2 * half:2 * half + 2].rearrange("p a t -> p (a t)"), sig="q_partner")
                    if step == 4:
                        pe.wait_ge(sem("qf_ready"), nth(1))
                        for h in range(NH):
                            mm(bank[h // 2][0:HD, h % 2 * T:(h % 2 + 1) * T], wukv[:, h, 0:HD], proj[:, J_CKV],
                               sig="mlak_ready" if h % 2 else None)
                    if step == 5:
                        pe.wait_ge(sem("mlakv_copied"), nth(3, 1))
                        for tt in range(TT):
                            mm(bank[0][:, tt * G:(tt + 1) * G], proj[:, J_CKV, tt * P:(tt + 1) * P], wukv[:, :, HD:2 * HD],
                               sig="mla_v_ready" if tt else None)
                        mm(bank[1][HD:UQ, 0:T], cst("r96")[HD:UQ, HD:UQ], proj[HD:UQ, J_KR], sig="kr_partner")

                pe.wait_ge(sem("xit_ready"), nth(2 * LEVELS, 1))
                pe.wait_ge(sem("tok_copied"), nth(2, 1))
                for half in range(2):
                    for m in range(4):
                        turn(bank[2 + half][:, m * P:(m + 1) * P], xit[:, 4 * half + m], sig="xt_turned" if m == 3 else None)
                for l in range(1, LEVELS):
                    last = l == LEVELS - 1
                    for half in range(2):
                        pe.wait_ge(sem("level_masked"), nth(2 * (LEVELS - 1), 2 * (l - 1) + half))
                        pe.wait_ge(sem("xin_ready"), nth(2 * (LEVELS - 1), 2 * (l - 1) + half))
                        for m in range(4):
                            mm(bank[2 + half][:, m * P:(m + 1) * P], mtm[:, 4 * half + m], xin[:, 4 * half + m],
                               sig="mx_ready" if m == 3 else None)
                    for half in range(2):
                        pe.wait_ge(sem("pin_ready"), nth(2 * (LEVELS - 1), 2 * (l - 1) + half))
                        if l == 1 and half == 0:
                            pe.wait_ge(sem("chunk_masked"), nth(4, 3))
                        pe.wait_ge(sem("xit_ready"), nth(2 * LEVELS, 2 * (l - 1) + half))
                        if not last:
                            for m in range(4):
                                mm(bank[4 + half][:, m * P:(m + 1) * P], xit[:, 4 * half + m], pin[:, 4 * half + m],
                                   sig="xmx_ready" if m == 3 else None)
                        for m in range(4):
                            mm(bank[6 + half][:, m * P:(m + 1) * P], pin[:, 4 * half + m], xit[:, 4 * half + m],
                               sig="xmx_t_ready" if m == 3 else None)
                    mla_step(l)
                SCORES, TURNED, ATTENDED = (0, 1, 7), (6, 3), (5, 4)

                def attend_scores(n):
                    h = n % NH
                    lo, hi, j = rows(h)
                    if n < NH:
                        query, key = proj[lo:hi, J_DQ + j], proj[lo:hi, J_DK + j]
                    else:
                        query, key = qf[:, h], kf[:, h]
                    if n == 0:
                        pe.wait_ge(sem("mlakv_copied"), nth(3, 2))
                        pe.wait_ge(sem("rope_ready"), nth(2, 1))
                    if n == 1:
                        pe.wait_ge(sem("kf_ready"), nth(1))
                    if n >= 3:
                        pe.wait_ge(sem("scores_used"), nth(2 * NH, n - 3))
                    o = bank[SCORES[n % 3]]
                    mm(o[:, 0:P], query[:, 0:P], key[:, 0:P])
                    mm(o[:, P:3 * P], query[:, P:T], key[:, 0:T], sig="scores_ready")

                def attend(n):
                    kind, h = n // NH, n % NH
                    lo, hi, j = rows(h)
                    b = n % 3
                    pe.wait_ge(sem("probs_ready"), nth(2 * NH, n))
                    if n >= 2:
                        pe.wait_ge(sem("pts_ready"), nth(2 * NH, n - 2))
                    o = bank[TURNED[n % 2]]
                    turn(o[:, 0:P], ssb[:, b, 0:P])
                    turn(o[:, P:T], ssb[:, b, P:2 * P])
                    turn(o[:, T:3 * P], ssb[:, b, 2 * P:3 * P], sig="pts_turned")
                    pe.wait_ge(sem("pts_ready"), nth(2 * NH, n))
                    o = bank[ATTENDED[kind]]
                    v = (proj[:, J_DV:J_DV + 2], mtok)[kind][:, :, h * HD:(h + 1) * HD]
                    mm(o[lo:hi, j * T:(j + 1) * T], v[:, 0], pts[:, n % 2, 0:T], True, False)
                    mm(o[lo:hi, j * T + P:(j + 1) * T], v[:, 1], pts[:, n % 2, T:3 * P], False, True, "attended")

                pe.wait_ge(sem("xit_ready"), nth(2 * LEVELS, 2 * LEVELS - 1))
                for c in range(TT):
                    for h in range(NH):
                        lo, hi, j = rows(h)
                        o = bank[2 + h % 2][:, j * HD:(j + 1) * HD]
                        if c:
                            if h == 0:
                                pe.wait_ge(sem("state_ready"), nth(1))
                            mm(o, kap[lo:hi, j, P:T], st[lo:hi, j], True, False)
                        mm(o, btm[:, mat(h, c)], vtok[:, c, h * HD:(h + 1) * HD], c == 0, True,
                           "r_ready" if h == NH - 1 else None)
                    if c == 0:
                        attend_scores(0)
                    pe.wait_ge(sem("rsol_ready"), nth(2, c))
                    for h in range(NH):
                        mm(bank[6][:, h * HD:(h + 1) * HD], xit[:, mat(h, c)], rsol[:, h],
                           sig="u_ready" if h == NH - 1 else None)
                    if c == 0:
                        attend_scores(1)
                    pe.wait_ge(sem("usol_ready"), nth(2, c))
                    if c == 0:
                        for h in range(NH):
                            lo, hi, j = rows(h)
                            o = bank[4][lo:hi, j * HD:(j + 1) * HD]
                            mm(o, btok[:, 0, h * HD:(h + 1) * HD], usol[:, 0, h], True, False)
                            mm(o, btok[:, 1, h * HD:(h + 1) * HD], vtok[:, 0, h * HD:(h + 1) * HD], False, True,
                               "state_summed" if h == NH - 1 else None)
                        attend_scores(2)
                for h in range(NH):
                    lo, hi, j = rows(h)
                    for c in range(TT):
                        o = bank[5 - h % 2][lo:hi, j * T + c * P:j * T + (c + 1) * P]
                        if c:
                            mm(o, st[lo:hi, j], rha[lo:hi, j, P:T], True, False)
                        mm(o, usol[:, c, h], ctm[:, mat(h, c)], c == 0, False)
                        mm(o, vtok[:, c, h * HD:(h + 1) * HD], dtm[:, mat(h, c)], False, True,
                           "y_ready" if c and h == NH - 1 else None)
                pe.wait_ge(sem("ysb_ready"), nth(1))
                mm(bank[2][:], cst("blk"), ysb[:].rearrange("p a t -> p (a t)"), sig="mean_ready")
                for n in range(2 * NH):
                    attend(n)
                    if n == 0:
                        pe.wait_ge(sem("yc_ready"), nth(1))
                        pe.wait_ge(sem("ysq_ready"), nth(1))
                        mm(bank[2][:], cst("blk"), mtm[:, 0:4].rearrange("p a t -> p (a t)"), sig="var_ready")
                    if n + 3 < 2 * NH:
                        attend_scores(n + 3)
                for name, n in (("ya_ready", 2), ("yd_ready", 2)):
                    pe.wait_ge(sem(name), n * (layer + 1))
                pe.wait_ge(sem("attn_copied"), nth(2, 1))
                for u in range(NU, LU):
                    for part in range(2):
                        if u == NU:
                            pe.wait_ge(sem("x_split"), x_before(layer, 1) + part + 1)
                        pe_unit_half(pe, layer, u, part, bank[2 + u - NU], True).then_inc(
                            sem(("half_used", "unit_used")[part]), 1)
                    if u > NU:
                        norm_part(2 * layer + 1, u - NU - 1)
                norm_part(2 * layer + 1, NO - 1)
                if layer == 0:
                    pe_ffn_dense(pe)
            pe_moe(pe, mm, turn)
            norm(2 * DEPTH)
            for k in range(KT):
                pe.wait_ge(sem("hT_ready"), 2 * DEPTH * KT + k + 1)
                for tt in range(TT):
                    turn(bank[k // 2][:, tt * T + k % 2 * P:tt * T + (k % 2 + 1) * P], hT[:, k, tt * P:(tt + 1) * P],
                         sig="out_turned" if k % 2 and tt else None)

        @block.scalar
        def _(act):
            settle = own(act, "act_chain")

            def f(o, i, func, sig="act_chain", scale=1.0, bias=None, accum=None):
                if bias is None and func != ACT.Copy:
                    bias = cst("zero", o.shape[0])
                kw = {"scale": scale}
                if bias is not None:
                    kw["bias"] = bias
                if accum is not None:
                    kw["accum_out"] = accum
                settle(nc.scalar.activation(o, i, func, **kw), sig)

            def copy(o, i, sig="act_chain"):
                settle(nc.scalar.copy(o, i), sig)

            def flat(a):
                return a.rearrange("p a t -> p (a t)")

            def square(n, q):
                act_sq = slice(2 * q, 2 * q + 2)
                f(flat(wide[:, act_sq]), flat(xT[:, act_sq]), ACT.Square, "sq_ready")

            def root(n):
                f(tiny[:], cst("zero"), ACT.Sqrt)
                act.wait_ge(sem("ss_ready"), n + 1)
                f(rstd[:, 0], bank[SUMS[n]][:, 0:T], ACT.Sqrt, "std_ready", 1.0 / D, cst("eps_rms"))

            def norm(n, beside):
                if n:
                    for q in range(NO):
                        act.wait_ge(sem("xT_ready"), NO * (n - 1) + q + 1)
                        square(n, q)
                beside()
                root(n)

            act.dma_start(par[:], A["par"]).then_inc(sem("par_in"), 16)
            for b in range(4):
                act.wait_ge(sem("x_turned"), b + 1)
                copy(flat(xT[:, 2 * b:2 * b + 2]), bank[b][:], "x_copied")
                if b == 0:
                    act.wait_ge(sem("const_in"), 16)
                square(0, b)
            act.wait_ge(sem("par_in"), 16)

            for layer in range(DEPTH):
                def nth(per, i=0):
                    return layer * per + i + 1

                norm(2 * layer, lambda: [act_unit_split(act, layer, 0, part) for part in range(2)])

                def unit(u):
                    if u < NU - 1:
                        for part in range(2):
                            act_unit_split(act, layer, u + 1, part)
                    at = [J_R, J_K, J_V, J_X, J_HQ, J_HF, J_HI, J_HG, J_DQ, J_DK, J_DV, J_CQ, J_CKV][u]
                    b = bank[u % 2]
                    act.wait_ge(sem("unit_used"), layer * LU + u + 1)
                    if u < NU - 1:
                        copy(flat(proj[:, at:at + 2]), b[:], "unit_copied")
                    else:
                        copy(proj[:, at], b[:, 0:T])
                        copy(proj[HD:UQ, J_KR], b[HD:UQ, T:2 * T], "unit_copied")

                act_split_x(act, 2 * layer)
                for u in range(6):
                    unit(u)
                if layer == 0:
                    act.wait_ge(sem("lbd_ready"), 1)
                    f(lbc[:, GT:2 * GT], lbc[:, GT:2 * GT], ACT.Sigmoid, "lb_ready")
                act.wait_ge(sem("shifted"), nth(8, 6))
                f(tw[:], sh[0:HD, 6], ACT.Tanh, "tw_ready")
                act.wait_ge(sem("shifted"), nth(8, 7))
                f(sg[:], sh[:, 7], ACT.Sigmoid, "tw_ready")
                unit(6)
                unit(7)
                hflat = hs[:].rearrange("p a b -> p (a b)")
                f(hflat[:, 0:2 * T], flat(proj[:, J_HF:J_HF + 2]), ACT.Sigmoid, "hsig_ready")
                f(hflat[:, 2 * T:4 * T], flat(proj[:, J_HQ:J_HQ + 2]), ACT.Sigmoid, "hsig_ready")
                f(hx[:].rearrange("p a b -> p (a b)"), flat(proj[:, J_HG:J_HG + 2]), ACT.Sigmoid, "hsig_ready")
                for i, name in enumerate(("rwkv_w0", "rwkv_a0")):
                    act.wait_ge(sem("lora_ready"), nth(3, i))
                    for j in range(GT):
                        f(rw[:, (SW, SA)[i], j], bank[2 + i][:, j * T:(j + 1) * T], ACT.Sigmoid, "sig_ready",
                          bias=prm(name, layer, j))
                act.wait_ge(sem("lora_ready"), nth(3, 2))
                copy(flat(rw[:, GG]), bank[4][:], "sig_ready")
                act.wait_ge(sem("kkr_ready"), nth(1))
                f(flat(diff[:]), flat(rw[:, KK]), ACT.Square, "kksq_ready")
                unit(8)
                act.wait_ge(sem("kkss_ready"), nth(1))
                f(flat(rw[:, BN]), bank[5][:], ACT.Sqrt, "kkstd_ready")
                act.wait_ge(sem("logs_ready"), nth(1))
                f(flat(rw[:, WT]), flat(rw[:, CS]), ACT.Exp, "decay_ready", -DECAY)
                f(flat(rw[:, WI]), flat(rw[:, CS]), ACT.Exp, "decay_ready", DECAY)
                f(flat(rw[:, CP]), flat(rw[:, CP]), ACT.Exp, "decay_ready", -DECAY)
                f(fac[:, 0:GT], fac[:, 0:GT], ACT.Exp, "decay_ready", -DECAY)
                for u in range(9, NU):
                    unit(u)
                    if layer == 0 and u == 9:
                        for i in range(4):
                            act.wait_ge(sem("angle_ready"), i + 1)
                            f(trig[:, i], trig[:, i], ACT.Sin, "trig_ready")
                act.wait_ge(sem("hgrn_crossed"), nth(1))
                for half in range(2):
                    copy(hx[:].rearrange("p (j h) b -> p h j b", h=2)[:, half],
                         bank[6 + half][:, 0:2 * P].rearrange("p (j b) -> p j b", b=P), "hx_copied" if half else "act_chain")
                sq = ssb[:].rearrange("p a b -> p (a b)")
                f(sq[:, 0:2 * T], flat(proj[:, J_CQ:J_CQ + 2]), ACT.Square)
                f(sq[:, 2 * T:3 * T], proj[:, J_CKV], ACT.Square, "latsq_ready")
                act.wait_ge(sem("tok_turned"), nth(2))
                copy(flat(vtok[:]), bank[2][:], "tok_copied")
                act.wait_ge(sem("tok_turned"), nth(2, 1))
                f(btok[:, 0], bank[3][:, 0:G], ACT.Copy, scale=-1.0)
                copy(btok[:, 1], bank[3][:, G:2 * G], "tok_copied")
                act.wait_ge(sem("latss_ready"), nth(1))
                f(rstd[:, 0], bank[1][:, 0:T], ACT.Sqrt, "latstd_ready", 1.0 / G, cst("eps_rms"))
                f(rstd[:, 1], bank[1][:, T:2 * T], ACT.Sqrt, "latstd_ready", 1.0 / P, cst("eps_rms"))
                act.wait_ge(sem("ho_ready"), nth(1))
                copy(hx[:].rearrange("p a b -> p (a b)"), bank[0][:], "ho_used")
                hsq, hstd = (b[:].rearrange("p a b -> p (a b)")[:, 0:2 * T] for b in (pts, ssb))
                f(hsq, hx[:].rearrange("p a b -> p (a b)"), ACT.Square, "hosq_ready")
                act.wait_ge(sem("hoss_ready"), nth(1))
                f(hstd, bank[0][:], ACT.Sqrt, "hoss_used", 1.0 / HD, cst("eps_rms"))

                def mla_step(step):
                    if step == 1:
                        for half in range(2):
                            act.wait_ge(sem("mlaq_ready"), nth(2, half))
                            copy(flat(qf[:, 2 * half:2 * half + 2]), bank[half][0:UQ, :], "mlaq_copied")
                    if step == 4:
                        for half in range(2):
                            act.wait_ge(sem("mlak_ready"), nth(2, half))
                            copy(flat(kf[0:HD, 2 * half:2 * half + 2]), bank[half][0:HD, :], "mlakv_copied")
                    if step == 5:
                        act.wait_ge(sem("mla_v_ready"), nth(1))
                        copy(flat(mtok), bank[0][:], "mlakv_copied")
                for l in range(1, LEVELS):
                    for half in range(2):
                        act.wait_ge(sem("mx_ready"), nth(12, 2 * (l - 1) + half))
                        if l > 1:
                            act.wait_ge(sem("xmx_t_ready"), nth(12, 2 * (l - 2) + half))
                        copy(flat(pin[:, 4 * half:4 * half + 4]), bank[2 + half][:], "pin_ready")
                    mla_step(l)

                def softmax(n):
                    b = n % 3
                    act.wait_ge(sem("max_ready"), nth(2 * NH, n))
                    f(ssb[:, b, 0:P], ssb[:, b, 0:P], ACT.Exp, bias=mx[:, b, 0:1], accum=den[:, b, 0:1])
                    f(ssb[:, b, P:3 * P], ssb[:, b, P:3 * P], ACT.Exp, "exp_ready", bias=mx[:, b, 1:2],
                      accum=den[:, b, 1:2])

                def turned(n):
                    act.wait_ge(sem("pts_turned"), nth(2 * NH, n))
                    if n >= 2:
                        act.wait_ge(sem("attended"), nth(2 * NH, n - 2))
                    copy(pts[:, n % 2], bank[(6, 3)[n % 2]][:, 0:3 * P], "pts_ready")
                    if n % NH == NH - 1:
                        kind = n // NH
                        act.wait_ge(sem("attended"), nth(2 * NH, n))
                        copy(flat(yT[:, 2 + 2 * kind:4 + 2 * kind]), bank[(5, 4)[kind]][:], "attn_copied")

                for c in range(TT):
                    act.wait_ge(sem("r_ready"), nth(2, c))
                    for half in range(2):
                        copy(rsol[:].rearrange("p (j h) v -> p h j v", h=2)[:, half],
                             bank[2 + half][:, 0:2 * HD].rearrange("p (j v) -> p j v", v=HD),
                             "rsol_ready" if half else "act_chain")
                    act.wait_ge(sem("u_ready"), nth(2, c))
                    copy(flat(usol[:, c]), bank[6][:, 0:G], "usol_ready")
                    softmax(c)
                act.wait_ge(sem("y_ready"), nth(1))
                copy(flat(ysb[0:HD]), bank[5][0:HD, :])
                copy(flat(ysb[HD:P]), bank[4][HD:P, :], "ysb_ready")
                softmax(2)
                turned(0)
                act.wait_ge(sem("yc_ready"), nth(1))
                f(flat(mtm[:, 0:4]), flat(ysb[:]), ACT.Square, "ysq_ready")
                act.wait_ge(sem("var_ready"), nth(1))
                f(flat(mtm[:, 4:8]), bank[2][:], ACT.Sqrt, "var_used", 1.0 / HD, cst("eps_ln"))
                for n in range(1, 2 * NH):
                    turned(n)
                    if n + 2 < 2 * NH:
                        softmax(n + 2)
                    if n == 2 * NH - 3:
                        act.wait_ge(sem("ya_ready"), nth(2, 1))
                        act_unit_split(act, layer, NU, 0)
                    if n == 2 * NH - 2:
                        act_split_x(act, None, (0,))
                act.wait_ge(sem("yd_ready"), nth(2, 1))
                act_split_x(act, None, (1,))
                act_unit_split(act, layer, NU, 1)
                up, down = act_split(act, (dense, job(0))[layer])
                n = 2 * layer + 1
                for q in range(NO):
                    if q < NO - 1:
                        for part in range(2):
                            act_unit_split(act, layer, NU + q + 1, part)
                    act.wait_ge(sem("xT_ready"), NO * (n - 1) + q + 1)
                    square(n, q)
                    if q == 2:
                        up(0, 0, 0, 0)
                root(n)
                up(0, 0, 0, 1)
                if layer == 0:
                    act_split_x(act, 1)
                up(1, 0, 1, 0)
                if layer == 0:
                    act_ffn_dense(act)
            act_moe(act, copy, f, square)
            root(2 * DEPTH)
            for b in range(4):
                act.wait_ge(sem("out_turned"), b + 1)
                copy(wide[:].rearrange("p (a b) t -> p a (b t)", a=TT)[:, :, b * T:(b + 1) * T],
                     bank[b][:].rearrange("p (a t) -> p a t", a=TT), "out_ready")

        @block.vector
        def _(dve):
            settle = own(dve, "dve_chain")

            def tt_(o, a, b, op, sig="dve_chain"):
                settle(nc.vector.tensor_tensor(o, a, b, op), sig)

            def ts(o, a, s1, s2, op0, op1=ALU.bypass, sig="dve_chain"):
                settle(nc.vector.tensor_scalar(o, a, s1, s2, op0, op1), sig)

            def stt(o, a, s, b, op0, op1, sig="dve_chain"):
                settle(nc.vector.scalar_tensor_tensor(o, a, s, b, op0, op1), sig)

            def recip(o, a, sig="dve_chain"):
                settle(nc.vector.reciprocal(o, a), sig)

            def flat(a):
                return a.rearrange("p a t -> p (a t)")

            def unit_split(layer, u):
                for part in range(2):
                    dve_unit_split(dve, layer, u, part)

            def norm(n, name, layer):
                dve.wait_ge(sem("std_ready"), n + 1)
                recip(rstd[:, 1], rstd[:, 0])
                for k in range(KT):
                    nc.vector.scalar_tensor_tensor(hT[:, k], xT[:, k], prm(name, layer, k), rstd[:, 1], ALU.mult, ALU.mult
                                                   ).then_inc(sem("hT_ready"), 1)

            settle(nc.vector.memset(zeros[:], 0.0))
            settle(nc.vector.memset(fac[:], 0.0))
            settle(nc.vector.memset(lbc[:], 0.0))

            def angle(i):
                if i == 0:
                    dve.wait_ge(sem("pos_in"), 16)
                    ts(rtmp[:, 1], posi, 1.0, None, ALU.mult)
                name, quarter = (("f64", 0.25), ("f64", 0.0), ("f96", 0.25), ("f96", 0.0))[i]
                ang, turns = trig[:, i], rtmp[:, 0]
                ts(ang, rtmp[:, 1], cst(name), None, ALU.mult)
                ts(turns, ang, float(1 / (2 * np.pi)), quarter, ALU.mult, ALU.add)
                ts(turns, turns, ROUND, ROUND, ALU.add, ALU.subtract)
                for part in TURN:
                    stt(ang, turns, -part, ang, ALU.mult, ALU.add)
                ts(ang, ang, float(np.pi / 2) if quarter else 0.0, float(np.float32(3.1415925)), ALU.add, ALU.min)
                ts(ang, ang, float(np.float32(-3.1415925)), None, ALU.max, sig="angle_ready")

            dve.wait_ge(sem("const_in"), 16)
            dve.wait_ge(sem("par_in"), 16)
            ka = PCOL["rwkv_k_a"][0]
            ts(omka[:], par[:, ka:ka + DEPTH * GT], -1.0, 1.0, ALU.mult, ALU.add)
            lb = PCOL["hgrn_lb_logits"][0]
            tt_(lbc[:, GT:2 * GT], par[:, lb + GT:lb + 2 * GT], par[:, lb:lb + GT], ALU.subtract, "lbd_ready")

            for layer in range(DEPTH):
                def nth(per, i=0):
                    return layer * per + i + 1

                unit_split(layer, 0)
                norm(2 * layer, "mix_norm", layer)
                dve_split_x(dve, x_before(layer, 0))
                for u in range(4):
                    unit_split(layer, u + 1)
                    dve.wait_ge(sem("unit_copied"), layer * NU + u + 1)
                    a = proj[:, 2 * u:2 * u + 2]
                    tt_(diff[:, :, 1:T], a[:, :, 0:T - 1], a[:, :, 1:T], ALU.subtract)
                    ts(diff[:, :, 0:1], a[:, :, 0:1], -1.0, None, ALU.mult)
                    for j in range(2):
                        stt(sh[:, 2 * u + j], diff[:, j], prm("rwkv_mu", layer, 2 * u + j), a[:, j], ALU.mult, ALU.add,
                            "shifted")
                for j in range(GT):
                    ts(rw[:, KK, j], sh[:, J_K + j], prm("rwkv_k_k", layer, j), None, ALU.mult,
                       sig="kkr_ready" if j else "dve_chain")
                for u in range(4, 8):
                    unit_split(layer, u + 1)
                    if layer == 0:
                        angle(u - 4)
                if layer == 0:
                    dve.wait_ge(sem("lb_ready"), 1)
                    ts(omlb[:], lbc[:], -1.0, 1.0, ALU.mult, ALU.add, "omlb_ready")
                dve.wait_ge(sem("sig_ready"), nth(5, 1))
                for j in range(GT):
                    for c in range(TT):
                        s = slice(c * P, (c + 1) * P)
                        settle(nc.vector.tensor_tensor_scan(rw[:, CS, j, s], cst("ones"), rw[:, SW, j, s], 0.0,
                                                            ALU.mult, ALU.add))
                for j in range(GT):
                    mid = [rw[:, CS, j, c * P + HD - 1:c * P + HD] for c in range(TT)]
                    tt_(fac[:, j:j + 1], rw[:, CS, j, P - 1:P], mid[0], ALU.subtract)
                    tt_(fac[:, j:j + 1], fac[:, j:j + 1], mid[1], ALU.add)
                    for c in range(TT):
                        settle(nc.vector.tensor_copy(fac[:, GT + c:GT + c + 1], mid[c]))
                        s = slice(c * P, (c + 1) * P)
                        ts(rw[:, CS, j, s], rw[:, CS, j, s], fac[:, GT + c:GT + c + 1], None, ALU.subtract)
                tt_(flat(rw[:, CP]), flat(rw[:, CS]), flat(rw[:, SW]), ALU.subtract, "logs_ready")

                def hgrn_mask(e):
                    for half in range(2):
                        dve.wait_ge(sem("hgrn_scored"), nth(16, 2 * e + half))
                        o = hs[:, 4 * half:4 * half + 4]
                        i = bank[6 + half][:].rearrange("p (a b) -> p a b", b=P)
                        if e == 0:
                            tt_(o, i, over(cst("id"), 4), ALU.mult, "hgrn_masked")
                        else:
                            settle(nc.vector.copy_predicated(o, over(lvl(e - 1), 4).bitcast(I32), i), "hgrn_masked")

                unit_split(layer, 9)
                hgrn_mask(0)
                dve.wait_ge(sem("kkstd_ready"), nth(1))
                ts(flat(rw[:, BN]), flat(rw[:, BN]), 1e-12, None, ALU.max)
                recip(flat(rw[:, BN]), flat(rw[:, BN]))
                tt_(flat(rw[:, KK]), flat(rw[:, KK]), flat(rw[:, BN]), ALU.mult)
                dve.wait_ge(sem("sig_ready"), nth(5, 3))
                for j in range(GT):
                    c = layer * GT + j
                    ts(rw[:, KM, j], rw[:, SA, j], prm("rwkv_k_a", layer, j), omka[:, c:c + 1], ALU.mult, ALU.add)
                tt_(flat(rw[:, KM]), flat(rw[:, KM]), flat(sh[:, J_K:J_K + 2]), ALU.mult)
                tt_(flat(rw[:, BN]), flat(sh[:, J_R:J_R + 2]), flat(rw[:, KM]), ALU.mult)
                hgrn_mask(1)
                for j in range(GT):
                    ts(diff[:, j], rw[:, BN, j], prm("rwkv_r_k", layer, j), None, ALU.mult,
                       sig="rkk_ready" if j else "dve_chain")
                unit_split(layer, 10)
                hgrn_mask(2)
                tt_(flat(rw[:, SA]), flat(rw[:, KK]), flat(rw[:, SA]), ALU.mult)
                dve.wait_ge(sem("decay_ready"), nth(4, 3))
                tt_(flat(kap[:]), flat(rw[:, KK]), flat(rw[:, CP]), ALU.mult)
                tt_(flat(bet[:]), flat(rw[:, SA]), flat(rw[:, WI]), ALU.mult)
                tt_(flat(kha[:]), flat(rw[:, KM]), flat(rw[:, WI]), ALU.mult)
                tt_(flat(rha[:]), flat(sh[:, J_R:J_R + 2]), flat(rw[:, WT]), ALU.mult, "chunks_ready")
                for e in range(3, LEVELS + 1):
                    hgrn_mask(e)
                    if e in (3, 5):
                        unit_split(layer, 11 + (e - 3) // 2)
                    if e == 4:
                        dve.wait_ge(sem("trig_ready"), 4)
                        for i, at in enumerate((J_DQ, J_DK)):
                            dve.wait_ge(sem("partner_ready"), nth(2, i))
                            tt_(rtmp[:], bank[2 + i][:].rearrange("p (a t) -> p a t", t=T), over(trig[:, 1], 2), ALU.mult)
                            tt_(proj[:, at:at + 2], proj[:, at:at + 2], over(trig[:, 0], 2), ALU.mult)
                            tt_(proj[:, at:at + 2], proj[:, at:at + 2], rtmp[:], ALU.add, "rope_ready")
                dve.wait_ge(sem("bonus_ready"), nth(1))
                tt_(flat(rw[:, BN]), bank[5][:], flat(sh[:, J_V:J_V + 2]), ALU.mult, "bonus_used")
                for n, (o, mask, sign) in enumerate(((atm, "ups", 1.0), (btm, "ups", 1.0), (ctm, "upi", -1.0),
                                                     (dtm, "upi", 1.0))):
                    dve.wait_ge(sem("chunk_ready"), nth(4, n))
                    b = 4 if n % 2 == 0 else 6
                    for half in range(2):
                        stt(o[:, 4 * half:4 * half + 4], bank[b + half][:].rearrange("p (a b) -> p a b", b=P), sign,
                            over(cst(mask), 4), ALU.mult, ALU.mult, "chunk_masked" if half else "dve_chain")
                    if n == 0:
                        for half in range(2):
                            hv = slice(4 * half, 4 * half + 4)
                            tt_(xit[:, hv], atm[:, hv], over(lvl(0), 4), ALU.mult)
                            stt(xit[:, hv], xit[:, hv], -1.0, over(cst("id"), 4), ALU.mult, ALU.add, "xit_ready")
                for half in range(2):
                    dve.wait_ge(sem("xt_turned"), nth(2, half))
                    settle(nc.vector.tensor_copy(flat(xin[:, 4 * half:4 * half + 4]), bank[2 + half][:]), "xin_ready")
                dve.wait_ge(sem("latstd_ready"), nth(2, 1))
                recip(flat(rstd[:]), flat(rstd[:]))
                for k in range(2):
                    stt(proj[:, J_CQ + k], proj[:, J_CQ + k], prm("mla_q_norm", layer, k), rstd[:, 0],
                        ALU.mult, ALU.mult, "lat_ready")
                stt(proj[:, J_CKV], proj[:, J_CKV], prm("mla_kv_norm", layer, 0), rstd[:, 1],
                    ALU.mult, ALU.mult, "lat_ready")
                hxf = hx[:].rearrange("p a b -> p (a b)")
                hstd = ssb[:].rearrange("p a b -> p (a b)")[:, 0:2 * T]

                def side_step(step):
                    r = slice(HD, UQ)
                    if step == 1:
                        dve.wait_ge(sem("hoss_used"), nth(1))
                        recip(hstd, hstd)
                    if step in (2, 3):
                        half = step - 2
                        dve.wait_ge(sem("q_partner"), nth(2, half))
                        hv = slice(2 * half, 2 * half + 2)
                        tt_(rtmp[r], bank[half][r, :].rearrange("p (a t) -> p a t", t=T), over(trig[r, 3], 2), ALU.mult)
                        tt_(qf[r, hv], qf[r, hv], over(trig[r, 2], 2), ALU.mult)
                        tt_(qf[r, hv], qf[r, hv], rtmp[r], ALU.add, "qf_ready" if half else "dve_chain")
                    if step == 4:
                        tt_(hxf, hxf, hstd, ALU.mult)
                        for j in range(GT):
                            stt(yT[:, 6 + j], hxf[:, j * T:(j + 1) * T], prm("hgrn_g_norm", layer, j), proj[:, J_HG + j],
                                ALU.mult, ALU.mult, "yd_ready")
                    if step == 5:
                        dve.wait_ge(sem("kr_partner"), nth(1))
                        tt_(rtmp[r, 0], bank[1][r, 0:T], trig[r, 3], ALU.mult)
                        tt_(proj[r, J_KR], proj[r, J_KR], trig[r, 2], ALU.mult)
                        tt_(kf[r], over(proj[r, J_KR], NH), over(rtmp[r, 0], NH), ALU.add, "kf_ready")

                for l in range(1, LEVELS):
                    for half in range(2):
                        hv = slice(4 * half, 4 * half + 4)
                        if l < LEVELS - 1:
                            dve.wait_ge(sem("xmx_ready"), nth(10, 2 * (l - 1) + half))
                            tt_(flat(xin[:, hv]), flat(xin[:, hv]), bank[4 + half][:], ALU.subtract, "xin_ready")
                        dve.wait_ge(sem("xmx_t_ready"), nth(12, 2 * (l - 1) + half))
                        tt_(flat(xit[:, hv]), flat(xit[:, hv]), bank[6 + half][:], ALU.subtract, "xit_ready")
                    side_step(l)

                def scores(n):
                    kind, b = n // NH, n % 3
                    dve.wait_ge(sem("scores_ready"), nth(2 * NH, n))
                    if n >= 3:
                        dve.wait_ge(sem("pts_turned"), nth(2 * NH, n - 3))
                    stt(ssb[:, b], bank[(0, 1, 7)[b]][:, 0:3 * P], float(np.float32((HD, UQ)[kind] ** -0.5)),
                        cst(("dil", "caus")[kind]), ALU.mult, ALU.add, "scores_used")
                    settle(nc.vector.tensor_reduce(mx[:, b, 0:1], ssb[:, b, 0:P], AX.X, ALU.max, negate=True))
                    settle(nc.vector.tensor_reduce(mx[:, b, 1:2], ssb[:, b, P:3 * P], AX.X, ALU.max, negate=True), "max_ready")

                def probs(n):
                    b = n % 3
                    dve.wait_ge(sem("exp_ready"), nth(2 * NH, n))
                    recip(den[:, b], den[:, b])
                    ts(ssb[:, b, 0:P], ssb[:, b, 0:P], den[:, b, 0:1], None, ALU.mult)
                    ts(ssb[:, b, P:3 * P], ssb[:, b, P:3 * P], den[:, b, 1:2], None, ALU.mult, sig="probs_ready")

                scores(0)
                dve.wait_ge(sem("state_summed"), nth(1))
                for j in range(GT):
                    ts(st[:, j], bank[4][:, j * HD:(j + 1) * HD], fac[:, j:j + 1], None, ALU.mult,
                       sig="state_ready" if j else "dve_chain")
                scores(1)
                scores(2)
                probs(0)
                dve.wait_ge(sem("mean_ready"), nth(1))
                stt(flat(ysb[:]), bank[2][:], -1.0 / HD, flat(ysb[:]), ALU.mult, ALU.add, "yc_ready")

                def rwkv_out(part):
                    if part < 2:
                        if part == 0:
                            dve.wait_ge(sem("var_used"), nth(1))
                        r = flat(mtm[:, 4 + 2 * part:6 + 2 * part])
                        recip(r, r)
                    elif part == 2:
                        tt_(flat(ysb[:]), flat(ysb[:]), flat(mtm[:, 4:8]), ALU.mult)
                    else:
                        j = part - 3
                        ts(ysb[:, j], ysb[:, j], prm("rwkv_ln_w", layer, j), prm("rwkv_ln_b", layer, j), ALU.mult, ALU.add)
                        tt_(ysb[:, j], ysb[:, j], rw[:, BN, j], ALU.add)
                        tt_(yT[:, j], ysb[:, j], rw[:, GG, j], ALU.mult, "ya_ready")

                for n in range(1, 2 * NH):
                    probs(n)
                    if n + 2 < 2 * NH:
                        scores(n + 2)
                    if n <= 5:
                        rwkv_out(n - 1)
                dve_unit_split(dve, layer, NU, 0)
                dve_split_x(dve, x_before(layer, 1))
                dve_unit_split(dve, layer, NU, 1)
                up, down = splitter(dve, split_low, (dense, job(0))[layer])
                for u in range(NO):
                    if u < NO - 1:
                        unit_split(layer, NU + u + 1)
                    if u == NO - 1:
                        up(0, 0, 0, 0)
                    dve.wait_ge(sem("unit_used"), layer * LU + NU + u + 1)
                    tt_(flat(xT[:, 2 * u:2 * u + 2]), flat(xT[:, 2 * u:2 * u + 2]), bank[2 + u][:], ALU.add, "xT_ready")
                norm(2 * layer + 1, "ffn_norm", layer)
                if layer == 0:
                    dve_split_x(dve, x_before(0, 2))
                up(0, 0, 0, 1)
                up(1, 0, 1, 0)
                if layer == 0:
                    dve_ffn_dense(dve, tt_)
            dve_moe(dve, settle, tt_, ts, stt, recip)
            norm(2 * DEPTH, "final_norm", 0)


NAMES = ["x", "positions", "w_in", "w_out", "rwkv_w2", "rwkv_a2", "rwkv_g2", "mla_w_uq", "mla_w_ukv", "ffn_w1", "ffn_w3",
         "ffn_w2", "moe_router", "moe_w1", "moe_w3", "moe_w2"]


def parameters(inputs):
    rows = [np.asarray(inputs[n]).reshape(-1, P) for n, _ in PARAMS] + [np.asarray(inputs["final_norm"]).reshape(-1, P)]
    return np.ascontiguousarray(np.concatenate(rows).T)


def kernel(**inputs):
    import concourse.bacc as bacc
    from concourse.bass_utils import run_bass_kernel_spmd

    nc = bacc.Bacc("TRN2", target_bir_lowering=False, num_devices=1)
    arrays = {f"in_{n}": np.ascontiguousarray(inputs[n]) for n in NAMES}
    arrays["in_const"] = constants()
    arrays["in_par"] = parameters(inputs)
    aps = {n[3:]: nc.dram_tensor(n, a.shape, mybir.dt.from_np(a.dtype), kind="ExternalInput").ap()
           for n, a in arrays.items()}
    out = nc.dram_tensor("out", (1, T, D), F32, kind="ExternalOutput").ap()
    program(nc, aps, out)
    r = run_bass_kernel_spmd(nc, [arrays], core_ids=[0])
    return r.results[0]["out"]
```
